# Optimizing a Trainium2 kernel written in Bass

```python
import jax, jax.numpy as jnp
from jax import lax
import numpy as np

D_MODEL = 1024
BATCH = 1
SEQ = 512
DEPTH = 1

CHUNK = 64
EPS = 1e-6
D_MIX = D_MODEL
ATT_HEADS = 8
ATT_KV_HEADS = 2
ATT_HEAD_DIM = 64
ATT_REP = ATT_HEADS // ATT_KV_HEADS
WINDOW = 128
WIN_CHUNKS = WINDOW // CHUNK
ATT_WIDTH = ATT_HEADS * ATT_HEAD_DIM
KV_WIDTH = ATT_KV_HEADS * ATT_HEAD_DIM
SGU_WIDTH = D_MIX - ATT_WIDTH
SGU_GROUPS = 4
SGU_GROUP_DIM = SGU_WIDTH // SGU_GROUPS
SGU_LEN = 128
IN_WIDTH = ATT_WIDTH + 2 * KV_WIDTH + 2 * SGU_WIDTH
PEER_HEADS = 8
N_KEYS = 128
N_EXPERTS = N_KEYS * N_KEYS
PEER_TOPK = 16
D_KEY = 256
D_HALF = D_KEY // 2
PEER_TOKEN_BLOCK = 128

kernel_name = "hybrid_swa_sink_gmlp_peer_block"

def _rms_norm(x, g):
    x32 = x.astype(jnp.float32)
    y = x32 * lax.rsqrt(jnp.mean(x32 * x32, axis=-1, keepdims=True) + EPS)
    return y.astype(x.dtype) * g

def _layer_norm(x, g):
    x32 = x.astype(jnp.float32)
    mu = jnp.mean(x32, axis=-1, keepdims=True)
    var = jnp.mean(jnp.square(x32 - mu), axis=-1, keepdims=True)
    return ((x32 - mu) * lax.rsqrt(var + EPS)).astype(x.dtype) * g

def _modulate(h, shift, scale):
    return h * (1 + scale[:, None, :]) + shift[:, None, :]

def _window_sink_attention(q, k, v, sinks):
    B, S = q.shape[:2]
    nc = S // CHUNK
    pad = WIN_CHUNKS - 1
    qc = q.reshape(B, nc, CHUNK, ATT_KV_HEADS, ATT_REP, ATT_HEAD_DIM)

    def band(t):
        t = t.reshape(B, nc, CHUNK, ATT_KV_HEADS, ATT_HEAD_DIM)
        t = jnp.pad(t, ((0, 0), (pad, 0), (0, 0), (0, 0), (0, 0)))
        return jnp.concatenate([t[:, i:i + nc] for i in range(WIN_CHUNKS)], axis=2)

    kb, vb = band(k), band(v)
    scores = jnp.einsum('bnqgrd,bnkgd->bngrqk', qc, kb).astype(jnp.float32) * (ATT_HEAD_DIM ** -0.5)
    key_chunk = jnp.arange(nc)[:, None] - pad + jnp.arange(WIN_CHUNKS * CHUNK)[None, :] // CHUNK
    valid = (key_chunk >= 0)[None, :, None, None, None, :]
    scores = jnp.where(valid, scores, jnp.finfo(jnp.float32).min)
    sink = jnp.broadcast_to(sinks.astype(jnp.float32).reshape(1, 1, ATT_KV_HEADS, ATT_REP, 1, 1),
                            scores.shape[:-1] + (1,))
    probs = jax.nn.softmax(jnp.concatenate([scores, sink], axis=-1), axis=-1)[..., :-1]
    out = jnp.einsum('bngrqk,bnkgd->bnqgrd', probs.astype(v.dtype), vb)
    return out.reshape(B, S, ATT_WIDTH)

def _spatial_gating(u, v, w_s, b_s, g_norm):
    B, S = u.shape[:2]
    nb = S // SGU_LEN
    vn = _layer_norm(v, g_norm).reshape(B, nb, SGU_LEN, SGU_GROUPS, SGU_GROUP_DIM)
    pos_chunk = jnp.arange(SGU_LEN) // CHUNK
    mask = pos_chunk[None, :] <= pos_chunk[:, None]
    w = jnp.where(mask[None], w_s, 0)
    mixed = jnp.einsum('gij,bnjgc->bnigc', w, vn) + b_s.T[None, None, :, :, None]
    return u * mixed.reshape(B, S, SGU_WIDTH)

def _peer(h, w_query, sub_keys, expert_down, expert_up):
    B, S, D = h.shape
    T = B * S
    xt = h.reshape(T, D)
    q = (xt @ w_query).reshape(T, PEER_HEADS, 2, D_HALF)
    s = jnp.einsum('thpd,hpnd->thpn', q, sub_keys).astype(jnp.float32)
    top_s, top_i = lax.top_k(s, PEER_TOPK)
    cand = (top_s[:, :, 0, :, None] + top_s[:, :, 1, None, :]).reshape(T, PEER_HEADS, PEER_TOPK * PEER_TOPK)
    best_s, best_c = lax.top_k(cand, PEER_TOPK)
    i1 = jnp.take_along_axis(top_i[:, :, 0], best_c // PEER_TOPK, axis=-1)
    i2 = jnp.take_along_axis(top_i[:, :, 1], best_c % PEER_TOPK, axis=-1)
    ids = (i1 * N_KEYS + i2).reshape(T, PEER_HEADS * PEER_TOPK)
    gates = jax.nn.softmax(best_s, axis=-1).reshape(T, PEER_HEADS * PEER_TOPK).astype(h.dtype)
    nb = T // PEER_TOKEN_BLOCK

    def block(args):
        xb, idb, gb = args
        a = jnp.einsum('tkd,td->tk', expert_down[idb], xb)
        act = jax.nn.gelu(a.astype(jnp.float32), approximate=False).astype(xb.dtype) * gb
        return jnp.einsum('tk,tkd->td', act, expert_up[idb])

    y = lax.map(block, (xt.reshape(nb, PEER_TOKEN_BLOCK, D),
                        ids.reshape(nb, PEER_TOKEN_BLOCK, -1),
                        gates.reshape(nb, PEER_TOKEN_BLOCK, -1)))
    return y.reshape(B, S, D)

def setup_inputs(seed: int = 0) -> dict:
    key = jax.random.key(seed)
    ks = jax.random.split(key, 20)
    D = D_MODEL
    nrm = lambda k, shape, s: jax.random.normal(k, shape, jnp.float32) * s
    gain = lambda k: 1.0 + nrm(k, (DEPTH, D), 0.05)
    return {
        "x": nrm(ks[0], (BATCH, SEQ, D), 1.0),
        "c": nrm(ks[1], (BATCH, D), 1.0),
        "w_ada": nrm(ks[2], (DEPTH, D, 6 * D), 0.5 * D ** -0.5),
        "b_ada": nrm(ks[3], (DEPTH, 6 * D), 0.01),
        "g_pre_mix": gain(ks[4]),
        "g_post_mix": gain(ks[5]),
        "g_pre_ffn": gain(ks[6]),
        "g_post_ffn": gain(ks[7]),
        "w_in": nrm(ks[8], (DEPTH, D, IN_WIDTH), D ** -0.5),
        "attn_sinks": nrm(ks[9], (DEPTH, ATT_HEADS), 1.0),
        "sgu_norm": 1.0 + nrm(ks[10], (DEPTH, SGU_WIDTH), 0.05),
        "sgu_w": nrm(ks[11], (DEPTH, SGU_GROUPS, SGU_LEN, SGU_LEN), SGU_LEN ** -0.5),
        "sgu_b": 1.0 + nrm(ks[12], (DEPTH, SGU_GROUPS, SGU_LEN), 0.1),
        "w_out": nrm(ks[13], (DEPTH, D_MIX, D), D_MIX ** -0.5),
        "peer_query": nrm(ks[14], (DEPTH, D, PEER_HEADS * D_KEY), D ** -0.5),
        "peer_keys": nrm(ks[15], (DEPTH, PEER_HEADS, 2, N_KEYS, D_HALF), D_HALF ** -0.5),
        "peer_down": nrm(ks[16], (DEPTH, N_EXPERTS, D), D ** -0.5),
        "peer_up": nrm(ks[17], (DEPTH, N_EXPERTS, D), D ** -0.5),
    }

def reference(x, c, w_ada, b_ada, g_pre_mix, g_post_mix, g_pre_ffn, g_post_ffn, w_in, attn_sinks,
              sgu_norm, sgu_w, sgu_b, w_out, peer_query, peer_keys, peer_down, peer_up):
    c_act = jax.nn.silu(c)
    o1 = ATT_WIDTH
    o2 = o1 + KV_WIDTH
    o3 = o2 + KV_WIDTH
    o4 = o3 + SGU_WIDTH
    for l in range(DEPTH):
        mod = c_act @ w_ada[l] + b_ada[l]
        sh1, sc1, gt1, sh2, sc2, gt2 = jnp.split(mod, 6, axis=-1)

        h = _modulate(_rms_norm(x, g_pre_mix[l]), sh1, sc1)
        z = h @ w_in[l]
        q, k, v, su, sv = jnp.split(z, [o1, o2, o3, o4], axis=-1)
        a_out = _window_sink_attention(q, k, v, attn_sinks[l])
        b_out = _spatial_gating(jax.nn.gelu(su, approximate=False), jax.nn.gelu(sv, approximate=False),
                                sgu_w[l], sgu_b[l], sgu_norm[l])
        mix = jnp.concatenate([a_out, b_out], axis=-1) @ w_out[l]
        x = x + gt1[:, None, :] * _rms_norm(mix, g_post_mix[l])

        h = _modulate(_rms_norm(x, g_pre_ffn[l]), sh2, sc2)
        y = _peer(h, peer_query[l], peer_keys[l], peer_down[l], peer_up[l])
        x = x + gt2[:, None, :] * _rms_norm(y, g_post_ffn[l])
    return x


_drawn_inputs = setup_inputs


def setup_inputs(seed=0):
    import zlib

    import numpy as np

    out = dict(_drawn_inputs(seed))
    spreads = {}
    factors = {'g_post_ffn': 4.136, 'attn_sinks': 4.288}
    for name, (base, spread) in spreads.items():
        noise = np.random.default_rng([zlib.crc32(name.encode()), seed]).standard_normal(out[name].shape)
        drawn = base * np.exp(spread * noise) if base else spread * noise
        out[name] = __import__('jax').numpy.asarray(drawn.astype(out[name].dtype))
    for name, factor in factors.items():
        out[name] = (out[name] * factor).astype(out[name].dtype)
    return out
```

```python
from contextlib import ExitStack

import concourse.bass as bass
from concourse import mybir

F32 = mybir.dt.float32
F32R = mybir.dt.float32r
U32 = mybir.dt.uint32
ALU = mybir.AluOpType
ACT = mybir.ActivationFunctionType
AXX = mybir.AxisListType.X

P = 128
D = 1024
T = 512
KT = D // P
NB = T // P
HEADS, KV_HEADS, HD = 8, 2, 64
CHUNK = 64
ATT = HEADS * HD
KVW = KV_HEADS * HD
SGU = D - ATT
GROUPS = SGU // P
IN_W = ATT + 2 * KVW + 2 * SGU
K_AT, V_AT = ATT, ATT + KVW
U_AT, SV_AT = ATT + 2 * KVW, ATT + 2 * KVW + SGU
PH = 8
TOPK = 16
KEYS = 128
TILES = KEYS
EPS = 1e-6
LOWEST = -3.0e38

ADA_COLUMN_A = [2, 3, 0, 1]
ADA_ROW_1 = [4, 5]
ADA_COLUMN_B = [8, 9, 6, 7]
ADA_ROW_2 = [10, 11]
ADA_ORDER = ADA_COLUMN_A + ADA_ROW_1 + ADA_COLUMN_B + ADA_ROW_2
ADA_SLOTS = 3
SH1, SC1, SH2, SC2 = 0, 8, 24, 32
ROW_C, ROW_B, ROW_G1, ROW_G2, ROWS = 0, 8, 56, 64, 72

Z_SV, Z_U, Z_K, Z_Q, Z_V, Z_VS, Z_JOBS = 0, 4, 8, 9, 13, 14, 15
Z_BANKS = [5, 6, 7, 1, 2, 3, 4]

HEAD_STEPS = 3 * 20 + 5
TB = 8
GROUP = 2


class Chain:

    def __init__(self, eng, sem):
        self.eng, self.sem, self.base, self.n = eng, sem, 0, 0

    def mark(self, ins):
        ins.then_inc(self.sem, 1)
        self.n += 1

    def wait(self):
        self.eng.wait_ge(self.sem, self.base + self.n)

    def link(self, ins):
        self.mark(ins)
        self.wait()

    def enter(self, turn, per_turn):
        self.before, self.per_turn = self.base + self.n, per_turn
        self.base, self.n = turn * per_turn + self.before, 0

    def leave(self, turns):
        assert self.n == self.per_turn, self.n
        self.base, self.n = self.before + turns * self.per_turn, 0


class Region:

    def __init__(self, nc, start, limit):
        self.nc, self.at, self.limit = nc, start, limit

    def __call__(self, name, shape, dt=F32):
        size = 4
        for n in shape:
            size *= n
        t = self.nc.alloc_sbuf_tensor_at(name, [P] + list(shape), dt, offset=self.at)
        self.at += -(-size // 32) * 32
        assert self.at <= self.limit, (name, self.at - self.limit)
        return t


def build_block(nc, x, c, w_ada, b_ada, g_pre_mix, g_post_mix, g_pre_ffn, g_post_ffn, w_in, attn_sinks,
                sgu_norm, sgu_w, sgu_b, w_out, peer_query, peer_keys, peer_down, peer_up, out):
    ctx = ExitStack()
    with ctx:
        def sem(name):
            return ctx.enter_context(nc.semaphore(name))

        base, limit = -(-nc.sbuf_base // 32) * 32, nc.sbuf_usable_end
        kept = Region(nc, base, limit)
        ident = kept("ident", [P])
        iota = kept("iota", [P])
        columns = kept("columns", [ROWS])
        modc = kept("modc", [48])
        scale1 = kept("scale1", [KT])
        scale2 = kept("scale2", [KT])
        ssq = kept("ssq", [32])
        root = kept("root", [32])
        svsum = kept("svsum", [NB])
        x1 = kept("x1", [NB, D])
        gg2 = kept("gg2", [D])
        h2_at = kept.at
        h2hi = kept("h2hi", [KT, T], F32R)
        h2lo = kept("h2lo", [KT, T], F32R)
        rest_at = kept.at

        r = Region(nc, h2_at, rest_at)
        qT = r("qT", [4, T])
        uT = r("uT", [GROUPS, T])
        catT_at = r.at
        catT = r("catT", [KT, T])
        xn1 = Region(nc, catT_at, rest_at)("xn1", [NB, D])
        r = Region(nc, rest_at, limit)
        gg1 = r("gg1", [D])
        hT_at = r.at
        HTW = CHUNK + T
        hT = r("hT", [KT, HTW])
        w_in_at = r.at
        w_in_sb = r("w_in_sb", [KT, IN_W])
        ada_at = r.at
        ada = [r(f"ada{i}", [KT, 512]) for i in range(ADA_SLOTS)]
        kT = r("kT", [HTW])
        v = r("v", [NB, KVW])
        vs = r("vs", [NB, KVW])
        sv = r("sv", [NB, SGU])
        wT = r("wT", [GROUPS, P])
        c_col = r("c_col", [KT])
        c_bc = r("c_bc", [KT, P])
        sgub = r("sgub", [GROUPS, P])
        sgun = r("sgun", [SGU])
        sinks = r("sinks", [HEADS])
        amax = r("amax", [HEADS])
        asum = r("asum", [HEADS])
        asink = r("asink", [HEADS])
        rows = r("rows", [P])
        sgw = r("sgw", [GROUPS, P])
        ajunk = sgw[:].rearrange("p g i -> p (g i)")
        r = Region(nc, hT_at, w_in_at)
        s_sb = [r(f"s_sb{i}", [HEADS, P]) for i in range(2)]
        pT = [r(f"pT{i}", [HEADS, P]) for i in range(2)]
        r = Region(nc, w_in_at, ada_at)
        w_out_sb = r("w_out_sb", [KT, D])
        gp1 = r("gp1", [D])
        gp2 = r("gp2", [D])
        xn2 = r("xn2", [NB, D])

        r = Region(nc, ada_at, limit)
        keys = r("keys", [2 * PH, P])
        wq = [r(f"wq{i}", [KT, P]) for i in range(2)]
        keysT = r("keysT", [2 * PH, P])
        wqhi = [r(f"wqhi{i}", [KT, P], F32R) for i in range(2)]
        wqlo = [r(f"wqlo{i}", [KT, P], F32R) for i in range(2)]
        assert r.at <= ada_at + ADA_SLOTS * KT * 512 * 4
        htmp = [r(f"htmp{i}", [T]) for i in range(2)]
        pqT = [r(f"pqT{i}", [T]) for i in range(2)]
        score = [r(f"score{i}", [NB, KEYS]) for i in range(2)]
        hit = [r(f"hit{i}", [NB, TOPK, TOPK]) for i in range(2)]
        r = Region(nc, w_in_at, ada_at)
        cand = r("cand", [NB, TOPK, TOPK])
        top = r("top", [2, NB, TOPK])
        topi = r("topi", [2, NB, TOPK], U32)
        topf = r("topf", [2, NB, TOPK])
        bests = r("bests", [NB, TOPK])
        besti = r("besti", [NB, TOPK], U32)
        pair = r("pair", [2, NB, TOPK], U32)
        pairf = r("pairf", [2, NB, TOPK])
        best = r("best", [NB, PH, TOPK])
        bsum = r("bsum", [NB, PH])
        pick = r("pick", [3, NB, PH, TOPK])
        r = Region(nc, rest_at, w_in_at)
        pickT = r("pickT", [3, T])
        onehot2 = [r(f"onehot2_{i}", [TB, KEYS]) for i in range(2)]
        gated1 = [r(f"gated1_{i}", [TB, KEYS]) for i in range(2)]
        r = Region(nc, r.at, limit)
        stage = [r(f"stage{i}", [KEYS, P]) for i in range(2)]
        r = Region(nc, rest_at, limit)
        y = r("y", [NB, D])
        down = [r(f"down{i}", [D]) for i in range(2)]
        up = [r(f"up{i}", [D]) for i in range(2)]
        gate = [r(f"gate{i}", [T]) for i in range(2)]
        dhi = [r(f"dhi{i}", [KT, P], F32R) for i in range(2)]
        dlo = [r(f"dlo{i}", [KT, P], F32R) for i in range(2)]
        uhi = [[r(f"uhi{g}{i}", [D], F32R) for i in range(GROUP)] for g in range(2)]
        ulo = [[r(f"ulo{g}{i}", [D], F32R) for i in range(GROUP)] for g in range(2)]
        gel = [r(f"gel{i}", [T]) for i in range(2)]
        acts = [r(f"acts{i}", [T]) for i in range(2)]
        ahi = [[r(f"ahi{g}{i}", [T], F32R) for i in range(GROUP)] for g in range(2)]
        alo = [[r(f"alo{g}{i}", [T], F32R) for i in range(GROUP)] for g in range(2)]
        junk = r("junk", [D])

        bank = [ctx.enter_context(nc.psum_tensor(f"bank{i}", [P, 512], F32)) for i in range(8)]
        gates_dram = nc.dram_tensor("gates_dram", [TILES, KEYS, T], F32).ap()

        x_v = x[0].rearrange("(b p) d -> b p d", p=P)
        out_v = out[0].rearrange("(b p) d -> b p d", p=P)
        ada_v = w_ada[0].rearrange("(k p) n -> p k n", p=P)
        w_in_v = w_in[0].rearrange("(k p) n -> p k n", p=P)
        w_out_v = w_out[0].rearrange("(k p) n -> p k n", p=P)
        wq_v = peer_query[0].rearrange("(k p) n -> p k n", p=P)
        keys_v = peer_keys[0].rearrange("h s n d -> n (h s) d")
        down_v = peer_down[0].rearrange("(n p) d -> n p d", p=P)
        up_v = peer_up[0].rearrange("(n p) d -> n p d", p=P)

        def row(ap):
            return ap.broadcast_to([P] + list(ap.shape[1:]))

        def one(view, n):
            return view[bass.ds(n, 1)].rearrange("o p m -> (o p) m")

        rows_in, misc_in, w_in_in, w_out_in = sem("rows_in"), sem("misc_in"), sem("w_in_in"), sem("w_out_in")
        x_in = [sem(f"x_in{i}") for i in range(NB)]
        ada_in = [sem(f"ada_in{i}") for i in range(ADA_SLOTS)]
        gp_in, keys_in = sem("gp_in"), sem("keys_in")
        wq_in = [sem(f"wq_in{i}") for i in range(2)]
        stored = [sem(f"stored{i}") for i in range(2)]
        down_in = [sem(f"down_in{i}") for i in range(2)]
        up_in = [sem(f"up_in{i}") for i in range(2)]
        gate_in = [sem(f"gate_in{i}") for i in range(2)]
        out_done = sem("out_done")
        ident_ok, zeros_ok = sem("ident_ok"), sem("zeros_ok")
        pe_rows, pe_wT, ada_used, pe_h1, pe_z = (sem(n) for n in ("pe_rows", "pe_wT", "ada_used", "pe_h1", "pe_z"))
        pe_s, pe_pt, pe_o, pe_sgu, pe_mix = (sem(n) for n in ("pe_s", "pe_pt", "pe_o", "pe_sgu", "pe_mix"))
        pe_keys, pe_h2, pe_q, pe_sc, pe_pick = (sem(n) for n in ("pe_keys", "pe_h2", "pe_q", "pe_sc", "pe_pick"))
        pe_g, pe_t, pe_d, pe_u = (sem(n) for n in ("pe_g", "pe_t", "pe_d", "pe_u"))
        act_silu, act_ss, act_root, act_h1, act_z, act_sv = (
            sem(n) for n in ("act_silu", "act_ss", "act_root", "act_h1", "act_z", "act_sv"))
        act_s, act_exp, act_pt, act_o = (sem(n) for n in ("act_s", "act_exp", "act_pt", "act_o"))
        act_keys, act_h2, act_wq, act_q, act_sc, act_gexp, act_pick, act_g = (
            sem(n) for n in ("act_keys", "act_h2", "act_wq", "act_q", "act_sc", "act_gexp", "act_pick", "act_g"))
        act_dhi, act_uhi, act_gelu, act_ahi = (sem(n) for n in ("act_dhi", "act_uhi", "act_gelu", "act_ahi"))
        dve = sem("dve")
        dve_c, dve_ms, dve_xn1, dve_mod, dve_h1, dve_wT = (
            sem(n) for n in ("dve_c", "dve_ms", "dve_xn1", "dve_mod", "dve_h1", "dve_wT"))
        dve_center, dve_vn, dve_sgu, dve_sub, dve_p, dve_gg = (
            sem(n) for n in ("dve_center", "dve_vn", "dve_sgu", "dve_sub", "dve_p", "dve_gg"))
        dve_mix, dve_x1, dve_xn2, dve_htmp, dve_h2 = (
            sem(n) for n in ("dve_mix", "dve_x1", "dve_xn2", "dve_htmp", "dve_h2"))
        dve_top, dve_pair, dve_sel, dve_bsub, dve_pick, dve_hot = (
            sem(n) for n in ("dve_top", "dve_pair", "dve_sel", "dve_bsub", "dve_pick", "dve_hot"))
        dve_dlo, dve_act, dve_alo, dve_y = (sem(n) for n in ("dve_dlo", "dve_act", "dve_alo", "dve_y"))
        pool_wq, pool_hit, pool_ulo, pool = (sem(n) for n in ("pool_wq", "pool_hit", "pool_ulo", "pool"))

        block = ctx.enter_context(nc.Block())

        @block.sync
        def _(sp):
            sp.dma_start(rows[ROW_C:ROW_C + KT, :], c.rearrange("o (k p) -> (o k) p", p=P)).then_inc(rows_in, 16)
            sp.dma_start(rows[ROW_B:ROW_B + 48, :], b_ada.rearrange("o (k p) -> (o k) p", p=P)).then_inc(rows_in, 16)
            sp.dma_start(rows[ROW_G1:ROW_G1 + KT, :], g_pre_mix.rearrange("o (k p) -> (o k) p", p=P)).then_inc(rows_in, 16)
            sp.dma_start(rows[ROW_G2:ROW_G2 + KT, :], g_pre_ffn.rearrange("o (k p) -> (o k) p", p=P)).then_inc(rows_in, 16)

            def load_ada(n):
                q = ADA_ORDER[n]
                if n >= ADA_SLOTS:
                    sp.wait_ge(ada_used, n - ADA_SLOTS + 1)
                sp.dma_start(ada[n % ADA_SLOTS][:], ada_v[:, :, q * 512:q * 512 + 512]).then_inc(ada_in[n % ADA_SLOTS], 16)

            for b in range(NB):
                sp.dma_start(x1[:, b, :], x_v[b]).then_inc(x_in[b], 16)
            for n in range(4):
                load_ada(n)
            for q in range(4):
                two = slice(2 * q, 2 * q + 2)
                sp.dma_start(w_in_sb[:, two, ATT:], w_in_v[:, two, ATT:]).then_inc(w_in_in, 16)
            for k in range(KT):
                for s in range(2):
                    sp.dma_start(w_in_sb[:, k, 0:ATT].rearrange("p (j s n) -> p j s n", j=4, s=2)[:, :, s, :],
                                 w_in_v[:, k, s * 256:s * 256 + 256].rearrange("p (j n) -> p j n", j=4)
                                 ).then_inc(w_in_in, 16)
            for n in range(4, 7):
                load_ada(n)
            sp.wait_ge(pe_z, Z_JOBS)
            sp.dma_start(gp1[:], row(g_post_mix)).then_inc(gp_in, 16)
            sp.dma_start(gp2[:], row(g_post_ffn)).then_inc(gp_in, 16)
            for q in range(2):
                sp.dma_start(w_out_sb[:, 4 * q:4 * q + 4, :], w_out_v[:, 4 * q:4 * q + 4, :]).then_inc(w_out_in, 16)
            for n in range(7, len(ADA_ORDER)):
                load_ada(n)

            sp.wait_ge(ada_used, len(ADA_ORDER))
            sp.dma_start(keys[:], keys_v).then_inc(keys_in, 16)

            def load_wq(h, s):
                sp.dma_start(wq[s][:], wq_v[:, :, bass.ds(h * 256 + s * P, P)]).then_inc(wq_in[s], 16)

            for s in range(2):
                load_wq(0, s)
            with sp.Fori(1, PH) as h:
                for s in range(2):
                    sp.wait_ge(act_wq, 2 * h - 1 + s)
                    sp.wait_ge(pool_wq, 2 * h - 1 + s)
                    load_wq(h, s)

            for b in range(NB):
                sp.wait_ge(act_g, (b + 1) * (P // 4))
                sp.dma_start(gates_dram[:, :, b * P:(b + 1) * P].rearrange("i p t -> p i t"),
                             stage[b % 2][:]).then_inc(stored[b % 2], 16)

            for s in range(2):
                sp.wait_ge(stored[s], 16 * NB // 2)
            def load_tile(n, s):
                sp.dma_start(down[s][:], one(down_v, n)).then_inc(down_in[s], 16)
                sp.dma_start(up[s][:], one(up_v, n)).then_inc(up_in[s], 16)
                sp.dma_start(gate[s][:], one(gates_dram, n)).then_inc(gate_in[s], 16)

            for s in range(2):
                load_tile(s, s)
            with sp.Fori(0, TILES // 2 - 1) as i:
                for s in range(2):
                    n = 2 * i + s
                    sp.wait_ge(pe_t, 2 * n + 2)
                    sp.dma_start(down[s][:], one(down_v, n + 2)).then_inc(down_in[s], 16)
                    sp.wait_ge(pool_ulo, n + 1)
                    sp.dma_start(up[s][:], one(up_v, n + 2)).then_inc(up_in[s], 16)
                    sp.wait_ge(dve_act, n + 1)
                    sp.dma_start(gate[s][:], one(gates_dram, n + 2)).then_inc(gate_in[s], 16)

            for b in range(NB):
                sp.wait_ge(dve_x1, NB + b + 1)
                sp.dma_start(out_v[b], x1[:, b, :]).then_inc(out_done, 16)
            sp.wait_ge(out_done, 16 * NB)

        @block.gpsimd
        def _(gp):
            gp.memset(ident[:], 0.0).then_inc(pool, 1)
            gp.iota(iota[:], pattern=[[1, P]], base=0, channel_multiplier=0,
                    allow_small_or_imprecise_dtypes=True).then_inc(ident_ok, 1)
            gp.wait_ge(pool, 1)
            gp.affine_select(out=ident[:], in_=ident[:], compare_op=ALU.not_equal, fill=1.0, base=0,
                             pattern=[[-1, P]], channel_multiplier=1).then_inc(ident_ok, 1)
            gp.wait_ge(ident_ok, 2)
            gp.memset(hT[:, :, 0:CHUNK], 0.0).then_inc(zeros_ok, 1)
            gp.wait_ge(zeros_ok, 1)
            gp.memset(kT[:, 0:CHUNK], 0.0).then_inc(zeros_ok, 1)
            gp.wait_ge(zeros_ok, 2)
            gp.memset(wT[CHUNK:P, :, 0:CHUNK], 0.0).then_inc(zeros_ok, 1)

            def split_wq(h):
                for s in range(2):
                    gp.wait_ge(act_wq, 2 * h + s + 1)
                    gp.tensor_tensor(wqlo[s][:], wq[s][:], wqhi[s][:].bitcast(F32), ALU.subtract).then_inc(pool_wq, 1)

            def weigh_hits(h):
                gp.wait_ge(dve_pair, 2 * h + 2)
                for s in range(2):
                    gp.tensor_tensor(hit[s][:], hit[s][:],
                                     topf[:, s].unsqueeze(2).broadcast_to([P, NB, TOPK, TOPK]),
                                     ALU.mult).then_inc(pool_hit, 1)

            split_wq(0)
            with gp.Fori(1, PH) as h:
                split_wq(h)
                weigh_hits(h - 1)
            weigh_hits(PH - 1)

            gp.wait_ge(stored[0], 16 * NB // 2)
            gp.wait_ge(stored[1], 16 * NB // 2)

            def split_up(i, g):
                for s in range(2):
                    n = 2 * i + s
                    gp.wait_ge(act_uhi, n + 1)
                    gp.tensor_tensor(ulo[g][s][:], up[s][:], uhi[g][s][:].bitcast(F32), ALU.subtract).then_inc(pool_ulo, 1)

            with gp.Fori(0, TILES // (2 * GROUP)) as i:
                for g in range(2):
                    split_up(2 * i + g, g)

        @block.scalar
        def _(act):
            act.dma_start(sgw[:], sgu_w[0].rearrange("g i j -> i g j")).then_inc(misc_in, 16)
            act.dma_start(gg1[:], row(b_ada[:, 2 * D:3 * D])).then_inc(misc_in, 16)
            act.dma_start(gg2[:], row(b_ada[:, 5 * D:6 * D])).then_inc(misc_in, 16)
            act.dma_start(sgub[:].rearrange("p g i -> p (g i)"), row(sgu_b.rearrange("o g i -> o (g i)"))).then_inc(misc_in, 16)
            act.dma_start(sgun[:], row(sgu_norm)).then_inc(misc_in, 16)
            act.dma_start(sinks[:], row(attn_sinks)).then_inc(misc_in, 16)
            act.wait_ge(rows_in, 64)
            act.activation(rows[0:KT, :], rows[0:KT, :], ACT.Silu).then_inc(act_silu, 1)
            for b in range(NB):
                act.wait_ge(x_in[b], 16)
                act.activation(xn1[:, b, :], x1[:, b, :], ACT.Square, accum_out=ssq[:, b:b + 1]).then_inc(act_ss, 1)
            act.wait_ge(dve_ms, 1)
            act.activation(root[:, 0:NB], ssq[:, 0:NB], ACT.Sqrt).then_inc(act_root, 1)
            act.wait_ge(dve_mod, 1)
            act.wait_ge(zeros_ok, 3)
            for j in range(1, KT, 2):
                act.wait_ge(pe_h1, j + 1)
                act.activation(hT[:, j, CHUNK:], bank[1 + j % 4][:], ACT.Identity,
                               bias=modc[:, SH1 + j:SH1 + j + 1], scale=scale1[:, j:j + 1]).then_inc(act_h1, 1)
            for m in range(Z_JOBS):
                act.wait_ge(pe_z, m + 1)
                got = bank[Z_BANKS[m % 7]]
                if m < Z_U:
                    act.activation(sv[:, m, :], got[:], ACT.Gelu, accum_out=svsum[:, m:m + 1]).then_inc(act_z, 1)
                elif m < Z_K:
                    act.activation(uT[:, m - Z_U, :], got[:], ACT.Gelu).then_inc(act_z, 1)
                elif m == Z_K:
                    act.activation(kT[:, CHUNK:], got[:], ACT.Copy).then_inc(act_z, 1)
                elif m < Z_V:
                    act.activation(qT[:, m - Z_Q, :], got[:], ACT.Copy, scale=HD ** -0.5).then_inc(act_z, 1)
                else:
                    dst = v if m == Z_V else vs
                    act.activation(dst[:].rearrange("p b n -> p (b n)"), got[:], ACT.Copy).then_inc(act_z, 1)
                if m == Z_Q:
                    for b in range(NB):
                        act.wait_ge(dve_center, b + 1)
                        if b:
                            act.wait_ge(act_sv, b)
                        act.activation(ajunk, sv[:, b, :], ACT.Square,
                                       accum_out=ssq[:, 4 + b:5 + b]).then_inc(act_sv, 1)
            act.wait_ge(dve_ms, 2)
            act.activation(root[:, 4:8], ssq[:, 4:8], ACT.Sqrt).then_inc(act_root, 1)

            def scores_out(b):
                if b >= 2:
                    act.wait_ge(pe_pt, 2 * b - 2)
                for s in range(2):
                    act.wait_ge(pe_s, 2 * b + s + 1)
                    act.activation(s_sb[b % 2][:, 4 * s:4 * s + 4, :].rearrange("p h k -> p (h k)"),
                                   bank[1 + s][:], ACT.Copy).then_inc(act_s, 1)

            def exps(b):
                act.wait_ge(dve_sub, 2 * b + 2)
                flat = s_sb[b % 2][:].rearrange("p h k -> p (h k)")
                act.activation(flat, flat, ACT.Exp).then_inc(act_exp, 1)
                act.activation(asink[:], asink[:], ACT.Exp).then_inc(act_exp, 1)

            def transposed_out(b):
                if b >= 2:
                    act.wait_ge(pe_o, b - 1)
                for s in range(2):
                    act.wait_ge(pe_pt, 2 * b + s + 1)
                    act.activation(pT[b % 2][:, 4 * s:4 * s + 4, :].rearrange("p h k -> p (h k)"),
                                   bank[3 + s][:], ACT.Copy).then_inc(act_pt, 1)

            scores_out(0)
            exps(0)
            for b in range(NB):
                if b + 1 < NB:
                    scores_out(b + 1)
                transposed_out(b)
                if b + 1 < NB:
                    exps(b + 1)
                act.wait_ge(pe_o, b + 1)
                act.activation(catT[:, 0:4, b * P:(b + 1) * P],
                               bank[5][:].rearrange("p (h q) -> p h q", h=4), ACT.Copy).then_inc(act_o, 1)
            for b in range(NB):
                for s in range(2):
                    act.wait_ge(pe_mix, 2 * b + s + 1)
                    act.activation(xn2[:, b, s * 512:s * 512 + 512], bank[1 + 2 * (b % 2) + s][:], ACT.Square,
                                   accum_out=ssq[:, 8 + 2 * b + s:9 + 2 * b + s]).then_inc(act_ss, 1)
                act.wait_ge(dve_ms, 3 + 2 * b)
                act.activation(root[:, 8 + b:9 + b], ssq[:, 16 + b:17 + b], ACT.Sqrt).then_inc(act_root, 1)
                act.wait_ge(dve_x1, b + 1)
                act.activation(xn2[:, b, :], x1[:, b, :], ACT.Square, accum_out=ssq[:, 20 + b:21 + b]).then_inc(act_ss, 1)
                act.wait_ge(dve_ms, 4 + 2 * b)
                act.activation(root[:, 12 + b:13 + b], ssq[:, 20 + b:21 + b], ACT.Sqrt).then_inc(act_root, 1)
            for m in range(4):
                act.wait_ge(pe_keys, m + 1)
                act.activation(keysT[:, 4 * m:4 * m + 4, :].rearrange("p n k -> p (n k)"), bank[5 + m % 2][:],
                               ACT.Copy).then_inc(act_keys, 1)
            for j in range(KT):
                act.wait_ge(dve_htmp, j + 1)
                act.activation(h2hi[:, j, :], htmp[j % 2][:], ACT.Copy).then_inc(act_h2, 1)

            def head(h, first=False):
                for s in range(2):
                    act.wait_ge(wq_in[s], 16 * h + 16)
                    if not first:
                        act.wait_ge(pe_q, 2 * h)
                    act.activation(wqhi[s][:], wq[s][:], ACT.Copy).then_inc(act_wq, 1)
                for s in range(2):
                    act.wait_ge(pe_q, 2 * h + s + 1)
                    if not first:
                        act.wait_ge(pe_sc, 2 * h)
                    act.activation(pqT[s][:], bank[1 + s][:], ACT.Copy).then_inc(act_q, 1)
                for s in range(2):
                    act.wait_ge(pe_sc, 2 * h + s + 1)
                    if not first:
                        act.wait_ge(dve_top, h)
                    act.activation(score[s][:].rearrange("p b k -> p (b k)"), bank[3 + s][:],
                                   ACT.Copy).then_inc(act_sc, 1)

            head(0, first=True)
            with act.Fori(1, PH) as h:
                head(h)
            act.wait_ge(dve_bsub, 1)
            act.activation(best[:].rearrange("p b h k -> p (b h k)"),
                           pick[:, 2].rearrange("p b h k -> p (b h k)"), ACT.Exp).then_inc(act_gexp, 1)
            for k in range(3):
                act.wait_ge(pe_pick, k + 1)
                act.activation(pickT[:, k, :], bank[5 + k][:], ACT.Copy).then_inc(act_pick, 1)

            for b in range(NB):
                if b >= 2:
                    act.wait_ge(stored[b % 2], 16)
                with act.Fori(0, P // (2 * TB)) as i:
                    for u in range(2):
                        for s in range(2):
                            act.wait_ge(pe_g, b * 32 + 4 * i + 2 * u + s + 1)
                            act.activation(
                                stage[b % 2][:, :, bass.ds(i * (2 * TB) + u * TB + 4 * s, 4)].rearrange("p i t -> p t i"),
                                bank[1 + 2 * u + s][:].rearrange("p (t i) -> p t i", t=4),
                                ACT.Copy).then_inc(act_g, 1)

            for s in range(2):
                act.wait_ge(stored[s], 16 * NB // 2)

            def down_hi(n, s):
                for k in range(2):
                    act.wait_ge(pe_t, 2 * n + k + 1)
                    act.activation(dhi[s][:, 4 * k:4 * k + 4, :].rearrange("p k e -> p (k e)"), bank[k][:],
                                   ACT.Copy).then_inc(act_dhi, 1)

            def tile(i, g, s, first=False, second=False, last=False):
                n = 2 * i + s
                if not last:
                    down_hi(n + 1, 1 - s)
                if not first and not second:
                    act.wait_ge(pe_u, 8 * (i - 1))
                act.wait_ge(up_in[s], 16 * i + 16)
                act.activation(uhi[g][s][:], up[s][:], ACT.Copy).then_inc(act_uhi, 1)
                act.wait_ge(pe_d, n + 1)
                if not first:
                    act.wait_ge(dve_act, n - 1)
                act.activation(gel[s][:], bank[2 + s][:], ACT.Gelu).then_inc(act_gelu, 1)
                act.wait_ge(dve_act, n + 1)
                act.activation(ahi[g][s][:], acts[s][:], ACT.Copy).then_inc(act_ahi, 1)

            down_hi(0, 0)
            for g in range(2):
                for s in range(2):
                    tile(g, g, s, first=g == 0, second=g == 1)
            with act.Fori(1, TILES // 4 - 1) as i:
                for g in range(2):
                    for s in range(2):
                        tile(2 * i + g, g, s)
            for g in range(2):
                for s in range(2):
                    tile(TILES // 2 - 2 + g, g, s, last=g == 1 and s == 1)
            for b in range(NB):
                act.wait_ge(dve_y, 8 * (TILES // 2))
                act.activation(junk[:], y[:, b, :], ACT.Square, accum_out=ssq[:, 24 + b:25 + b]).then_inc(act_ss, 1)
                act.wait_ge(act_ss, NB + 3 * NB + b + 1)
            act.wait_ge(dve_ms, 3 + 2 * NB)
            act.activation(root[:, 16:20], ssq[:, 24:28], ACT.Sqrt).then_inc(act_root, 1)

        @block.vector
        def _(ve):
            ch = Chain(ve, dve)

            def mean_square(dst, src, width):
                return ve.tensor_scalar(dst, src, 1.0 / width, EPS, ALU.mult, ALU.add)

            ve.wait_ge(pe_rows, 1)
            ch.link(ve.tensor_copy(columns[:], bank[7][:, 0:ROWS]))
            ch.link(ve.tensor_copy(c_col[:], columns[:, 0:KT]))
            ve.tensor_copy(c_bc[:], c_col[:].unsqueeze(2).broadcast_to([P, KT, P])).then_inc(dve_c, 1)
            ve.wait_ge(zeros_ok, 3)
            ve.wait_ge(pe_wT, 1)
            got = bank[6][:].rearrange("p (g i) -> p g i", g=GROUPS)
            ch.link(ve.tensor_copy(wT[0:CHUNK, :, :], got[0:CHUNK]))
            ve.tensor_copy(wT[CHUNK:P, :, CHUNK:P], got[CHUNK:P, :, CHUNK:P]).then_inc(dve_wT, 1)
            ve.wait_ge(act_ss, NB)
            mean_square(ssq[:, 0:NB], ssq[:, 0:NB], D).then_inc(dve_ms, 1)
            ve.wait_ge(act_root, 1)
            ch.link(ve.reciprocal(root[:, 0:NB], root[:, 0:NB]))
            for b in range(NB):
                ve.tensor_scalar(xn1[:, b, :], x1[:, b, :], root[:, b:b + 1], None, ALU.mult).then_inc(dve_xn1, 1)

            def add_bias(first):
                ch.mark(ve.tensor_tensor(modc[:, first:first + KT], bank[0][:, first:first + KT],
                                         columns[:, ROW_B + first:ROW_B + first + KT], ALU.add))

            def make_scale(dst, first, row_g):
                return ve.scalar_tensor_tensor(out=dst[:], in0=modc[:, first:first + KT], scalar=1.0,
                                               in1=columns[:, row_g:row_g + KT], op0=ALU.add, op1=ALU.mult)

            ve.wait_ge(ada_used, 4)
            add_bias(SC1)
            add_bias(SH1)
            ch.wait()
            make_scale(scale1, SC1, ROW_G1).then_inc(dve_mod, 1)
            ve.wait_ge(dve_mod, 1)
            for j in range(0, KT, 2):
                ve.wait_ge(pe_h1, j + 1)
                ve.tensor_scalar(hT[:, j, CHUNK:], bank[1 + j % 4][:], scale1[:, j:j + 1],
                                 modc[:, SH1 + j:SH1 + j + 1], ALU.mult, ALU.add).then_inc(dve_h1, 1)
            ve.wait_ge(act_z, Z_U)
            ch.link(ve.tensor_scalar(svsum[:], svsum[:], -1.0 / SGU, None, ALU.mult))
            for b in range(NB):
                ve.tensor_scalar(sv[:, b, :], sv[:, b, :], svsum[:, b:b + 1], None, ALU.add).then_inc(dve_center, 1)
            ve.wait_ge(act_sv, NB)
            mean_square(ssq[:, 4:8], ssq[:, 4:8], SGU).then_inc(dve_ms, 1)
            ve.wait_ge(act_root, 2)
            ch.link(ve.reciprocal(root[:, 4:8], root[:, 4:8]))
            ve.wait_ge(misc_in, 16 * 6)
            for b in range(NB):
                ve.scalar_tensor_tensor(out=sv[:, b, :], in0=sv[:, b, :], scalar=root[:, 4 + b:5 + b], in1=sgun[:],
                                        op0=ALU.mult, op1=ALU.mult).then_inc(dve_vn, 1)

            def softmax_front(b):
                s = s_sb[b % 2]
                ve.wait_ge(act_s, 2 * b + 2)
                if b == 0:
                    ch.link(ve.memset(s[0:CHUNK, :, 0:CHUNK], LOWEST))
                ch.link(ve.tensor_reduce(out=amax[:], in_=s[:], axis=AXX, op=ALU.max))
                ch.link(ve.tensor_tensor(amax[:], amax[:], sinks[:], ALU.max))
                ve.tensor_tensor(asink[:], sinks[:], amax[:], ALU.subtract).then_inc(dve_sub, 1)
                ve.tensor_tensor(s[:], s[:], amax[:].unsqueeze(2).broadcast_to([P, HEADS, P]),
                                 ALU.subtract).then_inc(dve_sub, 1)

            def softmax_back(b):
                s = s_sb[b % 2]
                ve.wait_ge(act_exp, 2 * b + 2)
                ch.link(ve.tensor_reduce(out=asum[:], in_=s[:], axis=AXX, op=ALU.add))
                ch.link(ve.tensor_tensor(asum[:], asum[:], asink[:], ALU.add))
                ch.link(ve.reciprocal(asum[:], asum[:]))
                ve.tensor_tensor(s[:], s[:], asum[:].unsqueeze(2).broadcast_to([P, HEADS, P]), ALU.mult).then_inc(dve_p, 1)

            def spatial(g):
                ve.wait_ge(pe_sgu, g + 1)
                dst = catT[:, 4 + g, :]
                ch.link(ve.tensor_tensor(dst.rearrange("p (b i) -> p b i", b=NB),
                                         bank[6][:].rearrange("p (b i) -> p b i", b=NB),
                                         sgub[:, g].unsqueeze(1).broadcast_to([P, NB, P]), ALU.add))
                ve.tensor_tensor(dst, dst, uT[:, g, :], ALU.mult).then_inc(dve_sgu, 1)

            def gate_half(n, gg, gp, s):
                ve.wait_ge(ada_used, n + 1)
                part = gg[:, s * 512:s * 512 + 512]
                ch.link(ve.tensor_tensor(part, bank[7][:], part, ALU.add))
                ve.wait_ge(gp_in, 32)
                ve.tensor_tensor(part, part, gp[:, s * 512:s * 512 + 512], ALU.mult).then_inc(dve_gg, 1)

            softmax_front(0)
            spatial(0)
            softmax_back(0)
            gate_half(4, gg1, gp1, 0)
            softmax_front(1)
            spatial(1)
            softmax_back(1)
            gate_half(5, gg1, gp1, 1)
            softmax_front(2)
            spatial(2)
            softmax_back(2)
            softmax_front(3)
            spatial(3)
            softmax_back(3)
            for b in range(NB):
                ve.wait_ge(act_ss, NB + 3 * b + 2)
                ch.link(ve.tensor_tensor(ssq[:, 16 + b:17 + b], ssq[:, 8 + 2 * b:9 + 2 * b], ssq[:, 9 + 2 * b:10 + 2 * b], ALU.add))
                mean_square(ssq[:, 16 + b:17 + b], ssq[:, 16 + b:17 + b], D).then_inc(dve_ms, 1)
                ve.wait_ge(act_root, 3 + 2 * b)
                ch.link(ve.reciprocal(root[:, 8 + b:9 + b], root[:, 8 + b:9 + b]))
                if b == 0:
                    ve.wait_ge(dve_gg, 2)
                for s in range(2):
                    half = slice(s * 512, s * 512 + 512)
                    ve.scalar_tensor_tensor(out=xn2[:, b, half], in0=bank[1 + 2 * (b % 2) + s][:],
                                            scalar=root[:, 8 + b:9 + b], in1=gg1[:, half],
                                            op0=ALU.mult, op1=ALU.mult).then_inc(dve_mix, 1)
                ve.wait_ge(dve_mix, 2 * b + 2)
                ve.tensor_tensor(x1[:, b, :], x1[:, b, :], xn2[:, b, :], ALU.add).then_inc(dve_x1, 1)
                ve.wait_ge(act_ss, NB + 3 * b + 3)
                mean_square(ssq[:, 20 + b:21 + b], ssq[:, 20 + b:21 + b], D).then_inc(dve_ms, 1)
                ve.wait_ge(act_root, 4 + 2 * b)
                ch.link(ve.reciprocal(root[:, 12 + b:13 + b], root[:, 12 + b:13 + b]))
                ve.tensor_scalar(xn2[:, b, :], x1[:, b, :], root[:, 12 + b:13 + b], None, ALU.mult).then_inc(dve_xn2, 1)
            gate_half(10, gg2, gp2, 0)
            gate_half(11, gg2, gp2, 1)
            add_bias(SC2)
            add_bias(SH2)
            ch.wait()
            ch.link(make_scale(scale2, SC2, ROW_G2))
            for j in range(KT + 1):
                if j < KT:
                    ve.wait_ge(pe_h2, j + 1)
                    if j >= 2:
                        ve.wait_ge(dve_h2, j - 1)
                    ve.tensor_scalar(htmp[j % 2][:], bank[1 + j % 4][:], scale2[:, j:j + 1],
                                     modc[:, SH2 + j:SH2 + j + 1], ALU.mult, ALU.add).then_inc(dve_htmp, 1)
                if j >= 1:
                    ve.wait_ge(act_h2, j)
                    ve.tensor_tensor(h2lo[:, j - 1, :], htmp[(j - 1) % 2][:], h2hi[:, j - 1, :].bitcast(F32),
                                     ALU.subtract).then_inc(dve_h2, 1)

            def stand_alone():
                ve.nop(nofuse=True)

            def top16(values, found, places):
                for half in range(2):
                    k = slice(8 * half, 8 * half + 8)
                    stand_alone()
                    for b in range(NB):
                        ch.mark(ve.max(found(b)[:, k], values(b)))
                    ch.wait()
                    stand_alone()
                    for b in range(NB):
                        ch.mark(ve.max_index(places(b)[:, k], found(b)[:, k], values(b)))
                    if half == 0:
                        ch.wait()
                        stand_alone()
                        for b in range(NB):
                            ch.mark(ve.match_replace(out=values(b), in_to_replace=found(b)[:, k], in_values=values(b),
                                                     imm_value=LOWEST))
                        ch.wait()

            def halves(h, first=False):
                for s in range(2):
                    ve.wait_ge(act_sc, 2 * h + s + 1)
                    top16(lambda b: score[s][:, b, :], lambda b: top[:, s, b, :], lambda b: topi[:, s, b, :])
                ch.wait()
                if not first:
                    ve.wait_ge(pool_hit, 2 * h)
                ve.tensor_copy(topf[:], topi[:]).then_inc(dve_top, 1)

            def sums(h):
                ve.wait_ge(dve_top, h + 1)
                ch.link(ve.tensor_tensor(cand[:], top[:, 0].unsqueeze(3).broadcast_to([P, NB, TOPK, TOPK]),
                                         top[:, 1].unsqueeze(2).broadcast_to([P, NB, TOPK, TOPK]), ALU.add))
                top16(lambda b: cand[:, b].rearrange("p i j -> p (i j)"), lambda b: bests[:, b, :],
                      lambda b: besti[:, b, :])
                ch.wait()
                ch.mark(ve.tensor_copy(best[:, :, bass.ds(h, 1), :].rearrange("p b o k -> p b (o k)"), bests[:]))
                ch.mark(ve.tensor_single_scalar(pair[:, 0], besti[:], 4, op=ALU.logical_shift_right))
                ch.mark(ve.tensor_single_scalar(pair[:, 1], besti[:], 15, op=ALU.bitwise_and))
                ch.wait()
                ch.link(ve.tensor_copy(pairf[:], pair[:]))
                for s in range(2):
                    ve.tensor_tensor(hit[s][:], pairf[:, s].unsqueeze(3).broadcast_to([P, NB, TOPK, TOPK]),
                                     iota[:, 0:TOPK].unsqueeze(1).unsqueeze(1).broadcast_to([P, NB, TOPK, TOPK]),
                                     ALU.is_equal).then_inc(dve_pair, 1)

            def select(h):
                ve.wait_ge(pool_hit, 2 * h + 2)
                for s in range(2):
                    ve.tensor_reduce(out=pick[:, s, :, bass.ds(h, 1), :].rearrange("p b o k -> p b (o k)"),
                                     in_=hit[s][:], axis=AXX, op=ALU.add).then_inc(dve_sel, 1)

            halves(0, first=True)
            sums(0)
            with ve.Fori(1, PH) as h:
                ch.enter(h - 1, HEAD_STEPS)
                halves(h)
                select(h - 1)
                sums(h)
                ch.leave(PH - 1)
            select(PH - 1)
            first = best[:, :, :, 0:1].broadcast_to([P, NB, PH, TOPK])
            ve.tensor_tensor(pick[:, 2], best[:], first, ALU.subtract).then_inc(dve_bsub, 1)
            ve.wait_ge(act_gexp, 1)
            ch.link(ve.tensor_reduce(out=bsum[:], in_=best[:], axis=AXX, op=ALU.add))
            ch.link(ve.reciprocal(bsum[:], bsum[:]))
            ve.tensor_tensor(pick[:, 2], best[:], bsum[:].unsqueeze(3).broadcast_to([P, NB, PH, TOPK]),
                             ALU.mult).then_inc(dve_pick, 1)

            ve.wait_ge(act_pick, 3)

            def hot_rows(m, u):
                tokens = bass.ds(m * TB, TB)
                ve.tensor_tensor(onehot2[u][:], iota[:].unsqueeze(1).broadcast_to([P, TB, KEYS]),
                                 pickT[:, 1, tokens].unsqueeze(2).broadcast_to([P, TB, KEYS]), ALU.is_equal).then_inc(dve_hot, 1)
                for k in range(TB):
                    ve.tensor_scalar(gated1[u][:, k, :], iota[:], pickT[:, 0, bass.ds(m * TB + k, 1)],
                                     pickT[:, 2, bass.ds(m * TB + k, 1)], ALU.is_equal, ALU.mult).then_inc(dve_hot, 1)

            for u in range(2):
                hot_rows(u, u)
            with ve.Fori(1, T // (2 * TB)) as i:
                for u in range(2):
                    ve.wait_ge(pe_g, 4 * i + 2 * u - 2)
                    hot_rows(2 * i + u, u)

            for s in range(2):
                ve.wait_ge(stored[s], 16 * NB // 2)
            ch.link(ve.memset(y[:], 0.0))

            def down_lo(n, s):
                if n is not None:
                    ve.wait_ge(pe_d, n - 1)
                for k in range(2):
                    ve.wait_ge(act_dhi, 2 * (0 if n is None else n) + k + 1)
                    part = slice(4 * k, 4 * k + 4)
                    ve.tensor_tensor(dlo[s][:, part, :].rearrange("p k e -> p (k e)"), bank[k][:],
                                     dhi[s][:, part, :].rearrange("p k e -> p (k e)").bitcast(F32),
                                     ALU.subtract).then_inc(dve_dlo, 1)

            def add_y(i, q):
                ve.wait_ge(pe_u, 8 * i + q + 1)
                part = y[:, q // 2, (q % 2) * 512:(q % 2) * 512 + 512]
                ve.tensor_tensor(part, part, bank[4 + q % 4][:], ALU.add).then_inc(dve_y, 1)

            def tile(i, g, s, first=False, last=False):
                n = 2 * i + s
                if not last:
                    down_lo(n + 1, 1 - s)
                if not first:
                    for q in range(4 * s, 4 * s + 4):
                        add_y(i - 1, q)
                ve.wait_ge(act_gelu, n + 1)
                ve.wait_ge(gate_in[s], 16 * i + 16)
                if not first:
                    ve.wait_ge(dve_alo, n - 1)
                ve.tensor_tensor(acts[s][:], gel[s][:], gate[s][:], ALU.mult).then_inc(dve_act, 1)
                ve.wait_ge(act_ahi, n + 1)
                ve.tensor_tensor(alo[g][s][:], acts[s][:], ahi[g][s][:].bitcast(F32), ALU.subtract).then_inc(dve_alo, 1)

            down_lo(None, 0)
            for g in range(2):
                for s in range(2):
                    tile(g, g, s, first=g == 0)
            with ve.Fori(1, TILES // 4 - 1) as i:
                for g in range(2):
                    for s in range(2):
                        tile(2 * i + g, g, s)
            for g in range(2):
                for s in range(2):
                    tile(TILES // 2 - 2 + g, g, s, last=g == 1 and s == 1)
            for q in range(8):
                add_y(TILES // 2 - 1, q)
            ve.wait_ge(act_ss, NB + 3 * NB + NB)
            mean_square(ssq[:, 24:28], ssq[:, 24:28], D).then_inc(dve_ms, 1)
            ve.wait_ge(act_root, 2 + 2 * NB + 1)
            ch.link(ve.reciprocal(root[:, 16:20], root[:, 16:20]))
            for b in range(NB):
                ch.mark(ve.scalar_tensor_tensor(out=y[:, b, :], in0=y[:, b, :], scalar=root[:, 16 + b:17 + b], in1=gg2[:],
                                                op0=ALU.mult, op1=ALU.mult))
                ch.wait()
                ve.tensor_tensor(x1[:, b, :], x1[:, b, :], y[:, b, :], ALU.add).then_inc(dve_x1, 1)

        @block.tensor
        def _(pe):
            pe.wait_ge(act_silu, 1)
            pe.wait_ge(ident_ok, 2)
            pe.transpose(bank[7][:, 0:ROWS], rows[0:ROWS, :], ident[0:ROWS, 0:ROWS]).then_inc(pe_rows, 1)
            pe.wait_ge(misc_in, 16 * 6)
            for g in range(GROUPS):
                last = pe.transpose(bank[6][:, g * P:(g + 1) * P], sgw[:, g, :], ident[:])
            last.then_inc(pe_wT, 1)
            pe.wait_ge(dve_c, 1)

            def ada_wait(n):
                pe.wait_ge(ada_in[n % ADA_SLOTS], 16 * (n // ADA_SLOTS + 1))

            def ada_columns(n):
                ada_wait(n)
                for j in range(4):
                    col = 4 * ADA_ORDER[n] + j
                    for k in range(KT):
                        last = pe.matmul(bank[0][:, col:col + 1], ada[n % ADA_SLOTS][:, k, j * P:(j + 1) * P],
                                         c_col[:, k:k + 1], start=k == 0, stop=k == KT - 1)
                last.then_inc(ada_used, 1)

            def ada_row(n):
                ada_wait(n)
                for k in range(KT):
                    last = pe.matmul(bank[7][:], c_bc[:, k, :], ada[n % ADA_SLOTS][:, k, :], start=k == 0, stop=k == KT - 1)
                last.then_inc(ada_used, 1)

            for n in range(4):
                ada_columns(n)
            for j in range(KT):
                if j == 0:
                    pe.wait_ge(dve_xn1, NB)
                if j >= 4:
                    pe.wait_ge(act_h1 if j % 2 else dve_h1, (j - 4) // 2 + 1)
                for b in range(NB):
                    last = pe.transpose(bank[1 + j % 4][:, b * P:(b + 1) * P], xn1[:, b, j * P:(j + 1) * P], ident[:])
                last.then_inc(pe_h1, 1)
            pe.wait_ge(act_h1, 4)
            pe.wait_ge(dve_h1, 4)
            pe.wait_ge(dve_wT, 1)
            pe.wait_ge(w_in_in, 16 * (4 + 2 * KT))
            for m in range(Z_JOBS):
                if m >= 7:
                    pe.wait_ge(act_z, m - 6)
                got = bank[Z_BANKS[m % 7]]
                if m < Z_U:
                    for k in range(KT):
                        last = pe.matmul(got[:], hT[:, k, CHUNK + m * P:CHUNK + (m + 1) * P],
                                         w_in_sb[:, k, SV_AT:SV_AT + SGU], start=k == 0, stop=k == KT - 1)
                elif m < Z_V:
                    for k in range(KT):
                        if m < Z_K:
                            w = w_in_sb[:, k, U_AT + (m - Z_U) * P:U_AT + (m - Z_U + 1) * P]
                        elif m == Z_K:
                            w = w_in_sb[:, k, K_AT:K_AT + KVW]
                        else:
                            w = w_in_sb[:, k, (m - Z_Q) * P:(m - Z_Q + 1) * P]
                        last = pe.matmul(got[:], w, hT[:, k, CHUNK:], start=k == 0, stop=k == KT - 1)
                else:
                    at = CHUNK if m == Z_V else 0
                    for b in range(NB):
                        for k in range(KT):
                            last = pe.matmul(got[:, b * P:(b + 1) * P], hT[:, k, at + b * P:at + (b + 1) * P],
                                             w_in_sb[:, k, V_AT:V_AT + KVW], start=k == 0, stop=k == KT - 1)
                last.then_inc(pe_z, 1)

            def scores(b):
                if b >= 1:
                    pe.wait_ge(act_s, 2 * b)
                for s in range(2):
                    side = slice(s * HD, (s + 1) * HD)
                    for j in range(4):
                        for q in range(2):
                            at = b * P + q * CHUNK
                            last = pe.matmul(bank[1 + s][q * CHUNK:(q + 1) * CHUNK, j * P:(j + 1) * P],
                                             qT[side, j, at:at + CHUNK], kT[side, at:at + P], start=True, stop=True)
                    last.then_inc(pe_s, 1)

            def transpose_probs(b):
                pe.wait_ge(dve_p, b + 1)
                if b >= 1:
                    pe.wait_ge(act_pt, 2 * b)
                for s in range(2):
                    for j in range(4):
                        last = pe.transpose(bank[3 + s][:, j * P:(j + 1) * P], s_sb[b % 2][:, 4 * s + j, :], ident[:])
                    last.then_inc(pe_pt, 1)

            def attend(b):
                pe.wait_ge(act_pt, 2 * b + 2)
                if b >= 1:
                    pe.wait_ge(act_o, b)
                for h in range(HEADS):
                    for q in range(2):
                        last = pe.matmul(bank[5][(h % 2) * HD:(h % 2 + 1) * HD, (h // 2) * P + q * CHUNK:(h // 2) * P + (q + 1) * CHUNK],
                                         (v if q else vs)[:, b, (h // 4) * HD:(h // 4 + 1) * HD],
                                         pT[b % 2][:, h, q * CHUNK:(q + 1) * CHUNK], start=True, stop=True)
                last.then_inc(pe_o, 1)

            def mix_positions(g):
                pe.wait_ge(dve_vn, NB)
                if g >= 1:
                    pe.wait_ge(dve_sgu, g)
                for b in range(NB):
                    last = pe.matmul(bank[6][:, b * P:(b + 1) * P], sv[:, b, g * P:(g + 1) * P], wT[:, g, :],
                                     start=True, stop=True)
                last.then_inc(pe_sgu, 1)

            pe.wait_ge(act_z, Z_JOBS)
            scores(0)
            mix_positions(0)
            ada_row(4)
            scores(1)
            transpose_probs(0)
            mix_positions(1)
            attend(0)
            pe.wait_ge(dve_gg, 1)
            ada_row(5)
            scores(2)
            transpose_probs(1)
            mix_positions(2)
            attend(1)
            ada_columns(6)
            scores(3)
            transpose_probs(2)
            mix_positions(3)
            attend(2)
            ada_columns(7)
            transpose_probs(3)
            attend(3)
            pe.wait_ge(w_out_in, 32)
            pe.wait_ge(act_o, NB)
            pe.wait_ge(dve_sgu, GROUPS)
            for b in range(NB):
                for s in range(2):
                    if b >= 2:
                        pe.wait_ge(dve_mix, 2 * (b - 2) + s + 1)
                    for k in range(KT):
                        last = pe.matmul(bank[1 + 2 * (b % 2) + s][:], catT[:, k, b * P:(b + 1) * P],
                                         w_out_sb[:, k, s * 512:s * 512 + 512], start=k == 0, stop=k == KT - 1)
                    last.then_inc(pe_mix, 1)
                if b < 2:
                    ada_columns(8 + b)
            pe.wait_ge(dve_gg, 2)
            ada_row(10)
            pe.wait_ge(dve_gg, 3)
            ada_row(11)
            pe.wait_ge(keys_in, 16)
            for m in range(4):
                if m >= 2:
                    pe.wait_ge(act_keys, m - 1)
                for k in range(4):
                    last = pe.transpose(bank[5 + m % 2][:, k * P:(k + 1) * P], keys[:, 4 * m + k, :], ident[:])
                last.then_inc(pe_keys, 1)
            pe.wait_ge(dve_xn2, NB)
            for j in range(KT):
                if j >= 4:
                    pe.wait_ge(dve_htmp, j - 3)
                for b in range(NB):
                    last = pe.transpose(bank[1 + j % 4][:, b * P:(b + 1) * P], xn2[:, b, j * P:(j + 1) * P], ident[:])
                last.then_inc(pe_h2, 1)
            pe.wait_ge(act_h2, KT)
            pe.wait_ge(dve_h2, KT)
            pe.wait_ge(act_keys, 4)
            def head(h, first=False):
                for s in range(2):
                    pe.wait_ge(act_wq, 2 * h + s + 1)
                    pe.wait_ge(pool_wq, 2 * h + s + 1)
                    for k in range(KT):
                        pe.matmul(bank[1 + s][:], wqhi[s][:, k, :], h2hi[:, k, :], start=k == 0, stop=False)
                        pe.matmul(bank[1 + s][:], wqhi[s][:, k, :], h2lo[:, k, :], start=False, stop=False)
                        last = pe.matmul(bank[1 + s][:], wqlo[s][:, k, :], h2hi[:, k, :], start=False, stop=k == KT - 1)
                    last.then_inc(pe_q, 1)
                for s in range(2):
                    pe.wait_ge(act_q, 2 * h + s + 1)
                    if not first:
                        pe.wait_ge(act_sc, 2 * h)
                    for b in range(NB):
                        last = pe.matmul(bank[3 + s][:, b * P:(b + 1) * P], pqT[s][:, b * P:(b + 1) * P],
                                         keysT[:, bass.ds(2 * h + s, 1), :].rearrange("p o k -> p (o k)"),
                                         start=True, stop=True)
                    last.then_inc(pe_sc, 1)

            head(0, first=True)
            with pe.Fori(1, PH) as h:
                head(h)
            pe.wait_ge(dve_pick, 1)
            pe.wait_ge(dve_sel, 2 * PH)
            for k in range(3):
                for b in range(NB):
                    last = pe.transpose(bank[5 + k][:, b * P:(b + 1) * P], pick[:, k, b].rearrange("p h k -> p (h k)"), ident[:])
                last.then_inc(pe_pick, 1)

            def gate_products(m, u, first=False):
                pe.wait_ge(dve_hot, 9 * m + 9)
                for s in range(2):
                    if not first:
                        pe.wait_ge(act_g, 2 * m + s - 3)
                    for k in range(4):
                        last = pe.matmul(bank[1 + 2 * u + s][:, k * P:(k + 1) * P], onehot2[u][:, 4 * s + k, :],
                                         gated1[u][:, 4 * s + k, :], start=True, stop=True)
                    last.then_inc(pe_g, 1)

            for u in range(2):
                gate_products(u, u, first=True)
            with pe.Fori(1, T // (2 * TB)) as i:
                for u in range(2):
                    gate_products(2 * i + u, u)


            def transpose_down(n, s, first=False):
                pe.wait_ge(down_in[s], 8 * (n - s) + 16)
                for k in range(2):
                    if not first:
                        pe.wait_ge(dve_dlo, 2 * n + k - 1)
                    for q in range(4):
                        at = (4 * k + q) * P
                        last = pe.transpose(bank[k][:, q * P:(q + 1) * P], down[s][:, at:at + P], ident[:])
                    last.then_inc(pe_t, 1)

            def multiply_down(n, s, first=False):
                pe.wait_ge(dve_dlo, 2 * n + 2)
                if not first:
                    pe.wait_ge(act_gelu, n - 1)
                for k in range(KT):
                    pe.matmul(bank[2 + s][:], dhi[s][:, k, :], h2hi[:, k, :], start=k == 0, stop=False)
                    pe.matmul(bank[2 + s][:], dhi[s][:, k, :], h2lo[:, k, :], start=False, stop=False)
                    last = pe.matmul(bank[2 + s][:], dlo[s][:, k, :], h2hi[:, k, :], start=False, stop=k == KT - 1)
                last.then_inc(pe_d, 1)

            def multiply_up(i, g, q, first=False):
                if q < 4 and not first:
                    pe.wait_ge(dve_y, 8 * i + q - 3)
                elif q >= 4:
                    pe.wait_ge(dve_y, 8 * i + q - 3)
                rows_, half = slice((q // 2) * P, (q // 2 + 1) * P), slice((q % 2) * 512, (q % 2) * 512 + 512)
                for s in range(GROUP):
                    pe.matmul(bank[4 + q % 4][:], ahi[g][s][:, rows_], uhi[g][s][:, half], start=s == 0, stop=False)
                    pe.matmul(bank[4 + q % 4][:], ahi[g][s][:, rows_], ulo[g][s][:, half], start=False, stop=False)
                    last = pe.matmul(bank[4 + q % 4][:], alo[g][s][:, rows_], uhi[g][s][:, half],
                                     start=False, stop=s == GROUP - 1)
                last.then_inc(pe_u, 1)

            def group_ready(i):
                pe.wait_ge(dve_alo, 2 * i + 2)
                pe.wait_ge(pool_ulo, 2 * i + 2)

            def tile(i, g, s, first=False, second=False, last=False):
                n = 2 * i + s
                if not last:
                    transpose_down(n + 1, 1 - s)
                multiply_down(n, s, first=first)
                if not first:
                    if s == 0:
                        group_ready(i - 1)
                    for q in range(4 * s, 4 * s + 4):
                        multiply_up(i - 1, 1 - g, q, first=second)

            transpose_down(0, 0, first=True)
            for g in range(2):
                for s in range(2):
                    tile(g, g, s, first=g == 0, second=g == 1)
            with pe.Fori(1, TILES // 4 - 1) as i:
                for g in range(2):
                    for s in range(2):
                        tile(2 * i + g, g, s)
            for g in range(2):
                for s in range(2):
                    tile(TILES // 2 - 2 + g, g, s, last=g == 1 and s == 1)
            group_ready(TILES // 2 - 1)
            for q in range(8):
                multiply_up(TILES // 2 - 1, 1, q)


_INS = ["x", "c", "w_ada", "b_ada", "g_pre_mix", "g_post_mix", "g_pre_ffn", "g_post_ffn", "w_in", "attn_sinks",
        "sgu_norm", "sgu_w", "sgu_b", "w_out", "peer_query", "peer_keys", "peer_down", "peer_up"]


def kernel(**inputs):
    import numpy as np
    import concourse.bacc as bacc
    from concourse.bass_utils import run_bass_kernel_spmd

    nc = bacc.Bacc("TRN2", target_bir_lowering=False, num_devices=1)
    arrays = {f"in_{n}": np.ascontiguousarray(inputs[n]) for n in _INS}
    args = [nc.dram_tensor(n, a.shape, mybir.dt.from_np(a.dtype), kind="ExternalInput").ap() for n, a in arrays.items()]
    result = nc.dram_tensor("out_x", arrays["in_x"].shape, F32, kind="ExternalOutput").ap()
    build_block(nc, *args, result)
    ran = run_bass_kernel_spmd(nc, [arrays], core_ids=[0])
    return ran.results[0]["out_x"]
```

```python
from contextlib import ExitStack

import concourse.bass as bass
from concourse import mybir

F32 = mybir.dt.float32
F32R = mybir.dt.float32r
U32 = mybir.dt.uint32
ALU = mybir.AluOpType
ACT = mybir.ActivationFunctionType
AXX = mybir.AxisListType.X

P = 128
D = 1024
T = 512
KT = D // P
NB = T // P
HEADS, KV_HEADS, HD = 8, 2, 64
CHUNK = 64
ATT = HEADS * HD
KVW = KV_HEADS * HD
SGU = D - ATT
GROUPS = SGU // P
IN_W = ATT + 2 * KVW + 2 * SGU
K_AT, V_AT = ATT, ATT + KVW
U_AT, SV_AT = ATT + 2 * KVW, ATT + 2 * KVW + SGU
PH = 8
TOPK = 16
KEYS = 128
TILES = KEYS
EPS = 1e-6
LOWEST = -3.0e38

ADA_COLUMN_A = [2, 3, 0, 1]
ADA_ROW_1 = [4, 5]
ADA_COLUMN_B = [8, 9, 6, 7]
ADA_ROW_2 = [10, 11]
ADA_ORDER = ADA_COLUMN_A + ADA_ROW_1 + ADA_COLUMN_B + ADA_ROW_2
ADA_SLOTS = 3
SH1, SC1, SH2, SC2 = 0, 8, 24, 32
ROW_C, ROW_B, ROW_G1, ROW_G2, ROWS = 0, 8, 56, 64, 72

Z_K, Z_Q, Z_V, Z_VS, Z_SV, Z_U, Z_JOBS = 0, 1, 5, 6, 7, 11, 15
Z_BANKS = [5, 6, 1, 2, 3] + [5, 6] * 5
Z_ADA = {2: 4, 3: 5, 4: 6, 5: 7, 6: 8, 7: 9, 9: 10, 10: 11}
HEAD_STEPS = 3 * 20 + 14
TB = 8
GB = NB - 1
TD = GB * P
PICKS = PH * TOPK
ROWS_16, ROWS_4 = 3, 8
AT_4 = ROWS_16 * TOPK
AT_1 = AT_4 + (ROWS_4 - ROWS_16) * 4
SUMS = AT_1 + TOPK - ROWS_4
OUTS = 2 * GB
GROUP = 2


class Chain:

    def __init__(self, eng, sem):
        self.eng, self.sem, self.base, self.n = eng, sem, 0, 0

    def mark(self, ins):
        ins.then_inc(self.sem, 1)
        self.n += 1

    def wait(self):
        self.eng.wait_ge(self.sem, self.base + self.n)

    def link(self, ins):
        self.mark(ins)
        self.wait()

    def enter(self, turn, per_turn):
        self.before, self.per_turn = self.base + self.n, per_turn
        self.base, self.n = turn * per_turn + self.before, 0

    def leave(self, turns):
        assert self.n == self.per_turn, self.n
        self.base, self.n = self.before + turns * self.per_turn, 0


class Region:

    def __init__(self, nc, start, limit):
        self.nc, self.at, self.limit = nc, start, limit

    def __call__(self, name, shape, dt=F32):
        size = 4
        for n in shape:
            size *= n
        t = self.nc.alloc_sbuf_tensor_at(name, [P] + list(shape), dt, offset=self.at)
        self.at += -(-size // 32) * 32
        assert self.at <= self.limit, (name, self.at - self.limit)
        return t


def build_block(nc, x, c, w_ada, b_ada, g_pre_mix, g_post_mix, g_pre_ffn, g_post_ffn, w_in, attn_sinks,
                sgu_norm, sgu_w, sgu_b, w_out, peer_query, peer_keys, peer_down, peer_up, out):
    ctx = ExitStack()
    with ctx:
        def sem(name):
            return ctx.enter_context(nc.semaphore(name))

        base, limit = -(-nc.sbuf_base // 32) * 32, nc.sbuf_usable_end
        kept = Region(nc, base, limit)
        ident = kept("ident", [P])
        iota = kept("iota", [P])
        ones = kept("ones", [P])
        columns = kept("columns", [ROWS])
        modc = kept("modc", [48])
        scale1 = kept("scale1", [KT])
        scale2 = kept("scale2", [KT])
        ssq = kept("ssq", [32])
        root = kept("root", [32])
        svsum = kept("svsum", [NB])
        x1 = kept("x1", [NB, D])
        gg2 = kept("gg2", [D])
        h2nat_at = kept.at
        h2nat = kept("h2nat", [D])
        ids_at = kept.at
        ids = kept("ids", [PICKS], U32)
        gate3 = kept("gate3", [PICKS])
        h2_at = kept.at
        h2hi = kept("h2hi", [KT, T], F32R)
        h2lo = kept("h2lo", [KT, T], F32R)
        rest_at = kept.at

        r = Region(nc, h2_at, rest_at)
        qT = r("qT", [4, T])
        uT_at = r.at
        uT = r("uT", [GROUPS, T])
        catT_at = r.at
        catT = r("catT", [KT, T])
        xn1 = Region(nc, catT_at, rest_at)("xn1", [NB, D])
        r = Region(nc, rest_at, limit)
        gg1 = r("gg1", [D])
        hT_at = r.at
        HTW = CHUNK + T
        hT = r("hT", [KT, HTW])
        w_in_at = r.at
        w_in_sb = r("w_in_sb", [KT, IN_W])
        ada_at = r.at
        ada = [r(f"ada{i}", [KT, 512]) for i in range(ADA_SLOTS)]
        kT = r("kT", [HTW])
        v = r("v", [NB, KVW])
        vs = r("vs", [NB, KVW])
        sv = r("sv", [NB, SGU])
        wT = r("wT", [GROUPS, P])
        c_col = r("c_col", [KT])
        part = [r("part0", [2, 512])]
        sinks = r("sinks", [HEADS])
        amax = r("amax", [HEADS])
        asum = r("asum", [HEADS])
        asink = [r(f"asink{i}", [HEADS]) for i in range(2)]
        rows = r("rows", [P])
        r = Region(nc, uT_at, uT_at + 2 * T * 4)
        sgw = r("sgw", [GROUPS, P])
        r = Region(nc, uT_at + 2 * T * 4, uT_at + 4 * T * 4)
        part += [r("part1", [2, 512])]
        ajunk = catT[:, KT - 1, :]
        r = Region(nc, h2nat_at, ids_at)
        sgub = r("sgub", [GROUPS, P])
        sgun = r("sgun", [SGU])
        r = Region(nc, ada_at, ada_at + KT * 512 * 4)
        s_sb = [r(f"s_sb{i}", [HEADS, P]) for i in range(2)]
        pT = [r(f"pT{i}", [HEADS, P]) for i in range(2)]
        r = Region(nc, ada_at + KT * 512 * 4, ada_at + 3 * KT * 512 * 4)
        w_out_sb = r("w_out_sb", [KT, D])
        r = Region(nc, w_in_at, ada_at)
        gp1 = r("gp1", [D])
        gp2 = r("gp2", [D])
        xn2 = r("xn2", [NB, D])

        keys_at = r.at
        keys = r("keys", [2 * PH, P])
        wq = [r(f"wq{i}", [KT, P]) for i in range(2)]
        keysT = r("keysT", [2 * PH, P])
        r = Region(nc, ada_at, limit)
        wqhi = [r(f"wqhi{i}", [KT, P], F32R) for i in range(2)]
        wqlo = [r(f"wqlo{i}", [KT, P], F32R) for i in range(2)]
        assert r.at <= ada_at + KT * 512 * 4
        htmp = [r(f"htmp{i}", [T]) for i in range(2)]
        pqT = [r(f"pqT{i}", [T]) for i in range(2)]
        score = [r(f"score{i}", [NB, KEYS]) for i in range(2)]
        hit = [r(f"hit{i}", [NB, TOPK, TOPK]) for i in range(2)]
        r = Region(nc, w_in_at, keys_at)
        cand = r("cand", [NB, SUMS])
        top = r("top", [2, NB, TOPK])
        topi = r("topi", [2, NB, TOPK], U32)
        topf = r("topf", [2, NB, TOPK])
        bests = r("bests", [NB, TOPK])
        besti = r("besti", [NB, TOPK], U32)
        pair = r("pair", [2, NB, TOPK], U32)
        pairf = r("pairf", [2, NB, TOPK])
        place = r("place", [NB, TOPK])
        start = r("start", [NB, TOPK])
        best = r("best", [NB, PH, TOPK])
        bsum = r("bsum", [NB, PH])
        pick = r("pick", [3, NB, PH, TOPK])
        r = Region(nc, rest_at, w_in_at)
        pickT = r("pickT", [3, TD])
        onehot2 = [r(f"onehot2_{i}", [TB, KEYS]) for i in range(2)]
        gated1 = [r(f"gated1_{i}", [TB, KEYS]) for i in range(2)]
        r = Region(nc, r.at, limit)
        stage = [r(f"stage{i}", [KEYS, P]) for i in range(2)]
        stage_1_at = r.at - KEYS * P * 4
        r = Region(nc, rest_at, limit)
        y = r("y", [NB, D])
        gate = [r(f"gate{i}", [TD]) for i in range(2)]
        gel = [r(f"gel{i}", [TD]) for i in range(2)]
        acts = [r(f"acts{i}", [TD]) for i in range(2)]
        ahi = [[r(f"ahi{g}{i}", [TD], F32R) for i in range(GROUP)] for g in range(2)]
        alo = [[r(f"alo{g}{i}", [TD], F32R) for i in range(GROUP)] for g in range(2)]
        junk = r("junk", [D])
        rows_d = [r(f"rows_d{i}", [D]) for i in range(4)]
        rows_u = [r(f"rows_u{i}", [D]) for i in range(4)]
        idx_d = [r(f"idx_d{i}", [1], U32) for i in range(4)]
        idx_u = [r(f"idx_u{i}", [1], U32) for i in range(4)]
        dots = r("dots", [4])
        gel3 = r("gel3", [4])
        coef = r("coef", [4])
        assert r.at <= stage_1_at
        r = Region(nc, stage_1_at, limit)
        down = [r(f"down{i}", [D]) for i in range(2)]
        up = [r(f"up{i}", [D]) for i in range(2)]
        dhi = [r(f"dhi{i}", [KT, P], F32R) for i in range(2)]
        dlo = [r(f"dlo{i}", [KT, P], F32R) for i in range(2)]
        uhi = [[r(f"uhi{g}{i}", [D], F32R) for i in range(GROUP)] for g in range(2)]
        ulo = [[r(f"ulo{g}{i}", [D], F32R) for i in range(GROUP)] for g in range(2)]

        bank = [ctx.enter_context(nc.psum_tensor(f"bank{i}", [P, 512], F32)) for i in range(8)]
        gates_dram = nc.dram_tensor("gates_dram", [TILES, KEYS, TD], F32).ap()

        x_v = x[0].rearrange("(b p) d -> b p d", p=P)
        out_v = out[0].rearrange("(b p) d -> b p d", p=P)
        ada_v = w_ada[0].rearrange("(k p) n -> p k n", p=P)
        w_in_v = w_in[0].rearrange("(k p) n -> p k n", p=P)
        w_out_v = w_out[0].rearrange("(k p) n -> p k n", p=P)
        wq_v = peer_query[0].rearrange("(k p) n -> p k n", p=P)
        keys_v = peer_keys[0].rearrange("h s n d -> n (h s) d")
        down_v = peer_down[0].rearrange("(n p) d -> n p d", p=P)
        up_v = peer_up[0].rearrange("(n p) d -> n p d", p=P)

        def row(ap):
            return ap.broadcast_to([P] + list(ap.shape[1:]))

        def one(view, n):
            return view[bass.ds(n, 1)].rearrange("o p m -> (o p) m")

        rows_in, misc_in, w_out_in = sem("rows_in"), sem("misc_in"), sem("w_out_in")
        w_qkv_in, w_sv_in, w_u_in = sem("w_qkv_in"), sem("w_sv_in"), sem("w_u_in")
        x_in = [sem(f"x_in{i}") for i in range(NB)]
        ada_in = [sem(f"ada_in{i}") for i in range(ADA_SLOTS)]
        gp_in, keys_in = sem("gp_in"), sem("keys_in")
        wq_in = [sem(f"wq_in{i}") for i in range(2)]
        stored = [sem(f"stored{i}") for i in range(2)]
        down_in = [sem(f"down_in{i}") for i in range(2)]
        up_in = [sem(f"up_in{i}") for i in range(2)]
        gate_in = [sem(f"gate_in{i}") for i in range(2)]
        rows_d_in = [sem(f"rows_d_in{i}") for i in range(4)]
        rows_u_in = [sem(f"rows_u_in{i}") for i in range(4)]
        stored_part = [sem(f"stored_part{i}") for i in range(4)]
        out_done = sem("out_done")
        ident_ok, zeros_ok = sem("ident_ok"), sem("zeros_ok")
        pe_rows, pe_wT, pe_ada, pe_h1, pe_z = (sem(n) for n in ("pe_rows", "pe_wT", "pe_ada", "pe_h1", "pe_z"))
        pe_s, pe_pt, pe_o, pe_sgu, pe_mix = (sem(n) for n in ("pe_s", "pe_pt", "pe_o", "pe_sgu", "pe_mix"))
        pe_keys, pe_h2, pe_q, pe_sc, pe_pick = (sem(n) for n in ("pe_keys", "pe_h2", "pe_q", "pe_sc", "pe_pick"))
        pe_g, pe_t, pe_d, pe_u, pe_hn = (sem(n) for n in ("pe_g", "pe_t", "pe_d", "pe_u", "pe_hn"))
        act_silu, act_ss, act_root, act_h1, act_z, act_sv = (
            sem(n) for n in ("act_silu", "act_ss", "act_root", "act_h1", "act_z", "act_sv"))
        act_s, act_exp, act_pt, act_o = (sem(n) for n in ("act_s", "act_exp", "act_pt", "act_o"))
        act_keys, act_h2, act_wq, act_q, act_sc, act_gexp, act_pick, act_g = (
            sem(n) for n in ("act_keys", "act_h2", "act_wq", "act_q", "act_sc", "act_gexp", "act_pick", "act_g"))
        act_dhi, act_uhi, act_gelu, act_ahi, act_hn, act_g3 = (
            sem(n) for n in ("act_dhi", "act_uhi", "act_gelu", "act_ahi", "act_hn", "act_g3"))
        dve = sem("dve")
        dve_ada = sem("dve_ada")
        dve_ms, dve_xn1, dve_mod, dve_h1, dve_wT = (
            sem(n) for n in ("dve_ms", "dve_xn1", "dve_mod", "dve_h1", "dve_wT"))
        dve_center, dve_vn, dve_sgu, dve_sub, dve_p, dve_gg = (
            sem(n) for n in ("dve_center", "dve_vn", "dve_sgu", "dve_sub", "dve_p", "dve_gg"))
        dve_mix, dve_x1, dve_xn2, dve_htmp, dve_h2 = (
            sem(n) for n in ("dve_mix", "dve_x1", "dve_xn2", "dve_htmp", "dve_h2"))
        dve_top, dve_pair, dve_sel, dve_bsub, dve_pick, dve_hot = (
            sem(n) for n in ("dve_top", "dve_pair", "dve_sel", "dve_bsub", "dve_pick", "dve_hot"))
        dve_dlo, dve_act, dve_alo, dve_y = (sem(n) for n in ("dve_dlo", "dve_act", "dve_alo", "dve_y"))
        dve_ids, dve_dot, dve_coef, dve_add = (sem(n) for n in ("dve_ids", "dve_dot", "dve_coef", "dve_add"))
        pool_wq, pool_hit, pool_ulo, pool_idx, pool = (
            sem(n) for n in ("pool_wq", "pool_hit", "pool_ulo", "pool_idx", "pool"))

        block = ctx.enter_context(nc.Block())

        @block.sync
        def _(sp):
            sp.dma_start(rows[ROW_C:ROW_C + KT, :], c.rearrange("o (k p) -> (o k) p", p=P)).then_inc(rows_in, 16)
            sp.dma_start(rows[ROW_B:ROW_B + 48, :], b_ada.rearrange("o (k p) -> (o k) p", p=P)).then_inc(rows_in, 16)
            sp.dma_start(rows[ROW_G1:ROW_G1 + KT, :], g_pre_mix.rearrange("o (k p) -> (o k) p", p=P)).then_inc(rows_in, 16)
            sp.dma_start(rows[ROW_G2:ROW_G2 + KT, :], g_pre_ffn.rearrange("o (k p) -> (o k) p", p=P)).then_inc(rows_in, 16)

            def load_ada(n):
                q = ADA_ORDER[n]
                if n >= ADA_SLOTS:
                    sp.wait_ge(dve_ada, 2 * (n - ADA_SLOTS + 1))
                sp.dma_start(ada[n % ADA_SLOTS][:], ada_v[:, :, q * 512:q * 512 + 512]).then_inc(ada_in[n % ADA_SLOTS], 16)

            for b in range(NB):
                sp.dma_start(x1[:, b, :], x_v[b]).then_inc(x_in[b], 16)
            for n in range(4):
                load_ada(n)
            sp.dma_start(w_in_sb[:, :, ATT:U_AT], w_in_v[:, :, ATT:U_AT]).then_inc(w_qkv_in, 16)
            for k in range(KT):
                for s in range(2):
                    sp.dma_start(w_in_sb[:, k, 0:ATT].rearrange("p (j s n) -> p j s n", j=4, s=2)[:, :, s, :],
                                 w_in_v[:, k, s * 256:s * 256 + 256].rearrange("p (j n) -> p j n", j=4)
                                 ).then_inc(w_qkv_in, 16)
            load_ada(4)
            load_ada(5)
            sp.dma_start(w_in_sb[:, :, SV_AT:], w_in_v[:, :, SV_AT:]).then_inc(w_sv_in, 16)
            load_ada(6)
            load_ada(7)
            sp.dma_start(w_in_sb[:, :, U_AT:SV_AT], w_in_v[:, :, U_AT:SV_AT]).then_inc(w_u_in, 16)
            for n in range(8, len(ADA_ORDER)):
                load_ada(n)
            sp.wait_ge(dve_ada, 2 * len(ADA_ORDER))
            for q in range(2):
                sp.dma_start(w_out_sb[:, 4 * q:4 * q + 4, :], w_out_v[:, 4 * q:4 * q + 4, :]).then_inc(w_out_in, 16)
            sp.wait_ge(pe_z, Z_JOBS)
            sp.dma_start(gp1[:], row(g_post_mix)).then_inc(gp_in, 16)
            sp.dma_start(gp2[:], row(g_post_ffn)).then_inc(gp_in, 16)

            sp.dma_start(keys[:], keys_v).then_inc(keys_in, 16)

            def load_wq(h, s):
                sp.dma_start(wq[s][:], wq_v[:, :, bass.ds(h * 256 + s * P, P)]).then_inc(wq_in[s], 16)

            for s in range(2):
                load_wq(0, s)
            with sp.Fori(1, PH) as h:
                for s in range(2):
                    sp.wait_ge(act_wq, 2 * h - 1 + s)
                    sp.wait_ge(pool_wq, 2 * h - 1 + s)
                    load_wq(h, s)

            def store_block(b, keys_1, signal):
                sp.dma_start(gates_dram[keys_1, :, b * P:(b + 1) * P].rearrange("i p t -> p i t"),
                             stage[b % 2][:, keys_1, :]).then_inc(signal, 16)

            def load_down(n, s):
                sp.dma_start(down[s][:], one(down_v, n)).then_inc(down_in[s], 16)

            def load_up(n, s):
                sp.dma_start(up[s][:], one(up_v, n)).then_inc(up_in[s], 16)

            def load_gate(n, s):
                sp.dma_start(gate[s][:], one(gates_dram, n)).then_inc(gate_in[s], 16)

            for b in range(GB - 1):
                sp.wait_ge(act_g, (b + 1) * (P // 4))
                store_block(b, slice(0, KEYS), stored[b % 2])
            sp.wait_ge(stored[1], 16)
            for s in range(2):
                load_down(s, s)
                load_up(s, s)
            sp.wait_ge(act_g, GB * (P // 4))
            for q in range(4):
                store_block(GB - 1, slice(32 * q, 32 * q + 32), stored_part[q])

            def turn(i):
                for s in range(2):
                    n = 2 * i + s
                    sp.wait_ge(pe_t, 2 * n + 2)
                    load_down(n + 2, s)
                    sp.wait_ge(pool_ulo, n + 1)
                    load_up(n + 2, s)
                    sp.wait_ge(dve_act, n + 1)
                    load_gate(n + 2, s)

            sp.wait_ge(stored[0], 16)
            sp.wait_ge(stored_part[0], 16)
            for q in range(1, 4):
                sp.wait_ge(stored_part[q], 16)
            for s in range(2):
                load_gate(s, s)
            turn(0)
            with sp.Fori(1, TILES // 2 - 1) as i:
                turn(i)

            for b in range(NB):
                sp.wait_ge(dve_x1, NB + b + 1)
                sp.dma_start(out_v[b], x1[:, b, :]).then_inc(out_done, 16)
            sp.wait_ge(out_done, 16 * NB)

        @block.gpsimd
        def _(gp):
            gp.memset(ident[:], 0.0).then_inc(pool, 1)
            gp.memset(ones[:], 1.0).then_inc(ident_ok, 1)
            gp.iota(iota[:], pattern=[[1, P]], base=0, channel_multiplier=0,
                    allow_small_or_imprecise_dtypes=True).then_inc(ident_ok, 1)
            gp.wait_ge(pool, 1)
            gp.affine_select(out=ident[:], in_=ident[:], compare_op=ALU.not_equal, fill=1.0, base=0,
                             pattern=[[-1, P]], channel_multiplier=1).then_inc(ident_ok, 1)
            gp.wait_ge(ident_ok, 3)
            gp.memset(hT[:, :, 0:CHUNK], 0.0).then_inc(zeros_ok, 1)
            gp.wait_ge(zeros_ok, 1)
            gp.memset(kT[:, 0:CHUNK], 0.0).then_inc(zeros_ok, 1)
            gp.wait_ge(zeros_ok, 2)
            gp.memset(wT[CHUNK:P, :, 0:CHUNK], 0.0).then_inc(zeros_ok, 1)

            def split_wq(h):
                for s in range(2):
                    gp.wait_ge(act_wq, 2 * h + s + 1)
                    gp.tensor_tensor(wqlo[s][:], wq[s][:], wqhi[s][:].bitcast(F32), ALU.subtract).then_inc(pool_wq, 1)

            def weigh_hits(h):
                gp.wait_ge(dve_pair, 2 * h + 2)
                for s in range(2):
                    gp.tensor_tensor(hit[s][:], hit[s][:],
                                     topf[:, s].unsqueeze(2).broadcast_to([P, NB, TOPK, TOPK]),
                                     ALU.mult).then_inc(pool_hit, 1)

            split_wq(0)
            with gp.Fori(1, PH) as h:
                split_wq(h)
                weigh_hits(h - 1)
            weigh_hits(PH - 1)

            for q in range(4):
                gp.wait_ge(stored_part[q], 16)
            gp.wait_ge(dve_ids, 1)

            ch = Chain(gp, pool_idx)

            def gather(rows_, table, idx, n, k):
                ch.link(gp.tensor_copy(idx[k][:], ids[:, bass.ds(n, 1)]))
                gp.nop(nofuse=True)
                return gp.indirect_dma_start(rows_[k][:], None, table[0], bass.IndirectOffsetOnAxis(ap=idx[k][:, 0:1], axis=0))

            def gather_up(n, k, first=False):
                if not first:
                    gp.wait_ge(dve_add, n - 3)
                gather(rows_u, peer_up, idx_u, n, k).then_inc(rows_u_in[k], 16)

            def turn(i, first=False, second=False):
                for k in range(4):
                    n = 4 * i + k
                    if not first:
                        gather_up(n - 4, k, first=second)
                        gp.wait_ge(dve_dot, n - 3)
                    gather(rows_d, peer_down, idx_d, n, k).then_inc(rows_d_in[k], 16)
                    gp.wait_ge(act_uhi, n + 1)
                    g, s = k // 2, k % 2
                    gp.tensor_tensor(ulo[g][s][:], up[s][:], uhi[g][s][:].bitcast(F32), ALU.subtract).then_inc(pool_ulo, 1)

            turn(0, first=True)
            turn(1, second=True)
            with gp.Fori(2, PICKS // 4) as i:
                ch.enter(i - 2, 8)
                turn(i)
                ch.leave(PICKS // 4 - 2)
            for k in range(4):
                gather_up(PICKS - 4 + k, k)

        @block.scalar
        def _(act):
            act.dma_start(sgw[:], sgu_w[0].rearrange("g i j -> i g j")).then_inc(misc_in, 16)
            act.dma_start(gg1[:], row(b_ada[:, 2 * D:3 * D])).then_inc(misc_in, 16)
            act.dma_start(gg2[:], row(b_ada[:, 5 * D:6 * D])).then_inc(misc_in, 16)
            act.dma_start(sgub[:].rearrange("p g i -> p (g i)"), row(sgu_b.rearrange("o g i -> o (g i)"))).then_inc(misc_in, 16)
            act.dma_start(sgun[:], row(sgu_norm)).then_inc(misc_in, 16)
            act.dma_start(sinks[:], row(attn_sinks)).then_inc(misc_in, 16)
            act.wait_ge(rows_in, 64)
            act.activation(rows[0:KT, :], rows[0:KT, :], ACT.Silu).then_inc(act_silu, 1)
            for b in range(NB):
                act.wait_ge(x_in[b], 16)
                act.activation(xn1[:, b, :], x1[:, b, :], ACT.Square, accum_out=ssq[:, b:b + 1]).then_inc(act_ss, 1)
            act.wait_ge(dve_ms, 1)
            act.activation(root[:, 0:NB], ssq[:, 0:NB], ACT.Sqrt).then_inc(act_root, 1)
            act.wait_ge(dve_mod, 1)
            act.wait_ge(zeros_ok, 3)
            for j in range(1, KT, 2):
                act.wait_ge(pe_h1, j + 1)
                act.activation(hT[:, j, CHUNK:], bank[1 + j % 4][:], ACT.Identity,
                               bias=modc[:, SH1 + j:SH1 + j + 1], scale=scale1[:, j:j + 1]).then_inc(act_h1, 1)

            def scores_out(b):
                if b >= 2:
                    act.wait_ge(pe_pt, 2 * b - 2)
                for s in range(2):
                    act.wait_ge(pe_s, 2 * b + s + 1)
                    act.activation(s_sb[b % 2][:, 4 * s:4 * s + 4, :].rearrange("p h k -> p (h k)"),
                                   bank[1 + s][:], ACT.Copy).then_inc(act_s, 1)

            def exps(b):
                act.wait_ge(dve_sub, 2 * b + 2)
                flat = s_sb[b % 2][:].rearrange("p h k -> p (h k)")
                act.activation(flat, flat, ACT.Exp).then_inc(act_exp, 1)
                act.activation(asink[b % 2][:], asink[b % 2][:], ACT.Exp).then_inc(act_exp, 1)

            def transposed_out(b):
                if b >= 2:
                    act.wait_ge(pe_o, b - 1)
                for s in range(2):
                    act.wait_ge(pe_pt, 2 * b + s + 1)
                    act.activation(pT[b % 2][:, 4 * s:4 * s + 4, :].rearrange("p h k -> p (h k)"),
                                   bank[3 + s][:], ACT.Copy).then_inc(act_pt, 1)

            def attended_out(b):
                act.wait_ge(pe_o, b + 1)
                act.activation(catT[:, 0:4, b * P:(b + 1) * P],
                               bank[3][:].rearrange("p (h q) -> p h q", h=4), ACT.Copy).then_inc(act_o, 1)

            for m in range(Z_JOBS):
                act.wait_ge(pe_z, m + 1)
                got = bank[Z_BANKS[m]]
                if m == Z_K:
                    act.activation(kT[:, CHUNK:], got[:], ACT.Copy).then_inc(act_z, 1)
                elif m < Z_V:
                    act.activation(qT[:, m - Z_Q, :], got[:], ACT.Copy, scale=HD ** -0.5).then_inc(act_z, 1)
                elif m < Z_SV:
                    dst = v if m == Z_V else vs
                    act.activation(dst[:].rearrange("p b n -> p (b n)"), got[:], ACT.Copy).then_inc(act_z, 1)
                elif m < Z_U:
                    act.activation(sv[:, m - Z_SV, :], got[:], ACT.Gelu, accum_out=svsum[:, m - Z_SV:m - Z_SV + 1]).then_inc(act_z, 1)
                else:
                    act.activation(uT[:, m - Z_U, :], got[:], ACT.Gelu).then_inc(act_z, 1)
                if m == Z_SV:
                    act.wait_ge(dve_ada, 2 * 10)
                    scores_out(0)
                elif m == Z_SV + 1:
                    exps(0)
                    scores_out(1)
                elif m == Z_SV + 2:
                    transposed_out(0)
                    exps(1)
                elif m == Z_SV + 3:
                    attended_out(0)
                    scores_out(2)
                elif m == Z_U:
                    transposed_out(1)
                    exps(2)
                elif m == Z_U + 1:
                    attended_out(1)
                    scores_out(3)
                    for b in range(NB):
                        act.wait_ge(dve_center, b + 1)
                        if b:
                            act.wait_ge(act_sv, b)
                        act.activation(ajunk, sv[:, b, :], ACT.Square,
                                       accum_out=ssq[:, 4 + b:5 + b]).then_inc(act_sv, 1)
                elif m == Z_U + 2:
                    transposed_out(2)
                    exps(3)
                elif m == Z_U + 3:
                    attended_out(2)
            act.wait_ge(dve_ms, 2)
            act.activation(root[:, 4:8], ssq[:, 4:8], ACT.Sqrt).then_inc(act_root, 1)
            transposed_out(3)
            attended_out(3)
            for b in range(NB):
                for s in range(2):
                    act.wait_ge(pe_mix, 2 * b + s + 1)
                    act.activation(xn2[:, b, s * 512:s * 512 + 512], bank[1 + 2 * (b % 2) + s][:], ACT.Square,
                                   accum_out=ssq[:, 8 + 2 * b + s:9 + 2 * b + s]).then_inc(act_ss, 1)
                act.wait_ge(dve_ms, 3 + 2 * b)
                act.activation(root[:, 8 + b:9 + b], ssq[:, 16 + b:17 + b], ACT.Sqrt).then_inc(act_root, 1)
                act.wait_ge(dve_x1, b + 1)
                act.activation(xn2[:, b, :], x1[:, b, :], ACT.Square, accum_out=ssq[:, 20 + b:21 + b]).then_inc(act_ss, 1)
                act.wait_ge(dve_ms, 4 + 2 * b)
                act.activation(root[:, 12 + b:13 + b], ssq[:, 20 + b:21 + b], ACT.Sqrt).then_inc(act_root, 1)

            def weights_hi(h, first=False):
                for s in range(2):
                    act.wait_ge(wq_in[s], 16 * h + 16)
                    if not first:
                        act.wait_ge(pe_q, 2 * h)
                    act.activation(wqhi[s][:], wq[s][:], ACT.Copy).then_inc(act_wq, 1)

            weights_hi(0, first=True)
            for m in range(4):
                act.wait_ge(pe_keys, m + 1)
                act.activation(keysT[:, 4 * m:4 * m + 4, :].rearrange("p n k -> p (n k)"), bank[5 + m % 2][:],
                               ACT.Copy).then_inc(act_keys, 1)
            for j in range(KT):
                act.wait_ge(dve_htmp, j + 1)
                act.activation(h2hi[:, j, :], htmp[j % 2][:], ACT.Copy).then_inc(act_h2, 1)
            for s in range(2):
                act.wait_ge(pe_hn, 4 * s + 4)
                act.activation(h2nat[:, s * 512:s * 512 + 512], bank[7 * s][:], ACT.Copy).then_inc(act_hn, 1)

            def head(h, first=False):
                if not first:
                    weights_hi(h)
                for s in range(2):
                    act.wait_ge(pe_q, 2 * h + s + 1)
                    if not first:
                        act.wait_ge(pe_sc, 2 * h)
                    act.activation(pqT[s][:], bank[1 + s][:], ACT.Copy).then_inc(act_q, 1)
                for s in range(2):
                    act.wait_ge(pe_sc, 2 * h + s + 1)
                    if not first:
                        act.wait_ge(dve_top, h)
                    act.activation(score[s][:].rearrange("p b k -> p (b k)"), bank[3 + s][:],
                                   ACT.Copy).then_inc(act_sc, 1)

            head(0, first=True)
            with act.Fori(1, PH) as h:
                head(h)
            act.wait_ge(dve_bsub, 1)
            act.activation(best[:].rearrange("p b h k -> p (b h k)"),
                           pick[:, 2].rearrange("p b h k -> p (b h k)"), ACT.Exp).then_inc(act_gexp, 1)
            for k in range(3):
                act.wait_ge(pe_pick, k + 1)
                act.activation(pickT[:, k, :], bank[5 + k][:, 0:TD], ACT.Copy).then_inc(act_pick, 1)

            for b in range(GB):
                if b >= 2:
                    act.wait_ge(stored[b % 2], 16)
                with act.Fori(0, P // (2 * TB)) as i:
                    for u in range(2):
                        for s in range(2):
                            act.wait_ge(pe_g, b * 32 + 4 * i + 2 * u + s + 1)
                            act.activation(
                                stage[b % 2][:, :, bass.ds(i * (2 * TB) + u * TB + 4 * s, 4)].rearrange("p i t -> p t i"),
                                bank[1 + 2 * u + s][:].rearrange("p (t i) -> p t i", t=4),
                                ACT.Copy).then_inc(act_g, 1)

            def down_hi(n, s):
                for k in range(2):
                    act.wait_ge(pe_t, 2 * n + k + 1)
                    act.activation(dhi[s][:, 4 * k:4 * k + 4, :].rearrange("p k e -> p (k e)"), bank[k][:],
                                   ACT.Copy).then_inc(act_dhi, 1)

            def tile(i, g, s, first=False, second=False, last=False):
                n = 2 * i + s
                if not last:
                    down_hi(n + 1, 1 - s)
                if not first and not second:
                    act.wait_ge(pe_u, OUTS * (i - 1))
                act.wait_ge(up_in[s], 16 * i + 16)
                act.activation(uhi[g][s][:], up[s][:], ACT.Copy).then_inc(act_uhi, 1)
                act.wait_ge(pe_d, n + 1)
                if first and s == 0:
                    for q in range(4):
                        act.wait_ge(stored_part[q], 16)
                if not first:
                    act.wait_ge(dve_act, n - 1)
                act.activation(gel[s][:], bank[2 + s][:, 0:TD], ACT.Gelu).then_inc(act_gelu, 1)
                act.wait_ge(dve_act, n + 1)
                act.activation(ahi[g][s][:], acts[s][:], ACT.Copy).then_inc(act_ahi, 1)

            def gelu_dots(i):
                act.wait_ge(dve_dot, 4 * i)
                act.activation(gel3[:], dots[:], ACT.Gelu).then_inc(act_g3, 1)

            down_hi(0, 0)
            for g in range(2):
                for s in range(2):
                    tile(g, g, s, first=g == 0, second=g == 1)
            with act.Fori(1, TILES // 4 - 1) as i:
                for g in range(2):
                    for s in range(2):
                        tile(2 * i + g, g, s)
                        if g == 0 and s == 0:
                            gelu_dots(i)
            for g in range(2):
                for s in range(2):
                    tile(TILES // 2 - 2 + g, g, s, last=g == 1 and s == 1)
                    if g == 0 and s == 0:
                        gelu_dots(TILES // 4 - 1)
            gelu_dots(TILES // 4)
            for b in range(NB):
                act.wait_ge(dve_y, OUTS * (TILES // 2)) if b < GB else act.wait_ge(dve_add, PICKS)
                act.activation(junk[:], y[:, b, :], ACT.Square, accum_out=ssq[:, 24 + b:25 + b]).then_inc(act_ss, 1)
                act.wait_ge(act_ss, NB + 3 * NB + b + 1)
            act.wait_ge(dve_ms, 3 + 2 * NB)
            act.activation(root[:, 16:20], ssq[:, 24:28], ACT.Sqrt).then_inc(act_root, 1)

        @block.vector
        def _(ve):
            ch = Chain(ve, dve)

            def mean_square(dst, src, width):
                return ve.tensor_scalar(dst, src, 1.0 / width, EPS, ALU.mult, ALU.add)

            ve.wait_ge(pe_rows, 1)
            ch.link(ve.tensor_copy(columns[:], bank[7][:, 0:ROWS]))
            ch.link(ve.tensor_copy(c_col[:], columns[:, 0:KT]))

            def multiply_ada(n):
                ve.wait_ge(ada_in[n % ADA_SLOTS], 16 * (n // ADA_SLOTS + 1))
                if n >= 2:
                    ve.wait_ge(pe_ada, n - 1)
                a, dst = ada[n % ADA_SLOTS], part[n % 2]
                for k in range(2):
                    ch.mark(ve.tensor_scalar(dst[:, k, :], a[:, k, :], c_col[:, k:k + 1], None, ALU.mult))
                for k in range(2, KT):
                    if k % 2 == 0:
                        ch.wait()
                    last = ve.scalar_tensor_tensor(out=dst[:, k % 2, :], in0=a[:, k, :], scalar=c_col[:, k:k + 1],
                                                   in1=dst[:, k % 2, :], op0=ALU.mult, op1=ALU.add)
                    if k < KT - 2:
                        ch.mark(last)
                    else:
                        last.then_inc(dve_ada, 1)

            ve.wait_ge(zeros_ok, 3)
            ve.wait_ge(pe_wT, 1)
            got = bank[6][:].rearrange("p (g i) -> p g i", g=GROUPS)
            ch.link(ve.tensor_copy(wT[0:CHUNK, :, :], got[0:CHUNK]))
            ve.tensor_copy(wT[CHUNK:P, :, CHUNK:P], got[CHUNK:P, :, CHUNK:P]).then_inc(dve_wT, 1)
            ve.wait_ge(act_ss, NB)
            mean_square(ssq[:, 0:NB], ssq[:, 0:NB], D).then_inc(dve_ms, 1)
            ve.wait_ge(act_root, 1)
            ch.link(ve.reciprocal(root[:, 0:NB], root[:, 0:NB]))
            for b in range(NB):
                ve.tensor_scalar(xn1[:, b, :], x1[:, b, :], root[:, b:b + 1], None, ALU.mult).then_inc(dve_xn1, 1)

            def add_bias(first):
                ch.mark(ve.tensor_tensor(modc[:, first:first + KT], bank[0][:, first:first + KT],
                                         columns[:, ROW_B + first:ROW_B + first + KT], ALU.add))

            def make_scale(dst, first, row_g):
                return ve.scalar_tensor_tensor(out=dst[:], in0=modc[:, first:first + KT], scalar=1.0,
                                               in1=columns[:, row_g:row_g + KT], op0=ALU.add, op1=ALU.mult)

            for n in range(4):
                multiply_ada(n)
            ve.wait_ge(pe_ada, 4)
            add_bias(SC1)
            add_bias(SH1)
            ch.wait()
            make_scale(scale1, SC1, ROW_G1).then_inc(dve_mod, 1)
            ve.wait_ge(dve_mod, 1)
            for j in range(0, KT, 2):
                ve.wait_ge(pe_h1, j + 1)
                ve.tensor_scalar(hT[:, j, CHUNK:], bank[1 + j % 4][:], scale1[:, j:j + 1],
                                 modc[:, SH1 + j:SH1 + j + 1], ALU.mult, ALU.add).then_inc(dve_h1, 1)
            def gate_half(n, gg, s):
                ve.wait_ge(pe_ada, n + 1)
                half = gg[:, s * 512:s * 512 + 512]
                ve.tensor_tensor(half, bank[7][:], half, ALU.add).then_inc(dve_gg, 1)


            def softmax_front(b):
                s = s_sb[b % 2]
                sink = asink[b % 2]
                ve.wait_ge(act_s, 2 * b + 2)
                if b == 0:
                    ch.link(ve.memset(s[0:CHUNK, :, 0:CHUNK], LOWEST))
                ch.link(ve.tensor_reduce(out=amax[:], in_=s[:], axis=AXX, op=ALU.max))
                ch.link(ve.tensor_tensor(amax[:], amax[:], sinks[:], ALU.max))
                ve.tensor_tensor(sink[:], sinks[:], amax[:], ALU.subtract).then_inc(dve_sub, 1)
                ve.tensor_tensor(s[:], s[:], amax[:].unsqueeze(2).broadcast_to([P, HEADS, P]),
                                 ALU.subtract).then_inc(dve_sub, 1)

            def softmax_back(b):
                s = s_sb[b % 2]
                ve.wait_ge(act_exp, 2 * b + 2)
                ch.link(ve.tensor_reduce(out=asum[:], in_=s[:], axis=AXX, op=ALU.add))
                ch.link(ve.tensor_tensor(asum[:], asum[:], asink[b % 2][:], ALU.add))
                ch.link(ve.reciprocal(asum[:], asum[:]))
                ve.tensor_tensor(s[:], s[:], asum[:].unsqueeze(2).broadcast_to([P, HEADS, P]), ALU.mult).then_inc(dve_p, 1)

            def spatial(g):
                ve.wait_ge(pe_sgu, g + 1)
                dst = catT[:, 4 + g, :]
                ch.link(ve.tensor_tensor(dst.rearrange("p (b i) -> p b i", b=NB),
                                         bank[5 + g % 2][:].rearrange("p (b i) -> p b i", b=NB),
                                         sgub[:, g].unsqueeze(1).broadcast_to([P, NB, P]), ALU.add))
                ve.tensor_tensor(dst, dst, uT[:, g, :], ALU.mult).then_inc(dve_sgu, 1)

            ve.wait_ge(misc_in, 16 * 6)
            multiply_ada(4)
            multiply_ada(5)
            gate_half(4, gg1, 0)
            multiply_ada(6)
            gate_half(5, gg1, 1)
            for n in range(7, 10):
                multiply_ada(n)
            softmax_front(0)
            multiply_ada(10)
            softmax_back(0)
            softmax_front(1)
            gate_half(10, gg2, 0)
            multiply_ada(11)
            softmax_back(1)
            gate_half(11, gg2, 1)
            ve.wait_ge(act_z, Z_U)
            ch.link(ve.tensor_scalar(svsum[:], svsum[:], -1.0 / SGU, None, ALU.mult))
            for b in range(NB):
                ve.tensor_scalar(sv[:, b, :], sv[:, b, :], svsum[:, b:b + 1], None, ALU.add).then_inc(dve_center, 1)
            softmax_front(2)
            softmax_back(2)
            softmax_front(3)
            ve.wait_ge(act_sv, NB)
            mean_square(ssq[:, 4:8], ssq[:, 4:8], SGU).then_inc(dve_ms, 1)
            softmax_back(3)
            ve.wait_ge(act_root, 2)
            ch.link(ve.reciprocal(root[:, 4:8], root[:, 4:8]))
            for b in range(NB):
                ve.scalar_tensor_tensor(out=sv[:, b, :], in0=sv[:, b, :], scalar=root[:, 4 + b:5 + b], in1=sgun[:],
                                        op0=ALU.mult, op1=ALU.mult).then_inc(dve_vn, 1)
            for g in range(GROUPS):
                spatial(g)
            ve.wait_ge(gp_in, 32)
            ve.wait_ge(dve_gg, 4)
            for gg, gp in ((gg1, gp1), (gg2, gp2)):
                ch.mark(ve.tensor_tensor(gg[:], gg[:], gp[:], ALU.mult))
            for b in range(NB):
                ve.wait_ge(act_ss, NB + 3 * b + 2)
                ch.link(ve.tensor_tensor(ssq[:, 16 + b:17 + b], ssq[:, 8 + 2 * b:9 + 2 * b], ssq[:, 9 + 2 * b:10 + 2 * b], ALU.add))
                mean_square(ssq[:, 16 + b:17 + b], ssq[:, 16 + b:17 + b], D).then_inc(dve_ms, 1)
                ve.wait_ge(act_root, 3 + 2 * b)
                ch.link(ve.reciprocal(root[:, 8 + b:9 + b], root[:, 8 + b:9 + b]))
                for s in range(2):
                    half = slice(s * 512, s * 512 + 512)
                    ve.scalar_tensor_tensor(out=xn2[:, b, half], in0=bank[1 + 2 * (b % 2) + s][:],
                                            scalar=root[:, 8 + b:9 + b], in1=gg1[:, half],
                                            op0=ALU.mult, op1=ALU.mult).then_inc(dve_mix, 1)
                ve.wait_ge(dve_mix, 2 * b + 2)
                ve.tensor_tensor(x1[:, b, :], x1[:, b, :], xn2[:, b, :], ALU.add).then_inc(dve_x1, 1)
                ve.wait_ge(act_ss, NB + 3 * b + 3)
                mean_square(ssq[:, 20 + b:21 + b], ssq[:, 20 + b:21 + b], D).then_inc(dve_ms, 1)
                ve.wait_ge(act_root, 4 + 2 * b)
                ch.link(ve.reciprocal(root[:, 12 + b:13 + b], root[:, 12 + b:13 + b]))
                ve.tensor_scalar(xn2[:, b, :], x1[:, b, :], root[:, 12 + b:13 + b], None, ALU.mult).then_inc(dve_xn2, 1)
            add_bias(SC2)
            add_bias(SH2)
            ch.wait()
            ch.link(make_scale(scale2, SC2, ROW_G2))
            for j in range(KT + 1):
                if j < KT:
                    ve.wait_ge(pe_h2, j + 1)
                    if j >= 2:
                        ve.wait_ge(dve_h2, j - 1)
                        ve.wait_ge(pe_hn, j - 1)
                    ve.tensor_scalar(htmp[j % 2][:], bank[1 + j % 4][:], scale2[:, j:j + 1],
                                     modc[:, SH2 + j:SH2 + j + 1], ALU.mult, ALU.add).then_inc(dve_htmp, 1)
                if j >= 1:
                    ve.wait_ge(act_h2, j)
                    ve.tensor_tensor(h2lo[:, j - 1, :], htmp[(j - 1) % 2][:], h2hi[:, j - 1, :].bitcast(F32),
                                     ALU.subtract).then_inc(dve_h2, 1)

            def stand_alone():
                ve.nop(nofuse=True)

            def top16(values, found, places):
                for half in range(2):
                    k = slice(8 * half, 8 * half + 8)
                    stand_alone()
                    for b in range(NB):
                        ch.mark(ve.max(found(b)[:, k], values(b)))
                    ch.wait()
                    stand_alone()
                    for b in range(NB):
                        ch.mark(ve.max_index(places(b)[:, k], found(b)[:, k], values(b)))
                    if half == 0:
                        ch.wait()
                        stand_alone()
                        for b in range(NB):
                            ch.mark(ve.match_replace(out=values(b), in_to_replace=found(b)[:, k], in_values=values(b),
                                                     imm_value=LOWEST))
                        ch.wait()

            def halves(h, first=False):
                for s in range(2):
                    ve.wait_ge(act_sc, 2 * h + s + 1)
                    top16(lambda b: score[s][:, b, :], lambda b: top[:, s, b, :], lambda b: topi[:, s, b, :])
                ch.wait()
                if not first:
                    ve.wait_ge(pool_hit, 2 * h)
                ve.tensor_copy(topf[:], topi[:]).then_inc(dve_top, 1)

            def sums(h):
                ve.wait_ge(dve_top, h + 1)
                for at, a, a_end, wide in ((0, 0, ROWS_16, TOPK), (AT_4, ROWS_16, ROWS_4, 4), (AT_1, ROWS_4, TOPK, 1)):
                    tall = a_end - a
                    ch.mark(ve.tensor_tensor(
                        cand[:, :, at:at + tall * wide].rearrange("p b (i j) -> p b i j", i=tall),
                        top[:, 0, :, a:a_end].unsqueeze(3).broadcast_to([P, NB, tall, wide]),
                        top[:, 1, :, 0:wide].unsqueeze(2).broadcast_to([P, NB, tall, wide]), ALU.add))
                ch.wait()
                top16(lambda b: cand[:, b], lambda b: bests[:, b, :], lambda b: besti[:, b, :])
                ch.wait()
                ch.mark(ve.tensor_copy(best[:, :, bass.ds(h, 1), :].rearrange("p b o k -> p b (o k)"), bests[:]))
                ch.mark(ve.tensor_single_scalar(pair[:, 0], besti[:], 4, op=ALU.logical_shift_right))
                ch.mark(ve.tensor_single_scalar(pair[:, 1], besti[:], 2, op=ALU.logical_shift_right))
                ch.mark(ve.tensor_copy(place[:], besti[:]))
                ch.wait()
                ch.link(ve.tensor_copy(pairf[:], pair[:]))
                a, b = pairf[:, 0], pairf[:, 1]
                ch.link(ve.scalar_tensor_tensor(out=a, in0=b, scalar=float(ROWS_16 - AT_4 // 4), in1=a,
                                                op0=ALU.add, op1=ALU.max))
                ch.link(ve.scalar_tensor_tensor(out=a, in0=place[:], scalar=float(ROWS_4 - AT_1), in1=a,
                                                op0=ALU.add, op1=ALU.max))
                ch.link(ve.tensor_scalar(start[:], a, 4.0, float(AT_4 - 4 * ROWS_16), ALU.mult, ALU.add))
                ch.link(ve.scalar_tensor_tensor(out=start[:], in0=a, scalar=float(TOPK), in1=start[:],
                                                op0=ALU.mult, op1=ALU.min))
                ch.link(ve.scalar_tensor_tensor(out=start[:], in0=a, scalar=float(AT_1 - ROWS_4), in1=start[:],
                                                op0=ALU.add, op1=ALU.min))
                ch.link(ve.tensor_tensor(b, place[:], start[:], ALU.subtract))
                for s in range(2):
                    ve.tensor_tensor(hit[s][:], pairf[:, s].unsqueeze(3).broadcast_to([P, NB, TOPK, TOPK]),
                                     iota[:, 0:TOPK].unsqueeze(1).unsqueeze(1).broadcast_to([P, NB, TOPK, TOPK]),
                                     ALU.is_equal).then_inc(dve_pair, 1)

            def select(h):
                ve.wait_ge(pool_hit, 2 * h + 2)
                for s in range(2):
                    ve.tensor_reduce(out=pick[:, s, :, bass.ds(h, 1), :].rearrange("p b o k -> p b (o k)"),
                                     in_=hit[s][:], axis=AXX, op=ALU.add).then_inc(dve_sel, 1)

            halves(0, first=True)
            sums(0)
            with ve.Fori(1, PH) as h:
                ch.enter(h - 1, HEAD_STEPS)
                halves(h)
                select(h - 1)
                sums(h)
                ch.leave(PH - 1)
            select(PH - 1)
            first = best[:, :, :, 0:1].broadcast_to([P, NB, PH, TOPK])
            ve.tensor_tensor(pick[:, 2], best[:], first, ALU.subtract).then_inc(dve_bsub, 1)
            ve.wait_ge(act_gexp, 1)
            ch.link(ve.tensor_reduce(out=bsum[:], in_=best[:], axis=AXX, op=ALU.add))
            ch.link(ve.reciprocal(bsum[:], bsum[:]))
            ve.tensor_tensor(pick[:, 2], best[:], bsum[:].unsqueeze(3).broadcast_to([P, NB, PH, TOPK]),
                             ALU.mult).then_inc(dve_pick, 1)

            ve.wait_ge(dve_pick, 1)
            number = best[:, GB].rearrange("p h k -> p (h k)")
            ch.mark(ve.tensor_copy(gate3[:], pick[:, 2, GB].rearrange("p h k -> p (h k)")))
            ch.link(ve.scalar_tensor_tensor(out=number, in0=pick[:, 0, GB].rearrange("p h k -> p (h k)"),
                                            scalar=float(KEYS), in1=pick[:, 1, GB].rearrange("p h k -> p (h k)"),
                                            op0=ALU.mult, op1=ALU.add))
            ve.tensor_copy(ids[:], number).then_inc(dve_ids, 1)
            ve.wait_ge(act_pick, 3)

            def hot_rows(m, u):
                tokens = bass.ds(m * TB, TB)
                ve.tensor_tensor(onehot2[u][:], iota[:].unsqueeze(1).broadcast_to([P, TB, KEYS]),
                                 pickT[:, 1, tokens].unsqueeze(2).broadcast_to([P, TB, KEYS]), ALU.is_equal).then_inc(dve_hot, 1)
                for k in range(TB):
                    ve.tensor_scalar(gated1[u][:, k, :], iota[:], pickT[:, 0, bass.ds(m * TB + k, 1)],
                                     pickT[:, 2, bass.ds(m * TB + k, 1)], ALU.is_equal, ALU.mult).then_inc(dve_hot, 1)

            for u in range(2):
                hot_rows(u, u)
            with ve.Fori(1, TD // (2 * TB)) as i:
                for u in range(2):
                    ve.wait_ge(pe_g, 4 * i + 2 * u - 2)
                    hot_rows(2 * i + u, u)


            def down_lo(n, s, first=False):
                if n is not None and not first:
                    ve.wait_ge(pe_d, n - 1)
                for k in range(2):
                    ve.wait_ge(act_dhi, 2 * (0 if n is None else n) + k + 1)
                    part = slice(4 * k, 4 * k + 4)
                    ve.tensor_tensor(dlo[s][:, part, :].rearrange("p k e -> p (k e)"), bank[k][:],
                                     dhi[s][:, part, :].rearrange("p k e -> p (k e)").bitcast(F32),
                                     ALU.subtract).then_inc(dve_dlo, 1)

            def add_y(i, g, q):
                ve.wait_ge(pe_u, OUTS * i + q + 1)
                part = y[:, q // 2, (q % 2) * 512:(q % 2) * 512 + 512]
                ve.tensor_tensor(part, part, bank[4 + (OUTS * g + q) % 4][:], ALU.add).then_inc(dve_y, 1)

            def dot(n, k, turn):
                ve.wait_ge(rows_d_in[k], 4 * (n - k) + 16)
                if k or turn is not None:
                    ve.wait_ge(dve_dot, n)
                if turn is not None:
                    ve.wait_ge(act_g3, turn)
                ve.scalar_tensor_tensor(out=junk[:], in0=rows_d[k][:], scalar=1.0, in1=h2nat[:], op0=ALU.mult,
                                        op1=ALU.mult, accum_out=dots[:, k:k + 1]).then_inc(dve_dot, 1)

            def coefficients(i):
                ve.wait_ge(act_g3, i)
                ve.tensor_tensor(coef[:], gel3[:], gate3[:, bass.ds(4 * (i - 1), 4)], ALU.mult).then_inc(dve_coef, 1)
                ve.wait_ge(dve_coef, i)

            def add_up(n, k):
                ve.wait_ge(rows_u_in[k], 4 * (n - k) + 16)
                ve.scalar_tensor_tensor(out=y[:, GB, :], in0=rows_u[k][:], scalar=coef[:, k:k + 1], in1=y[:, GB, :],
                                        op0=ALU.mult, op1=ALU.add).then_inc(dve_add, 1)
                ve.wait_ge(dve_add, n + 1)

            def tile(i, g, s, turn, first=False, last=False):
                n, k = 2 * i + s, 2 * g + s
                if not last and not (first and s == 0):
                    down_lo(n + 1, 1 - s)
                if not first:
                    for q in range(3 * s, 3 * s + 3):
                        add_y(i - 1, 1 - g, q)
                ve.wait_ge(act_gelu, n + 1)
                ve.wait_ge(gate_in[s], 16 * i + 16)
                if not first:
                    ve.wait_ge(dve_alo, n - 1)
                ve.tensor_tensor(acts[s][:], gel[s][:], gate[s][:], ALU.mult).then_inc(dve_act, 1)
                ve.wait_ge(act_ahi, n + 1)
                ve.tensor_tensor(alo[g][s][:], acts[s][:], ahi[g][s][:].bitcast(F32), ALU.subtract).then_inc(dve_alo, 1)
                if turn is not None and k == 0:
                    coefficients(turn)
                if turn is not None:
                    add_up(n - 4, k)
                dot(n, k, turn)

            down_lo(None, 0)
            down_lo(1, 1, first=True)
            for q in range(4):
                ve.wait_ge(stored_part[q], 16)
            ch.link(ve.memset(y[:], 0.0))
            for g in range(2):
                for s in range(2):
                    tile(g, g, s, None, first=g == 0)
            with ve.Fori(1, TILES // 4 - 1) as i:
                for g in range(2):
                    for s in range(2):
                        tile(2 * i + g, g, s, i)
            for g in range(2):
                for s in range(2):
                    tile(TILES // 2 - 2 + g, g, s, TILES // 4 - 1, last=g == 1 and s == 1)
            coefficients(TILES // 4)
            for q in range(OUTS):
                add_y(TILES // 2 - 1, 1, q)
                if q < 4:
                    add_up(PICKS - 4 + q, q)
            ve.wait_ge(act_ss, NB + 3 * NB + NB)
            mean_square(ssq[:, 24:28], ssq[:, 24:28], D).then_inc(dve_ms, 1)
            ve.wait_ge(act_root, 2 + 2 * NB + 1)
            ch.link(ve.reciprocal(root[:, 16:20], root[:, 16:20]))
            for b in range(NB):
                ch.mark(ve.scalar_tensor_tensor(out=y[:, b, :], in0=y[:, b, :], scalar=root[:, 16 + b:17 + b], in1=gg2[:],
                                                op0=ALU.mult, op1=ALU.mult))
                ch.wait()
                ve.tensor_tensor(x1[:, b, :], x1[:, b, :], y[:, b, :], ALU.add).then_inc(dve_x1, 1)

        @block.tensor
        def _(pe):
            pe.wait_ge(act_silu, 1)
            pe.wait_ge(ident_ok, 3)
            pe.transpose(bank[7][:, 0:ROWS], rows[0:ROWS, :], ident[0:ROWS, 0:ROWS]).then_inc(pe_rows, 1)
            pe.wait_ge(misc_in, 16 * 6)
            for g in range(GROUPS):
                last = pe.transpose(bank[6][:, g * P:(g + 1) * P], sgw[:, g, :], ident[:])
            last.then_inc(pe_wT, 1)

            def ada_chunk(n):
                pe.wait_ge(dve_ada, 2 * n + 2)
                if n in (4, 5, 10, 11):
                    if n != 4:
                        pe.wait_ge(dve_gg, {5: 1, 10: 2, 11: 3}[n])
                    for e in range(2):
                        last = pe.matmul(bank[7][:], ones[:], part[n % 2][:, e, :], start=e == 0, stop=e == 1)
                else:
                    for j in range(4):
                        col = 4 * ADA_ORDER[n] + j
                        for e in range(2):
                            last = pe.matmul(bank[0][:, col:col + 1], part[n % 2][:, e, j * P:(j + 1) * P],
                                             ones[:, 0:1], start=e == 0, stop=e == 1)
                last.then_inc(pe_ada, 1)

            for n in range(4):
                ada_chunk(n)
            for j in range(KT):
                if j == 0:
                    pe.wait_ge(dve_xn1, NB)
                if j >= 4:
                    pe.wait_ge(act_h1 if j % 2 else dve_h1, (j - 4) // 2 + 1)
                for b in range(NB):
                    last = pe.transpose(bank[1 + j % 4][:, b * P:(b + 1) * P], xn1[:, b, j * P:(j + 1) * P], ident[:])
                last.then_inc(pe_h1, 1)
            pe.wait_ge(act_h1, 4)
            pe.wait_ge(dve_h1, 4)
            pe.wait_ge(dve_wT, 1)
            def scores(b):
                if b >= 1:
                    pe.wait_ge(act_s, 2 * b)
                for s in range(2):
                    side = slice(s * HD, (s + 1) * HD)
                    for j in range(4):
                        for q in range(2):
                            at = b * P + q * CHUNK
                            last = pe.matmul(bank[1 + s][q * CHUNK:(q + 1) * CHUNK, j * P:(j + 1) * P],
                                             qT[side, j, at:at + CHUNK], kT[side, at:at + P], start=True, stop=True)
                    last.then_inc(pe_s, 1)

            def transpose_probs(b):
                pe.wait_ge(dve_p, b + 1)
                if b >= 1:
                    pe.wait_ge(act_o, b)
                for s in range(2):
                    for j in range(4):
                        last = pe.transpose(bank[3 + s][:, j * P:(j + 1) * P], s_sb[b % 2][:, 4 * s + j, :], ident[:])
                    last.then_inc(pe_pt, 1)

            def attend(b):
                pe.wait_ge(act_pt, 2 * b + 2)
                for h in range(HEADS):
                    for q in range(2):
                        last = pe.matmul(bank[3][(h % 2) * HD:(h % 2 + 1) * HD, (h // 2) * P + q * CHUNK:(h // 2) * P + (q + 1) * CHUNK],
                                         (v if q else vs)[:, b, (h // 4) * HD:(h // 4 + 1) * HD],
                                         pT[b % 2][:, h, q * CHUNK:(q + 1) * CHUNK], start=True, stop=True)
                last.then_inc(pe_o, 1)

            def mix_positions(g):
                pe.wait_ge(dve_vn, NB)
                if g >= 2:
                    pe.wait_ge(dve_sgu, g - 1)
                for b in range(NB):
                    last = pe.matmul(bank[5 + g % 2][:, b * P:(b + 1) * P], sv[:, b, g * P:(g + 1) * P], wT[:, g, :],
                                     start=True, stop=True)
                last.then_inc(pe_sgu, 1)

            pe.wait_ge(w_qkv_in, 16 * (1 + 2 * KT))
            for m in range(Z_JOBS):
                if m >= 5:
                    pe.wait_ge(act_z, m - 4 if m < Z_SV else m - 1)
                got = bank[Z_BANKS[m]]
                if m == Z_SV:
                    pe.wait_ge(w_sv_in, 16)
                elif m == Z_U:
                    pe.wait_ge(w_u_in, 16)
                if Z_SV <= m < Z_U:
                    at = CHUNK + (m - Z_SV) * P
                    for k in range(KT):
                        last = pe.matmul(got[:], hT[:, k, at:at + P], w_in_sb[:, k, SV_AT:SV_AT + SGU],
                                         start=k == 0, stop=k == KT - 1)
                elif m < Z_V or m >= Z_U:
                    for k in range(KT):
                        if m >= Z_U:
                            w = w_in_sb[:, k, U_AT + (m - Z_U) * P:U_AT + (m - Z_U + 1) * P]
                        elif m == Z_K:
                            w = w_in_sb[:, k, K_AT:K_AT + KVW]
                        else:
                            w = w_in_sb[:, k, (m - Z_Q) * P:(m - Z_Q + 1) * P]
                        last = pe.matmul(got[:], w, hT[:, k, CHUNK:], start=k == 0, stop=k == KT - 1)
                else:
                    at = CHUNK if m == Z_V else 0
                    for b in range(NB):
                        for k in range(KT):
                            last = pe.matmul(got[:, b * P:(b + 1) * P], hT[:, k, at + b * P:at + (b + 1) * P],
                                             w_in_sb[:, k, V_AT:V_AT + KVW], start=k == 0, stop=k == KT - 1)
                last.then_inc(pe_z, 1)
                if m in Z_ADA:
                    ada_chunk(Z_ADA[m])
                if m == Z_SV:
                    pe.wait_ge(act_z, Z_SV)
                    scores(0)
                elif m == Z_SV + 1:
                    scores(1)
                elif m == Z_SV + 2:
                    transpose_probs(0)
                elif m == Z_SV + 3:
                    attend(0)
                    scores(2)
                elif m == Z_U:
                    transpose_probs(1)
                elif m == Z_U + 1:
                    attend(1)
                    scores(3)
                elif m == Z_U + 2:
                    transpose_probs(2)
                elif m == Z_U + 3:
                    attend(2)
            transpose_probs(3)
            pe.wait_ge(act_z, Z_JOBS)
            mix_positions(0)
            attend(3)
            for g in range(1, GROUPS):
                mix_positions(g)
            pe.wait_ge(w_out_in, 32)
            pe.wait_ge(act_o, NB)
            pe.wait_ge(dve_sgu, GROUPS)
            for b in range(NB):
                for s in range(2):
                    if b >= 2:
                        pe.wait_ge(dve_mix, 2 * (b - 2) + s + 1)
                    for k in range(KT):
                        last = pe.matmul(bank[1 + 2 * (b % 2) + s][:], catT[:, k, b * P:(b + 1) * P],
                                         w_out_sb[:, k, s * 512:s * 512 + 512], start=k == 0, stop=k == KT - 1)
                    last.then_inc(pe_mix, 1)
            pe.wait_ge(keys_in, 16)
            for m in range(4):
                if m >= 2:
                    pe.wait_ge(act_keys, m - 1)
                for k in range(4):
                    last = pe.transpose(bank[5 + m % 2][:, k * P:(k + 1) * P], keys[:, 4 * m + k, :], ident[:])
                last.then_inc(pe_keys, 1)
            pe.wait_ge(dve_xn2, NB)
            for j in range(KT + 1):
                if j < KT:
                    if j >= 4:
                        pe.wait_ge(dve_htmp, j - 3)
                    for b in range(NB):
                        last = pe.transpose(bank[1 + j % 4][:, b * P:(b + 1) * P], xn2[:, b, j * P:(j + 1) * P], ident[:])
                    last.then_inc(pe_h2, 1)
                if j >= 1:
                    k = j - 1
                    pe.wait_ge(dve_htmp, k + 1)
                    pe.transpose(bank[7 * (k // 4)][:, (k % 4) * P:(k % 4 + 1) * P], htmp[k % 2][:, GB * P:T],
                                 ident[:]).then_inc(pe_hn, 1)
            pe.wait_ge(act_h2, KT)
            pe.wait_ge(dve_h2, KT)
            pe.wait_ge(act_keys, 4)
            def head(h, first=False):
                for s in range(2):
                    pe.wait_ge(act_wq, 2 * h + s + 1)
                    pe.wait_ge(pool_wq, 2 * h + s + 1)
                    for k in range(KT):
                        pe.matmul(bank[1 + s][:], wqhi[s][:, k, :], h2hi[:, k, :], start=k == 0, stop=False)
                        pe.matmul(bank[1 + s][:], wqhi[s][:, k, :], h2lo[:, k, :], start=False, stop=False)
                        last = pe.matmul(bank[1 + s][:], wqlo[s][:, k, :], h2hi[:, k, :], start=False, stop=k == KT - 1)
                    last.then_inc(pe_q, 1)
                for s in range(2):
                    pe.wait_ge(act_q, 2 * h + s + 1)
                    if not first:
                        pe.wait_ge(act_sc, 2 * h)
                    for b in range(NB):
                        last = pe.matmul(bank[3 + s][:, b * P:(b + 1) * P], pqT[s][:, b * P:(b + 1) * P],
                                         keysT[:, bass.ds(2 * h + s, 1), :].rearrange("p o k -> p (o k)"),
                                         start=True, stop=True)
                    last.then_inc(pe_sc, 1)

            head(0, first=True)
            with pe.Fori(1, PH) as h:
                head(h)
            pe.wait_ge(dve_pick, 1)
            pe.wait_ge(dve_sel, 2 * PH)
            for k in range(3):
                for b in range(GB):
                    last = pe.transpose(bank[5 + k][:, b * P:(b + 1) * P], pick[:, k, b].rearrange("p h k -> p (h k)"), ident[:])
                last.then_inc(pe_pick, 1)

            def gate_products(m, u, first=False):
                pe.wait_ge(dve_hot, 9 * m + 9)
                for s in range(2):
                    if not first:
                        pe.wait_ge(act_g, 2 * m + s - 3)
                    for k in range(4):
                        last = pe.matmul(bank[1 + 2 * u + s][:, k * P:(k + 1) * P], onehot2[u][:, 4 * s + k, :],
                                         gated1[u][:, 4 * s + k, :], start=True, stop=True)
                    last.then_inc(pe_g, 1)

            for u in range(2):
                gate_products(u, u, first=True)
            with pe.Fori(1, TD // (2 * TB)) as i:
                for u in range(2):
                    gate_products(2 * i + u, u)


            def transpose_down(n, s, first=False):
                pe.wait_ge(down_in[s], 8 * (n - s) + 16)
                for k in range(2):
                    if not first:
                        pe.wait_ge(dve_dlo, 2 * n + k - 1)
                    elif k:
                        pe.wait_ge(act_g, GB * (P // 4))
                    for q in range(4):
                        at = (4 * k + q) * P
                        last = pe.transpose(bank[k][:, q * P:(q + 1) * P], down[s][:, at:at + P], ident[:])
                    last.then_inc(pe_t, 1)

            def multiply_down(n, s, first=False):
                pe.wait_ge(dve_dlo, 2 * n + 2)
                if not first:
                    pe.wait_ge(act_gelu, n - 1)
                for k in range(KT):
                    pe.matmul(bank[2 + s][:, 0:TD], dhi[s][:, k, :], h2hi[:, k, 0:TD], start=k == 0, stop=False)
                    pe.matmul(bank[2 + s][:, 0:TD], dhi[s][:, k, :], h2lo[:, k, 0:TD], start=False, stop=False)
                    last = pe.matmul(bank[2 + s][:, 0:TD], dlo[s][:, k, :], h2hi[:, k, 0:TD], start=False, stop=k == KT - 1)
                last.then_inc(pe_d, 1)

            def multiply_up(i, g, q, first=False):
                if q >= 4 or not first:
                    pe.wait_ge(dve_y, OUTS * i + q - 3)
                got = bank[4 + (OUTS * g + q) % 4]
                tokens, half = slice((q // 2) * P, (q // 2 + 1) * P), slice((q % 2) * 512, (q % 2) * 512 + 512)
                for s in range(GROUP):
                    pe.matmul(got[:], ahi[g][s][:, tokens], uhi[g][s][:, half], start=s == 0, stop=False)
                    pe.matmul(got[:], ahi[g][s][:, tokens], ulo[g][s][:, half], start=False, stop=False)
                    last = pe.matmul(got[:], alo[g][s][:, tokens], uhi[g][s][:, half], start=False, stop=s == GROUP - 1)
                last.then_inc(pe_u, 1)

            def group_ready(i):
                pe.wait_ge(dve_alo, 2 * i + 2)
                pe.wait_ge(pool_ulo, 2 * i + 2)

            def tile(i, g, s, first=False, second=False, last=False):
                n = 2 * i + s
                if not last:
                    transpose_down(n + 1, 1 - s)
                multiply_down(n, s, first=first)
                if not first:
                    if s == 0:
                        group_ready(i - 1)
                    for q in range(3 * s, 3 * s + 3):
                        multiply_up(i - 1, 1 - g, q, first=second)

            transpose_down(0, 0, first=True)
            for g in range(2):
                for s in range(2):
                    tile(g, g, s, first=g == 0, second=g == 1)
            with pe.Fori(1, TILES // 4 - 1) as i:
                for g in range(2):
                    for s in range(2):
                        tile(2 * i + g, g, s)
            for g in range(2):
                for s in range(2):
                    tile(TILES // 2 - 2 + g, g, s, last=g == 1 and s == 1)
            group_ready(TILES // 2 - 1)
            for q in range(OUTS):
                multiply_up(TILES // 2 - 1, 1, q)


_INS = ["x", "c", "w_ada", "b_ada", "g_pre_mix", "g_post_mix", "g_pre_ffn", "g_post_ffn", "w_in", "attn_sinks",
        "sgu_norm", "sgu_w", "sgu_b", "w_out", "peer_query", "peer_keys", "peer_down", "peer_up"]


def kernel(**inputs):
    import numpy as np
    import concourse.bacc as bacc
    from concourse.bass_utils import run_bass_kernel_spmd

    nc = bacc.Bacc("TRN2", target_bir_lowering=False, num_devices=1)
    arrays = {f"in_{n}": np.ascontiguousarray(inputs[n]) for n in _INS}
    args = [nc.dram_tensor(n, a.shape, mybir.dt.from_np(a.dtype), kind="ExternalInput").ap() for n, a in arrays.items()]
    result = nc.dram_tensor("out_x", arrays["in_x"].shape, F32, kind="ExternalOutput").ap()
    build_block(nc, *args, result)
    ran = run_bass_kernel_spmd(nc, [arrays], core_ids=[0])
    return ran.results[0]["out_x"]
```

```python
from contextlib import ExitStack

import concourse.bass as bass
from concourse import mybir

F32 = mybir.dt.float32
F32R = mybir.dt.float32r
U32 = mybir.dt.uint32
ALU = mybir.AluOpType
ACT = mybir.ActivationFunctionType
AXX = mybir.AxisListType.X

P = 128
D = 1024
T = 512
KT = D // P
NB = T // P
HEADS, KV_HEADS, HD = 8, 2, 64
CHUNK = 64
ATT = HEADS * HD
KVW = KV_HEADS * HD
SGU = D - ATT
GROUPS = SGU // P
IN_W = ATT + 2 * KVW + 2 * SGU
K_AT, V_AT = ATT, ATT + KVW
U_AT, SV_AT = ATT + 2 * KVW, ATT + 2 * KVW + SGU
PH = 8
TOPK = 16
KEYS = 128
TILES = KEYS
EPS = 1e-6
LOWEST = -3.0e38

ADA_COLUMN_A = [2, 3, 0, 1]
ADA_ROW_1 = [4, 5]
ADA_COLUMN_B = [8, 9, 6, 7]
ADA_ROW_2 = [10, 11]
ADA_ORDER = ADA_COLUMN_A + ADA_ROW_1 + ADA_COLUMN_B + ADA_ROW_2
ADA_SLOTS = 3
SH1, SC1, SH2, SC2 = 0, 8, 24, 32
ROW_C, ROW_B, ROW_G1, ROW_G2, ROWS = 0, 8, 56, 64, 72

Z_K, Z_Q, Z_V, Z_VS, Z_SV, Z_U, Z_JOBS = 0, 1, 5, 6, 7, 11, 15
Z_BANKS = [5, 6, 1, 2, 3] + [5, 6] * 5
Z_ADA = {2: 4, 3: 5, 4: 6, 5: 7, 6: 8, 7: 9, 9: 10, 10: 11}
HEAD_STEPS = 3 * 20 + 12
TB = 8
BY_POOL, BY_ACT = 2, 2
GB = NB - 1
TD = GB * P
PICKS = PH * TOPK
ROWS_16, ROWS_4 = 3, 8
AT_4 = ROWS_16 * TOPK
AT_1 = AT_4 + (ROWS_4 - ROWS_16) * 4
SUMS = AT_1 + TOPK - ROWS_4
OUTS = 2 * GB
GROUP = 2


class Chain:

    def __init__(self, eng, sem):
        self.eng, self.sem, self.base, self.n = eng, sem, 0, 0

    def mark(self, ins):
        ins.then_inc(self.sem, 1)
        self.n += 1

    def wait(self, but=0):
        self.eng.wait_ge(self.sem, self.base + self.n - but)

    def link(self, ins):
        self.mark(ins)
        self.wait()

    def enter(self, turn, per_turn):
        self.before, self.per_turn = self.base + self.n, per_turn
        self.base, self.n = turn * per_turn + self.before, 0

    def leave(self, turns):
        assert self.n == self.per_turn, self.n
        self.base, self.n = self.before + turns * self.per_turn, 0


class Region:

    def __init__(self, nc, start, limit):
        self.nc, self.at, self.limit = nc, start, limit

    def __call__(self, name, shape, dt=F32):
        size = 4
        for n in shape:
            size *= n
        t = self.nc.alloc_sbuf_tensor_at(name, [P] + list(shape), dt, offset=self.at)
        self.at += -(-size // 32) * 32
        assert self.at <= self.limit, (name, self.at - self.limit)
        return t


def build_block(nc, x, c, w_ada, b_ada, g_pre_mix, g_post_mix, g_pre_ffn, g_post_ffn, w_in, attn_sinks,
                sgu_norm, sgu_w, sgu_b, w_out, peer_query, peer_keys, peer_down, peer_up, out):
    ctx = ExitStack()
    with ctx:
        def sem(name):
            return ctx.enter_context(nc.semaphore(name))

        base, limit = -(-nc.sbuf_base // 32) * 32, nc.sbuf_usable_end
        kept = Region(nc, base, limit)
        ident = kept("ident", [P])
        iota = kept("iota", [P])
        ones = kept("ones", [P])
        columns = kept("columns", [ROWS])
        modc_at = kept.at
        modc = kept("modc", [48])
        scale1 = kept("scale1", [KT])
        scale2 = kept("scale2", [KT])
        ssq = kept("ssq", [32])
        root = kept("root", [32])
        svsum = kept("svsum", [NB])
        x1 = kept("x1", [NB, D])
        gg2 = kept("gg2", [D])
        h2nat_at = kept.at
        h2nat = kept("h2nat", [D])
        ids_at = kept.at
        ids = kept("ids", [PICKS], U32)
        gate3 = kept("gate3", [PICKS])
        h2_at = kept.at
        h2hi = kept("h2hi", [KT, T], F32R)
        h2lo = kept("h2lo", [KT, T], F32R)
        rest_at = kept.at

        r = Region(nc, h2_at, rest_at)
        qT = r("qT", [4, T])
        uT_at = r.at
        uT = r("uT", [GROUPS, T])
        catT_at = r.at
        catT = r("catT", [KT, T])
        xn1 = Region(nc, catT_at, rest_at)("xn1", [NB, D])
        r = Region(nc, rest_at, limit)
        gg1 = r("gg1", [D])
        hT_at = r.at
        HTW = CHUNK + T
        hT = r("hT", [KT, HTW])
        w_in_at = r.at
        w_in_sb = r("w_in_sb", [KT, IN_W])
        ada_at = r.at
        ada = [r(f"ada{i}", [KT, 512]) for i in range(ADA_SLOTS)]
        kT = r("kT", [HTW])
        v = r("v", [NB, KVW])
        vs = r("vs", [NB, KVW])
        sv = r("sv", [NB, SGU])
        wT = r("wT", [GROUPS, P])
        c_col = r("c_col", [KT])
        part = [r("part0", [2, 512])]
        sinks = r("sinks", [HEADS])
        amax = r("amax", [HEADS])
        asum = r("asum", [HEADS])
        asink = [r(f"asink{i}", [HEADS]) for i in range(2)]
        rows = r("rows", [P])
        r = Region(nc, uT_at, uT_at + 2 * T * 4)
        sgw = r("sgw", [GROUPS, P])
        r = Region(nc, uT_at + 2 * T * 4, uT_at + 4 * T * 4)
        part += [r("part1", [2, 512])]
        ajunk = catT[:, KT - 1, :]
        r = Region(nc, h2nat_at, ids_at)
        sgub = r("sgub", [GROUPS, P])
        sgun = r("sgun", [SGU])
        r = Region(nc, ada_at, ada_at + KT * 512 * 4)
        s_sb = [r(f"s_sb{i}", [HEADS, P]) for i in range(2)]
        pT = [r(f"pT{i}", [HEADS, P]) for i in range(2)]
        r = Region(nc, ada_at + KT * 512 * 4, ada_at + 3 * KT * 512 * 4)
        w_out_sb = r("w_out_sb", [KT, D])
        r = Region(nc, w_in_at, ada_at)
        gp1 = r("gp1", [D])
        gp2 = r("gp2", [D])
        xn2 = r("xn2", [NB, D])

        keys_at = r.at
        keys = r("keys", [2 * PH, P])
        wq = [r(f"wq{i}", [KT, P]) for i in range(2)]
        keysT = r("keysT", [2 * PH, P])
        r = Region(nc, ada_at, limit)
        wqhi = [r(f"wqhi{i}", [KT, P], F32R) for i in range(2)]
        wqlo = [r(f"wqlo{i}", [KT, P], F32R) for i in range(2)]
        assert r.at <= ada_at + KT * 512 * 4
        htmp = [r(f"htmp{i}", [T]) for i in range(2)]
        pqT = [r(f"pqT{i}", [T]) for i in range(2)]
        score = [r(f"score{i}", [NB, KEYS]) for i in range(2)]
        hit = [r(f"hit{i}", [NB, TOPK, TOPK]) for i in range(2)]
        r = Region(nc, w_in_at, keys_at)
        cand = r("cand", [NB, SUMS])
        top = r("top", [2, NB, TOPK])
        topi = r("topi", [2, NB, TOPK], U32)
        topf = r("topf", [2, NB, TOPK])
        bests = r("bests", [NB, TOPK])
        besti = r("besti", [NB, TOPK], U32)
        pair = r("pair", [2, NB, TOPK], U32)
        pairf = r("pairf", [2, NB, TOPK])
        place = r("place", [NB, TOPK])
        start = r("start", [NB, TOPK])
        best = r("best", [NB, PH, TOPK])
        bsum = r("bsum", [NB, PH])
        pick = r("pick", [3, NB, PH, TOPK])
        r = Region(nc, rest_at, w_in_at)
        pickT = r("pickT", [3, TD])
        onehot2 = [r(f"onehot2_{i}", [TB, KEYS]) for i in range(2)]
        gated1 = [r(f"gated1_{i}", [TB, KEYS]) for i in range(2)]
        r = Region(nc, r.at, limit)
        stage = [r(f"stage{i}", [KEYS, P]) for i in range(2)]
        stage_1_at = r.at - KEYS * P * 4
        r = Region(nc, modc_at, modc_at + 48 * 4)
        own = [r(f"own{i}", [3, BY_POOL]) for i in range(2)]
        r = Region(nc, rest_at, limit)
        gate = [r(f"gate{i}", [TD]) for i in range(2)]
        gel = [r(f"gel{i}", [TD]) for i in range(2)]
        acts = [r(f"acts{i}", [TD]) for i in range(2)]
        ahi = [[r(f"ahi{g}{i}", [TD], F32R) for i in range(GROUP)] for g in range(2)]
        alo = [[r(f"alo{g}{i}", [TD], F32R) for i in range(GROUP)] for g in range(2)]
        y = r("y", [NB, D])
        junk = r("junk", [D])
        rows_d = [r(f"rows_d{i}", [D]) for i in range(4)]
        rows_u = [r(f"rows_u{i}", [D]) for i in range(4)]
        idx_d = [r(f"idx_d{i}", [1], U32) for i in range(4)]
        idx_u = [r(f"idx_u{i}", [1], U32) for i in range(4)]
        dots = r("dots", [4])
        gel3 = r("gel3", [4])
        coef = r("coef", [4])
        assert r.at <= stage_1_at
        r = Region(nc, stage_1_at, limit)
        down = [r(f"down{i}", [D]) for i in range(2)]
        up = [r(f"up{i}", [D]) for i in range(2)]
        dhi = [r(f"dhi{i}", [KT, P], F32R) for i in range(2)]
        dlo = [r(f"dlo{i}", [KT, P], F32R) for i in range(2)]
        uhi = [[r(f"uhi{g}{i}", [D], F32R) for i in range(GROUP)] for g in range(2)]
        ulo = [[r(f"ulo{g}{i}", [D], F32R) for i in range(GROUP)] for g in range(2)]

        bank = [ctx.enter_context(nc.psum_tensor(f"bank{i}", [P, 512], F32)) for i in range(8)]
        gates_dram = nc.dram_tensor("gates_dram", [TILES, KEYS, TD], F32).ap()

        x_v = x[0].rearrange("(b p) d -> b p d", p=P)
        out_v = out[0].rearrange("(b p) d -> b p d", p=P)
        ada_v = w_ada[0].rearrange("(k p) n -> p k n", p=P)
        w_in_v = w_in[0].rearrange("(k p) n -> p k n", p=P)
        w_out_v = w_out[0].rearrange("(k p) n -> p k n", p=P)
        wq_v = peer_query[0].rearrange("(k p) n -> p k n", p=P)
        keys_v = peer_keys[0].rearrange("h s n d -> n (h s) d")
        down_v = peer_down[0].rearrange("(n p) d -> n p d", p=P)
        up_v = peer_up[0].rearrange("(n p) d -> n p d", p=P)

        def row(ap):
            return ap.broadcast_to([P] + list(ap.shape[1:]))

        def one(view, n):
            return view[bass.ds(n, 1)].rearrange("o p m -> (o p) m")

        rows_in, sgw_in, misc_in, w_out_in = sem("rows_in"), sem("sgw_in"), sem("misc_in"), sem("w_out_in")
        w_qkv_in, w_sv_in, w_u_in = sem("w_qkv_in"), sem("w_sv_in"), sem("w_u_in")
        x_in = [sem(f"x_in{i}") for i in range(NB)]
        ada_in = [sem(f"ada_in{i}") for i in range(ADA_SLOTS)]
        gp_in, keys_in = sem("gp_in"), sem("keys_in")
        wq_in = [sem(f"wq_in{i}") for i in range(2)]
        stored = [sem(f"stored{i}") for i in range(2)]
        down_in = [sem(f"down_in{i}") for i in range(2)]
        up_in = [sem(f"up_in{i}") for i in range(2)]
        gate_in = [sem(f"gate_in{i}") for i in range(2)]
        rows_d_in = [sem(f"rows_d_in{i}") for i in range(4)]
        rows_u_in = [sem(f"rows_u_in{i}") for i in range(4)]
        stored_part = [sem(f"stored_part{i}") for i in range(4)]
        out_done = sem("out_done")
        ident_ok, zeros_ok = sem("ident_ok"), sem("zeros_ok")
        pe_rows, pe_wT, pe_ada, pe_h1, pe_z = (sem(n) for n in ("pe_rows", "pe_wT", "pe_ada", "pe_h1", "pe_z"))
        pe_s, pe_pt, pe_o, pe_sgu, pe_mix = (sem(n) for n in ("pe_s", "pe_pt", "pe_o", "pe_sgu", "pe_mix"))
        pe_keys, pe_h2, pe_q, pe_sc, pe_pick = (sem(n) for n in ("pe_keys", "pe_h2", "pe_q", "pe_sc", "pe_pick"))
        pe_g, pe_t, pe_d, pe_u, pe_hn = (sem(n) for n in ("pe_g", "pe_t", "pe_d", "pe_u", "pe_hn"))
        act_silu, act_ss, act_root, act_h1, act_z, act_sv = (
            sem(n) for n in ("act_silu", "act_ss", "act_root", "act_h1", "act_z", "act_sv"))
        act_s, act_exp, act_pt, act_o = (sem(n) for n in ("act_s", "act_exp", "act_pt", "act_o"))
        act_keys, act_h2, act_wq, act_q, act_sc, act_gexp, act_pick, act_g = (
            sem(n) for n in ("act_keys", "act_h2", "act_wq", "act_q", "act_sc", "act_gexp", "act_pick", "act_g"))
        act_far, act_hit = sem("act_far"), sem("act_hit")
        act_away, act_hot = sem("act_away"), sem("act_hot")
        act_dhi, act_uhi, act_gelu, act_ahi, act_hn, act_g3 = (
            sem(n) for n in ("act_dhi", "act_uhi", "act_gelu", "act_ahi", "act_hn", "act_g3"))
        dve = sem("dve")
        dve_ada = sem("dve_ada")
        dve_ms, dve_xn1, dve_mod, dve_h1, dve_wT = (
            sem(n) for n in ("dve_ms", "dve_xn1", "dve_mod", "dve_h1", "dve_wT"))
        dve_center, dve_vn, dve_sgu, dve_sub, dve_p, dve_gg = (
            sem(n) for n in ("dve_center", "dve_vn", "dve_sgu", "dve_sub", "dve_p", "dve_gg"))
        dve_mix, dve_x1, dve_xn2, dve_htmp, dve_h2 = (
            sem(n) for n in ("dve_mix", "dve_x1", "dve_xn2", "dve_htmp", "dve_h2"))
        dve_half, dve_top, dve_pair, dve_sel, dve_bsub, dve_pick, dve_hot = (
            sem(n) for n in ("dve_half", "dve_top", "dve_pair", "dve_sel", "dve_bsub", "dve_pick", "dve_hot"))
        dve_dlo, dve_act, dve_alo, dve_y = (sem(n) for n in ("dve_dlo", "dve_act", "dve_alo", "dve_y"))
        dve_ids, dve_dot, dve_coef, dve_add, dve_normed = (sem(n) for n in ("dve_ids", "dve_dot", "dve_coef", "dve_add", "dve_normed"))
        pool_wq, pool_off, pool_hit, pool_hot, pool_own, pool_ulo, pool_idx, pool_x1, pool = (
            sem(n) for n in ("pool_wq", "pool_off", "pool_hit", "pool_hot", "pool_own", "pool_ulo", "pool_idx", "pool_x1", "pool"))

        block = ctx.enter_context(nc.Block())

        @block.sync
        def _(sp):
            sp.dma_start(rows[ROW_C:ROW_C + KT, :], c.rearrange("o (k p) -> (o k) p", p=P)).then_inc(rows_in, 16)
            sp.dma_start(rows[ROW_B:ROW_B + 48, :], b_ada.rearrange("o (k p) -> (o k) p", p=P)).then_inc(rows_in, 16)
            sp.dma_start(rows[ROW_G1:ROW_G1 + KT, :], g_pre_mix.rearrange("o (k p) -> (o k) p", p=P)).then_inc(rows_in, 16)
            sp.dma_start(rows[ROW_G2:ROW_G2 + KT, :], g_pre_ffn.rearrange("o (k p) -> (o k) p", p=P)).then_inc(rows_in, 16)

            def load_ada(n):
                q = ADA_ORDER[n]
                if n >= ADA_SLOTS:
                    sp.wait_ge(dve_ada, 2 * (n - ADA_SLOTS + 1))
                sp.dma_start(ada[n % ADA_SLOTS][:], ada_v[:, :, q * 512:q * 512 + 512]).then_inc(ada_in[n % ADA_SLOTS], 16)

            load_ada(0)
            for b in range(NB):
                sp.dma_start(x1[:, b, :], x_v[b]).then_inc(x_in[b], 16)
            for n in range(1, 4):
                load_ada(n)
            sp.dma_start(w_in_sb[:, :, ATT:U_AT], w_in_v[:, :, ATT:U_AT]).then_inc(w_qkv_in, 16)
            for k in range(KT):
                for s in range(2):
                    sp.dma_start(w_in_sb[:, k, 0:ATT].rearrange("p (j s n) -> p j s n", j=4, s=2)[:, :, s, :],
                                 w_in_v[:, k, s * 256:s * 256 + 256].rearrange("p (j n) -> p j n", j=4)
                                 ).then_inc(w_qkv_in, 16)
            sp.dma_start(gg1[:], row(b_ada[:, 2 * D:3 * D])).then_inc(misc_in, 16)
            sp.dma_start(gg2[:], row(b_ada[:, 5 * D:6 * D])).then_inc(misc_in, 16)
            sp.dma_start(sgub[:].rearrange("p g i -> p (g i)"), row(sgu_b.rearrange("o g i -> o (g i)"))).then_inc(misc_in, 16)
            sp.dma_start(sgun[:], row(sgu_norm)).then_inc(misc_in, 16)
            sp.dma_start(sinks[:], row(attn_sinks)).then_inc(misc_in, 16)
            load_ada(4)
            load_ada(5)
            sp.dma_start(w_in_sb[:, :, SV_AT:], w_in_v[:, :, SV_AT:]).then_inc(w_sv_in, 16)
            load_ada(6)
            load_ada(7)
            sp.dma_start(w_in_sb[:, :, U_AT:SV_AT], w_in_v[:, :, U_AT:SV_AT]).then_inc(w_u_in, 16)
            for n in range(8, len(ADA_ORDER)):
                load_ada(n)
            sp.wait_ge(dve_ada, 2 * len(ADA_ORDER))
            for q in range(2):
                sp.dma_start(w_out_sb[:, 4 * q:4 * q + 4, :], w_out_v[:, 4 * q:4 * q + 4, :]).then_inc(w_out_in, 16)
            sp.wait_ge(pe_z, Z_JOBS)
            sp.dma_start(gp1[:], row(g_post_mix)).then_inc(gp_in, 16)
            sp.dma_start(gp2[:], row(g_post_ffn)).then_inc(gp_in, 16)

            sp.dma_start(keys[:], keys_v).then_inc(keys_in, 16)

            def load_wq(h, s):
                sp.dma_start(wq[s][:], wq_v[:, :, bass.ds(h * 256 + s * P, P)]).then_inc(wq_in[s], 16)

            for s in range(2):
                load_wq(0, s)
            with sp.Fori(1, PH) as h:
                for s in range(2):
                    sp.wait_ge(act_wq, 2 * h - 1 + s)
                    sp.wait_ge(pool_wq, 2 * h - 1 + s)
                    load_wq(h, s)

            def store_block(b, keys_1, signal):
                sp.dma_start(gates_dram[keys_1, :, b * P:(b + 1) * P].rearrange("i p t -> p i t"),
                             stage[b % 2][:, keys_1, :]).then_inc(signal, 16)

            def load_down(n, s):
                sp.dma_start(down[s][:], one(down_v, n)).then_inc(down_in[s], 16)

            def load_up(n, s):
                sp.dma_start(up[s][:], one(up_v, n)).then_inc(up_in[s], 16)

            def load_gate(n, s):
                sp.dma_start(gate[s][:], one(gates_dram, n)).then_inc(gate_in[s], 16)

            for b in range(GB - 1):
                sp.wait_ge(act_g, (b + 1) * (P // 4))
                store_block(b, slice(0, KEYS), stored[b % 2])
            sp.wait_ge(stored[1], 16)
            for s in range(2):
                load_down(s, s)
                load_up(s, s)
            sp.wait_ge(stored[0], 16)
            sp.wait_ge(act_g, GB * (P // 4))
            store_block(GB - 1, slice(0, 32), stored_part[0])
            sp.wait_ge(stored_part[0], 16)
            for s in range(2):
                load_gate(s, s)

            def turn(i, first=False):
                for s in range(2):
                    n = 2 * i + s
                    sp.wait_ge(pe_t, 2 * n + 2)
                    load_down(n + 2, s)
                    sp.wait_ge(pool_ulo, n + 1)
                    load_up(n + 2, s)
                    sp.wait_ge(dve_act, n + 1)
                    load_gate(n + 2, s)
                    if first:
                        store_block(GB - 1, slice(32 * s + 32, 32 * s + 64), stored_part[s + 1])

            turn(0, first=True)
            store_block(GB - 1, slice(96, KEYS), stored_part[3])
            turn(1)
            for q in range(1, 4):
                sp.wait_ge(stored_part[q], 16)
            with sp.Fori(2, TILES // 2 - 1) as i:
                turn(i)

            for b in range(NB):
                if b < 2:
                    sp.wait_ge(pool_x1, b + 1)
                else:
                    sp.wait_ge(dve_x1, NB + b - 1)
                sp.dma_start(out_v[b], x1[:, b, :]).then_inc(out_done, 16)
            sp.wait_ge(out_done, 16 * NB)

        @block.gpsimd
        def _(gp):
            gp.memset(ident[:], 0.0).then_inc(pool, 1)
            gp.memset(ones[:], 1.0).then_inc(ident_ok, 1)
            gp.iota(iota[:], pattern=[[1, P]], base=0, channel_multiplier=0,
                    allow_small_or_imprecise_dtypes=True).then_inc(ident_ok, 1)
            gp.wait_ge(pool, 1)
            gp.affine_select(out=ident[:], in_=ident[:], compare_op=ALU.not_equal, fill=1.0, base=0,
                             pattern=[[-1, P]], channel_multiplier=1).then_inc(ident_ok, 1)
            gp.wait_ge(ident_ok, 3)
            gp.memset(hT[:, :, 0:CHUNK], 0.0).then_inc(zeros_ok, 1)
            gp.wait_ge(zeros_ok, 1)
            gp.memset(kT[:, 0:CHUNK], 0.0).then_inc(zeros_ok, 1)
            gp.wait_ge(zeros_ok, 2)
            gp.memset(wT[CHUNK:P, :, 0:CHUNK], 0.0).then_inc(zeros_ok, 1)

            def split_wq(h, s):
                gp.wait_ge(act_wq, 2 * h + s + 1)
                gp.tensor_tensor(wqlo[s][:], wq[s][:], wqhi[s][:].bitcast(F32), ALU.subtract).then_inc(pool_wq, 1)

            def weigh_hits(h, first=False, splits=(True, True)):
                gp.wait_ge(dve_pair, h + 1)
                if not first:
                    gp.wait_ge(dve_sel, 2 * h)
                for s in range(2):
                    gp.tensor_tensor(hit[s][:], pairf[:, s].unsqueeze(3).broadcast_to([P, NB, TOPK, TOPK]),
                                     iota[:, 0:TOPK].unsqueeze(1).unsqueeze(1).broadcast_to([P, NB, TOPK, TOPK]),
                                     ALU.subtract).then_inc(pool_off, 1)
                gp.wait_ge(dve_top, h + 1)
                if splits[1]:
                    split_wq(h + 2, 1)
                for s in range(2):
                    gp.wait_ge(act_hit, 2 * h + s + 1)
                    gp.tensor_tensor(hit[s][:], hit[s][:],
                                     topf[:, s].unsqueeze(2).broadcast_to([P, NB, TOPK, TOPK]),
                                     ALU.mult).then_inc(pool_hit, 1)
                if splits[0]:
                    split_wq(h + 3, 0)

            for h in range(2):
                for s in range(2):
                    split_wq(h, s)
            split_wq(2, 0)
            weigh_hits(0, first=True)
            with gp.Fori(1, PH - 3) as h:
                weigh_hits(h)
            weigh_hits(PH - 3, splits=(False, True))
            weigh_hits(PH - 2, splits=(False, False))
            weigh_hits(PH - 1, splits=(False, False))

            gp.wait_ge(act_pick, 3)

            ch = Chain(gp, pool_own)

            def hot_rows(m, u):
                ch.link(gp.tensor_copy(own[u][:], pickT[:, :, bass.ds(m * TB + TB - BY_POOL, BY_POOL)]))
                gp.nop(nofuse=True)
                for k in range(BY_POOL):
                    gp.tensor_scalar(gated1[u][:, TB - BY_POOL + k, :], iota[:], own[u][:, 0, k:k + 1], own[u][:, 2, k:k + 1],
                                     ALU.is_equal, ALU.mult).then_inc(pool_hot, 1)

            for u in range(2):
                hot_rows(u, u)
            with gp.Fori(1, TD // (2 * TB)) as i:
                ch.enter(i - 1, 2)
                for u in range(2):
                    gp.wait_ge(pe_g, 4 * i + 2 * u - 2)
                    gp.wait_ge(pool_hot, BY_POOL * (2 * i + u - 1))
                    hot_rows(2 * i + u, u)
                ch.leave(TD // (2 * TB) - 1)

            ch = Chain(gp, pool_idx)

            def split_up(n, k):
                gp.wait_ge(act_uhi, n + 1)
                g, s = k // 2, k % 2
                gp.tensor_tensor(ulo[g][s][:], up[s][:], uhi[g][s][:].bitcast(F32), ALU.subtract).then_inc(pool_ulo, 1)

            def gather(rows_, table, idx, n, k):
                ch.link(gp.tensor_copy(idx[k][:], ids[:, bass.ds(n, 1)]))
                gp.nop(nofuse=True)
                return gp.indirect_dma_start(rows_[k][:], None, table[0], bass.IndirectOffsetOnAxis(ap=idx[k][:, 0:1], axis=0))

            def gather_up(n, k, first=False):
                if not first:
                    gp.wait_ge(dve_add, n - 3)
                gather(rows_u, peer_up, idx_u, n, k).then_inc(rows_u_in[k], 16)

            def turn(i, first=False, second=False):
                for k in range(4):
                    n = 4 * i + k
                    if not first:
                        gather_up(n - 4, k, first=second)
                        gp.wait_ge(dve_dot, n - 3)
                    gather(rows_d, peer_down, idx_d, n, k).then_inc(rows_d_in[k], 16)
                    if not first:
                        split_up(n, k)

            for k in range(4):
                split_up(k, k)
            for q in range(4):
                gp.wait_ge(stored_part[q], 16)
            gp.wait_ge(dve_ids, 1)
            turn(0, first=True)
            turn(1, second=True)
            with gp.Fori(2, PICKS // 4) as i:
                ch.enter(i - 2, 8)
                turn(i)
                ch.leave(PICKS // 4 - 2)
            for k in range(4):
                gather_up(PICKS - 4 + k, k)
            for b in range(2):
                gp.wait_ge(dve_normed, b + 1)
                gp.tensor_tensor(x1[:, b, :], x1[:, b, :], y[:, b, :], ALU.add).then_inc(pool_x1, 1)

        @block.scalar
        def _(act):
            act.dma_start(sgw[:], sgu_w[0].rearrange("g i j -> i g j")).then_inc(sgw_in, 16)
            act.wait_ge(rows_in, 64)
            act.activation(rows[0:KT, :], rows[0:KT, :], ACT.Silu).then_inc(act_silu, 1)
            for b in range(NB):
                act.wait_ge(x_in[b], 16)
                act.activation(xn1[:, b, :], x1[:, b, :], ACT.Square, accum_out=ssq[:, b:b + 1]).then_inc(act_ss, 1)
            act.wait_ge(dve_ms, 1)
            act.activation(root[:, 0:NB], ssq[:, 0:NB], ACT.Sqrt).then_inc(act_root, 1)
            act.wait_ge(dve_mod, 1)
            act.wait_ge(zeros_ok, 3)
            for j in range(1, KT, 2):
                act.wait_ge(pe_h1, j + 1)
                act.activation(hT[:, j, CHUNK:], bank[1 + j % 4][:], ACT.Identity,
                               bias=modc[:, SH1 + j:SH1 + j + 1], scale=scale1[:, j:j + 1]).then_inc(act_h1, 1)

            def scores_out(b):
                if b >= 2:
                    act.wait_ge(pe_pt, 2 * b - 2)
                for s in range(2):
                    act.wait_ge(pe_s, 2 * b + s + 1)
                    act.activation(s_sb[b % 2][:, 4 * s:4 * s + 4, :].rearrange("p h k -> p (h k)"),
                                   bank[1 + s][:], ACT.Copy).then_inc(act_s, 1)

            def exps(b):
                act.wait_ge(dve_sub, 2 * b + 2)
                flat = s_sb[b % 2][:].rearrange("p h k -> p (h k)")
                act.activation(flat, flat, ACT.Exp).then_inc(act_exp, 1)
                act.activation(asink[b % 2][:], asink[b % 2][:], ACT.Exp).then_inc(act_exp, 1)

            def transposed_out(b):
                if b >= 2:
                    act.wait_ge(pe_o, b - 1)
                for s in range(2):
                    act.wait_ge(pe_pt, 2 * b + s + 1)
                    act.activation(pT[b % 2][:, 4 * s:4 * s + 4, :].rearrange("p h k -> p (h k)"),
                                   bank[3 + s][:], ACT.Copy).then_inc(act_pt, 1)

            def attended_out(b):
                act.wait_ge(pe_o, b + 1)
                act.activation(catT[:, 0:4, b * P:(b + 1) * P],
                               bank[3][:].rearrange("p (h q) -> p h q", h=4), ACT.Copy).then_inc(act_o, 1)

            for m in range(Z_JOBS):
                act.wait_ge(pe_z, m + 1)
                got = bank[Z_BANKS[m]]
                if m == Z_K:
                    act.activation(kT[:, CHUNK:], got[:], ACT.Copy).then_inc(act_z, 1)
                elif m < Z_V:
                    act.activation(qT[:, m - Z_Q, :], got[:], ACT.Copy, scale=HD ** -0.5).then_inc(act_z, 1)
                elif m < Z_SV:
                    dst = v if m == Z_V else vs
                    act.activation(dst[:].rearrange("p b n -> p (b n)"), got[:], ACT.Copy).then_inc(act_z, 1)
                elif m < Z_U:
                    act.activation(sv[:, m - Z_SV, :], got[:], ACT.Gelu, accum_out=svsum[:, m - Z_SV:m - Z_SV + 1]).then_inc(act_z, 1)
                else:
                    act.activation(uT[:, m - Z_U, :], got[:], ACT.Gelu).then_inc(act_z, 1)
                if m == Z_SV:
                    act.wait_ge(dve_ada, 2 * 10)
                    scores_out(0)
                elif m == Z_SV + 1:
                    exps(0)
                    scores_out(1)
                elif m == Z_SV + 2:
                    transposed_out(0)
                    exps(1)
                elif m == Z_SV + 3:
                    attended_out(0)
                    scores_out(2)
                elif m == Z_U:
                    transposed_out(1)
                    exps(2)
                elif m == Z_U + 1:
                    attended_out(1)
                    scores_out(3)
                    for b in range(NB):
                        act.wait_ge(dve_center, b + 1)
                        if b:
                            act.wait_ge(act_sv, b)
                        act.activation(ajunk, sv[:, b, :], ACT.Square,
                                       accum_out=ssq[:, 4 + b:5 + b]).then_inc(act_sv, 1)
                elif m == Z_U + 2:
                    transposed_out(2)
                    act.wait_ge(dve_ms, 2)
                    act.activation(root[:, 4:8], ssq[:, 4:8], ACT.Sqrt).then_inc(act_root, 1)
                    exps(3)
                elif m == Z_U + 3:
                    attended_out(2)
            transposed_out(3)
            attended_out(3)

            def keys_out(m):
                act.wait_ge(pe_keys, m + 1)
                act.activation(keysT[:, 4 * m:4 * m + 4, :].rearrange("p n k -> p (n k)"), bank[5 + m % 2][:],
                               ACT.Copy).then_inc(act_keys, 1)

            def weights_hi(h, halves, first=False):
                for s in halves:
                    act.wait_ge(wq_in[s], 16 * h + 16)
                    if not first:
                        act.wait_ge(pe_q, 2 * h - 1 + s)
                    act.activation(wqhi[s][:], wq[s][:], ACT.Copy).then_inc(act_wq, 1)

            for b in range(NB):
                for s in range(2):
                    act.wait_ge(pe_mix, 2 * b + s + 1)
                    act.activation(xn2[:, b, s * 512:s * 512 + 512], bank[1 + 2 * (b % 2) + s][:], ACT.Square,
                                   accum_out=ssq[:, 8 + 2 * b + s:9 + 2 * b + s]).then_inc(act_ss, 1)
                act.wait_ge(dve_ms, 3 + 2 * b)
                act.activation(root[:, 8 + b:9 + b], ssq[:, 16 + b:17 + b], ACT.Sqrt).then_inc(act_root, 1)
                act.wait_ge(dve_x1, b + 1)
                act.activation(xn2[:, b, :], x1[:, b, :], ACT.Square, accum_out=ssq[:, 20 + b:21 + b]).then_inc(act_ss, 1)
                act.wait_ge(dve_ms, 4 + 2 * b)
                act.activation(root[:, 12 + b:13 + b], ssq[:, 20 + b:21 + b], ACT.Sqrt).then_inc(act_root, 1)
                if b == 0:
                    weights_hi(0, (0, 1), first=True)
                elif b < 3:
                    keys_out(2 * b - 2)
                    keys_out(2 * b - 1)
            for j in range(KT):
                act.wait_ge(dve_htmp, j + 1)
                act.activation(h2hi[:, j, :], htmp[j % 2][:], ACT.Copy).then_inc(act_h2, 1)
            for s in range(2):
                act.wait_ge(pe_hn, 4 * s + 4)
                act.activation(h2nat[:, s * 512:s * 512 + 512], bank[7 * s][:], ACT.Copy).then_inc(act_hn, 1)

            def queries_out(h, halves, first=False):
                for s in halves:
                    act.wait_ge(pe_q, 2 * h + s + 1)
                    if not first:
                        act.wait_ge(pe_sc, 2 * h)
                    act.activation(pqT[s][:], bank[1 + s][:], ACT.Copy).then_inc(act_q, 1)

            def scores_of_out(h, halves, first=False):
                for s in halves:
                    act.wait_ge(pe_sc, 2 * h + s + 1)
                    if not first:
                        act.wait_ge(dve_half, h)
                    act.activation(score[s][:].rearrange("p b k -> p (b k)"), bank[3 + s][:],
                                   ACT.Copy).then_inc(act_sc, 1)

            def hits(h):
                for s in range(2):
                    flat = hit[s][:].rearrange("p b i j -> p (b i j)")
                    act.wait_ge(pool_off, 2 * h + s + 1)
                    act.activation(flat, flat, ACT.Abs).then_inc(act_far, 1)
                    act.wait_ge(act_far, 2 * h + s + 1)
                    act.activation(flat, flat, ACT.Relu, bias=ones[:, 0:1], scale=-1.0).then_inc(act_hit, 1)

            for s in range(2):
                queries_out(0, (s,), first=True)
                weights_hi(1, (s,))
                scores_of_out(0, (s,), first=True)
            with act.Fori(1, PH - 1) as h:
                for s in range(2):
                    queries_out(h, (s,))
                    weights_hi(h + 1, (s,))
                scores_of_out(h, (0, 1))
                hits(h - 1)
            queries_out(PH - 1, (0, 1))
            scores_of_out(PH - 1, (0, 1))
            hits(PH - 2)
            act.wait_ge(dve_bsub, 1)
            act.activation(best[:].rearrange("p b h k -> p (b h k)"),
                           pick[:, 2].rearrange("p b h k -> p (b h k)"), ACT.Exp).then_inc(act_gexp, 1)
            hits(PH - 1)
            for k in range(3):
                act.wait_ge(pe_pick, k + 1)
                act.activation(pickT[:, k, :], bank[5 + k][:, 0:TD], ACT.Copy).then_inc(act_pick, 1)

            act.wait_ge(act_pick, 3)

            def hot_rows(m, u):
                for k in range(TB - BY_ACT, TB):
                    act.activation(onehot2[u][:, k, :], iota[:], ACT.Abs, bias=pickT[:, 1, bass.ds(m * TB + k, 1)],
                                   scale=-1.0).then_inc(act_away, 1)
                act.wait_ge(act_away, BY_ACT * (m + 1))
                own = onehot2[u][:, TB - BY_ACT:, :]
                act.activation(own, own, ACT.Relu, bias=ones[:, 0:1], scale=-1.0).then_inc(act_hot, 1)

            def gates_out(b, i, u):
                for s in range(2):
                    act.wait_ge(pe_g, b * 32 + 4 * i + 2 * u + s + 1)
                    act.activation(
                        stage[b % 2][:, :, bass.ds(i * (2 * TB) + u * TB + 4 * s, 4)].rearrange("p i t -> p t i"),
                        bank[1 + 2 * u + s][:].rearrange("p (t i) -> p t i", t=4),
                        ACT.Copy).then_inc(act_g, 1)

            for u in range(2):
                hot_rows(u, u)
            turns = P // (2 * TB)
            for b in range(GB):
                if b >= 2:
                    act.wait_ge(stored[b % 2], 16)
                with act.Fori(0, turns - 1 if b == GB - 1 else turns) as i:
                    for u in range(2):
                        gates_out(b, i, u)
                        hot_rows(b * 2 * turns + 2 * i + u + 2, u)
            for u in range(2):
                gates_out(GB - 1, turns - 1, u)

            def down_hi(n, s):
                for k in range(2):
                    act.wait_ge(pe_t, 2 * n + k + 1)
                    act.activation(dhi[s][:, 4 * k:4 * k + 4, :].rearrange("p k e -> p (k e)"), bank[k][:],
                                   ACT.Copy).then_inc(act_dhi, 1)

            def tile(i, g, s, first=False, second=False, last=False):
                n = 2 * i + s
                if not last:
                    down_hi(n + 1, 1 - s)
                if not first and not second:
                    act.wait_ge(pe_u, OUTS * (i - 1))
                act.wait_ge(up_in[s], 16 * i + 16)
                act.activation(uhi[g][s][:], up[s][:], ACT.Copy).then_inc(act_uhi, 1)
                act.wait_ge(pe_d, n + 1)
                if not first:
                    act.wait_ge(dve_act, n - 1)
                act.activation(gel[s][:], bank[2 + s][:, 0:TD], ACT.Gelu).then_inc(act_gelu, 1)
                act.wait_ge(dve_act, n + 1)
                act.activation(ahi[g][s][:], acts[s][:], ACT.Copy).then_inc(act_ahi, 1)

            def gelu_dots(i):
                act.wait_ge(dve_dot, 4 * i)
                act.activation(gel3[:], dots[:], ACT.Gelu).then_inc(act_g3, 1)

            down_hi(0, 0)
            for g in range(2):
                for s in range(2):
                    tile(g, g, s, first=g == 0, second=g == 1)
            with act.Fori(1, TILES // 4 - 1) as i:
                for g in range(2):
                    for s in range(2):
                        tile(2 * i + g, g, s)
                        if g == 0 and s == 0:
                            gelu_dots(i)
            for g in range(2):
                for s in range(2):
                    tile(TILES // 2 - 2 + g, g, s, last=g == 1 and s == 1)
                    if g == 0 and s == 0:
                        gelu_dots(TILES // 4 - 1)
            gelu_dots(TILES // 4)
            for b in range(NB):
                if b < GB:
                    act.wait_ge(dve_y, OUTS * (TILES // 2 - 1) + 2 * b + 2)
                else:
                    act.wait_ge(dve_add, PICKS)
                act.activation(junk[:], y[:, b, :], ACT.Square, accum_out=ssq[:, 24 + b:25 + b]).then_inc(act_ss, 1)
                act.wait_ge(act_ss, NB + 3 * NB + b + 1)
                if b % 2:
                    act.wait_ge(dve_ms, 2 + 2 * NB + b // 2 + 1)
                    act.activation(root[:, 15 + b:17 + b], ssq[:, 23 + b:25 + b], ACT.Sqrt).then_inc(act_root, 1)

        @block.vector
        def _(ve):
            ch = Chain(ve, dve)

            def mean_square(dst, src, width):
                return ve.tensor_scalar(dst, src, 1.0 / width, EPS, ALU.mult, ALU.add)

            ve.wait_ge(pe_rows, 1)
            ch.link(ve.tensor_copy(columns[:], bank[7][:, 0:ROWS]))
            ch.link(ve.tensor_copy(c_col[:], columns[:, 0:KT]))

            def multiply_ada(n):
                ve.wait_ge(ada_in[n % ADA_SLOTS], 16 * (n // ADA_SLOTS + 1))
                if n >= 2:
                    ve.wait_ge(pe_ada, n - 1)
                a, dst = ada[n % ADA_SLOTS], part[n % 2]
                for k in range(2):
                    ch.mark(ve.tensor_scalar(dst[:, k, :], a[:, k, :], c_col[:, k:k + 1], None, ALU.mult))
                for k in range(2, KT):
                    if k % 2 == 0:
                        ch.wait()
                    last = ve.scalar_tensor_tensor(out=dst[:, k % 2, :], in0=a[:, k, :], scalar=c_col[:, k:k + 1],
                                                   in1=dst[:, k % 2, :], op0=ALU.mult, op1=ALU.add)
                    if k < KT - 2:
                        ch.mark(last)
                    else:
                        last.then_inc(dve_ada, 1)

            ve.wait_ge(zeros_ok, 3)
            ve.wait_ge(pe_wT, 1)
            got = bank[6][:].rearrange("p (g i) -> p g i", g=GROUPS)
            ch.link(ve.tensor_copy(wT[0:CHUNK, :, :], got[0:CHUNK]))
            ve.tensor_copy(wT[CHUNK:P, :, CHUNK:P], got[CHUNK:P, :, CHUNK:P]).then_inc(dve_wT, 1)
            multiply_ada(0)
            ve.wait_ge(act_ss, NB)
            mean_square(ssq[:, 0:NB], ssq[:, 0:NB], D).then_inc(dve_ms, 1)
            ve.wait_ge(act_root, 1)
            ch.link(ve.reciprocal(root[:, 0:NB], root[:, 0:NB]))
            for b in range(NB):
                ve.tensor_scalar(xn1[:, b, :], x1[:, b, :], root[:, b:b + 1], None, ALU.mult).then_inc(dve_xn1, 1)

            def add_bias(first):
                ch.mark(ve.tensor_tensor(modc[:, first:first + KT], bank[0][:, first:first + KT],
                                         columns[:, ROW_B + first:ROW_B + first + KT], ALU.add))

            def make_scale(dst, first, row_g):
                return ve.scalar_tensor_tensor(out=dst[:], in0=modc[:, first:first + KT], scalar=1.0,
                                               in1=columns[:, row_g:row_g + KT], op0=ALU.add, op1=ALU.mult)

            for n in range(1, 4):
                multiply_ada(n)
            ve.wait_ge(pe_ada, 4)
            add_bias(SC1)
            add_bias(SH1)
            ch.wait()
            make_scale(scale1, SC1, ROW_G1).then_inc(dve_mod, 1)
            ve.wait_ge(dve_mod, 1)
            for j in range(0, KT, 2):
                ve.wait_ge(pe_h1, j + 1)
                ve.tensor_scalar(hT[:, j, CHUNK:], bank[1 + j % 4][:], scale1[:, j:j + 1],
                                 modc[:, SH1 + j:SH1 + j + 1], ALU.mult, ALU.add).then_inc(dve_h1, 1)
            def gate_half(n, gg, s):
                ve.wait_ge(pe_ada, n + 1)
                half = gg[:, s * 512:s * 512 + 512]
                ve.tensor_tensor(half, bank[7][:], half, ALU.add).then_inc(dve_gg, 1)


            def softmax_front(b):
                s = s_sb[b % 2]
                sink = asink[b % 2]
                ve.wait_ge(act_s, 2 * b + 2)
                if b == 0:
                    ch.link(ve.memset(s[0:CHUNK, :, 0:CHUNK], LOWEST))
                ch.link(ve.tensor_reduce(out=amax[:], in_=s[:], axis=AXX, op=ALU.max))
                ch.link(ve.tensor_tensor(amax[:], amax[:], sinks[:], ALU.max))
                ve.tensor_tensor(sink[:], sinks[:], amax[:], ALU.subtract).then_inc(dve_sub, 1)
                ve.tensor_tensor(s[:], s[:], amax[:].unsqueeze(2).broadcast_to([P, HEADS, P]),
                                 ALU.subtract).then_inc(dve_sub, 1)

            def softmax_back(b):
                s = s_sb[b % 2]
                ve.wait_ge(act_exp, 2 * b + 2)
                ch.link(ve.tensor_reduce(out=asum[:], in_=s[:], axis=AXX, op=ALU.add))
                ch.link(ve.tensor_tensor(asum[:], asum[:], asink[b % 2][:], ALU.add))
                ch.link(ve.reciprocal(asum[:], asum[:]))
                ve.tensor_tensor(s[:], s[:], asum[:].unsqueeze(2).broadcast_to([P, HEADS, P]), ALU.mult).then_inc(dve_p, 1)

            def spatial(g):
                ve.wait_ge(pe_sgu, g + 1)
                dst = catT[:, 4 + g, :]
                ch.link(ve.tensor_tensor(dst.rearrange("p (b i) -> p b i", b=NB),
                                         bank[5 + g % 2][:].rearrange("p (b i) -> p b i", b=NB),
                                         sgub[:, g].unsqueeze(1).broadcast_to([P, NB, P]), ALU.add))
                ve.tensor_tensor(dst, dst, uT[:, g, :], ALU.mult).then_inc(dve_sgu, 1)

            multiply_ada(4)
            multiply_ada(5)
            ve.wait_ge(misc_in, 16 * 5)
            gate_half(4, gg1, 0)
            multiply_ada(6)
            gate_half(5, gg1, 1)
            for n in range(7, 10):
                multiply_ada(n)
            softmax_front(0)
            multiply_ada(10)
            softmax_back(0)
            softmax_front(1)
            gate_half(10, gg2, 0)
            multiply_ada(11)
            softmax_back(1)
            gate_half(11, gg2, 1)
            ve.wait_ge(act_z, Z_U)
            ch.link(ve.tensor_scalar(svsum[:], svsum[:], -1.0 / SGU, None, ALU.mult))
            for b in range(NB):
                ve.tensor_scalar(sv[:, b, :], sv[:, b, :], svsum[:, b:b + 1], None, ALU.add).then_inc(dve_center, 1)
            softmax_front(2)
            softmax_back(2)
            softmax_front(3)
            ve.wait_ge(act_sv, NB)
            mean_square(ssq[:, 4:8], ssq[:, 4:8], SGU).then_inc(dve_ms, 1)
            ve.wait_ge(act_root, 2)
            ch.link(ve.reciprocal(root[:, 4:8], root[:, 4:8]))
            for b in range(NB):
                ve.scalar_tensor_tensor(out=sv[:, b, :], in0=sv[:, b, :], scalar=root[:, 4 + b:5 + b], in1=sgun[:],
                                        op0=ALU.mult, op1=ALU.mult).then_inc(dve_vn, 1)
            softmax_back(3)
            for g in range(GROUPS):
                spatial(g)
            ve.wait_ge(gp_in, 32)
            ve.wait_ge(dve_gg, 4)
            for gg, gp in ((gg1, gp1), (gg2, gp2)):
                ch.mark(ve.tensor_tensor(gg[:], gg[:], gp[:], ALU.mult))
            for b in range(NB):
                ve.wait_ge(act_ss, NB + 3 * b + 2)
                ch.link(ve.tensor_tensor(ssq[:, 16 + b:17 + b], ssq[:, 8 + 2 * b:9 + 2 * b], ssq[:, 9 + 2 * b:10 + 2 * b], ALU.add))
                mean_square(ssq[:, 16 + b:17 + b], ssq[:, 16 + b:17 + b], D).then_inc(dve_ms, 1)
                ve.wait_ge(act_root, 3 + 2 * b)
                ch.link(ve.reciprocal(root[:, 8 + b:9 + b], root[:, 8 + b:9 + b]))
                for s in range(2):
                    half = slice(s * 512, s * 512 + 512)
                    ve.scalar_tensor_tensor(out=xn2[:, b, half], in0=bank[1 + 2 * (b % 2) + s][:],
                                            scalar=root[:, 8 + b:9 + b], in1=gg1[:, half],
                                            op0=ALU.mult, op1=ALU.mult).then_inc(dve_mix, 1)
                ve.wait_ge(dve_mix, 2 * b + 2)
                ve.tensor_tensor(x1[:, b, :], x1[:, b, :], xn2[:, b, :], ALU.add).then_inc(dve_x1, 1)
                ve.wait_ge(act_ss, NB + 3 * b + 3)
                mean_square(ssq[:, 20 + b:21 + b], ssq[:, 20 + b:21 + b], D).then_inc(dve_ms, 1)
                ve.wait_ge(act_root, 4 + 2 * b)
                ch.link(ve.reciprocal(root[:, 12 + b:13 + b], root[:, 12 + b:13 + b]))
                ve.tensor_scalar(xn2[:, b, :], x1[:, b, :], root[:, 12 + b:13 + b], None, ALU.mult).then_inc(dve_xn2, 1)
            add_bias(SC2)
            add_bias(SH2)
            ch.wait()
            ch.link(make_scale(scale2, SC2, ROW_G2))
            for j in range(KT + 1):
                if j < KT:
                    ve.wait_ge(pe_h2, j + 1)
                    if j >= 2:
                        ve.wait_ge(dve_h2, j - 1)
                        ve.wait_ge(pe_hn, j - 1)
                    ve.tensor_scalar(htmp[j % 2][:], bank[3 + j % 4][:], scale2[:, j:j + 1],
                                     modc[:, SH2 + j:SH2 + j + 1], ALU.mult, ALU.add).then_inc(dve_htmp, 1)
                if j >= 1:
                    ve.wait_ge(act_h2, j)
                    ve.tensor_tensor(h2lo[:, j - 1, :], htmp[(j - 1) % 2][:], h2hi[:, j - 1, :].bitcast(F32),
                                     ALU.subtract).then_inc(dve_h2, 1)

            def stand_alone():
                ve.nop(nofuse=True)

            def after_the_list(b):
                if b % 2 == 0:
                    ch.wait(but=2)
                    stand_alone()

            def top16(values, found, places):
                for half in range(2):
                    k = slice(8 * half, 8 * half + 8)
                    for b in range(NB):
                        if half == 1:
                            after_the_list(b)
                        elif b == 0:
                            stand_alone()
                        ch.mark(ve.max(found(b)[:, k], values(b)))
                    for b in range(NB):
                        after_the_list(b)
                        ch.mark(ve.max_index(places(b)[:, k], found(b)[:, k], values(b)))
                    if half == 0:
                        for b in range(NB):
                            after_the_list(b)
                            ch.mark(ve.match_replace(out=values(b), in_to_replace=found(b)[:, k], in_values=values(b),
                                                     imm_value=LOWEST))

            def halves(h):
                for s in range(2):
                    ve.wait_ge(act_sc, 2 * h + s + 1)
                    top16(lambda b: score[s][:, b, :], lambda b: top[:, s, b, :], lambda b: topi[:, s, b, :])

            def select(h):
                ve.wait_ge(pool_hit, 2 * h + 2)
                for s in range(2):
                    ve.tensor_reduce(out=pick[:, s, :, bass.ds(h, 1), :].rearrange("p b o k -> p b (o k)"),
                                     in_=hit[s][:], axis=AXX, op=ALU.add).then_inc(dve_sel, 1)

            def sums(h, first=False):
                ch.wait()
                for at, a, a_end, wide in ((0, 0, ROWS_16, TOPK), (AT_4, ROWS_16, ROWS_4, 4), (AT_1, ROWS_4, TOPK, 1)):
                    tall = a_end - a
                    last = ve.tensor_tensor(
                        cand[:, :, at:at + tall * wide].rearrange("p b (i j) -> p b i j", i=tall),
                        top[:, 0, :, a:a_end].unsqueeze(3).broadcast_to([P, NB, tall, wide]),
                        top[:, 1, :, 0:wide].unsqueeze(2).broadcast_to([P, NB, tall, wide]), ALU.add)
                    if a_end < TOPK:
                        ch.mark(last)
                last.then_inc(dve_half, 1)
                ch.wait()
                ve.wait_ge(dve_half, h + 1)
                top16(lambda b: cand[:, b], lambda b: bests[:, b, :], lambda b: besti[:, b, :])
                if not first:
                    select(h - 1)
                ve.tensor_copy(topf[:], topi[:]).then_inc(dve_top, 1)
                ch.wait()
                ch.mark(ve.tensor_copy(best[:, :, bass.ds(h, 1), :].rearrange("p b o k -> p b (o k)"), bests[:]))
                ch.mark(ve.tensor_single_scalar(pair[:, 0], besti[:], 4, op=ALU.logical_shift_right))
                ch.mark(ve.tensor_single_scalar(pair[:, 1], besti[:], 2, op=ALU.logical_shift_right))
                ch.mark(ve.tensor_copy(place[:], besti[:]))
                ch.wait()
                ch.link(ve.tensor_copy(pairf[:], pair[:]))
                a, b = pairf[:, 0], pairf[:, 1]
                ch.link(ve.scalar_tensor_tensor(out=a, in0=b, scalar=float(ROWS_16 - AT_4 // 4), in1=a,
                                                op0=ALU.add, op1=ALU.max))
                ch.link(ve.scalar_tensor_tensor(out=a, in0=place[:], scalar=float(ROWS_4 - AT_1), in1=a,
                                                op0=ALU.add, op1=ALU.max))
                ch.link(ve.tensor_scalar(start[:], a, 4.0, float(AT_4 - 4 * ROWS_16), ALU.mult, ALU.add))
                ch.link(ve.scalar_tensor_tensor(out=start[:], in0=a, scalar=float(TOPK), in1=start[:],
                                                op0=ALU.mult, op1=ALU.min))
                ch.link(ve.scalar_tensor_tensor(out=start[:], in0=a, scalar=float(AT_1 - ROWS_4), in1=start[:],
                                                op0=ALU.add, op1=ALU.min))
                ve.tensor_tensor(b, place[:], start[:], ALU.subtract).then_inc(dve_pair, 1)

            halves(0)
            sums(0, first=True)
            with ve.Fori(1, PH) as h:
                ch.enter(h - 1, HEAD_STEPS)
                halves(h)
                sums(h)
                ch.leave(PH - 1)
            first = best[:, :, :, 0:1].broadcast_to([P, NB, PH, TOPK])
            ve.tensor_tensor(pick[:, 2], best[:], first, ALU.subtract).then_inc(dve_bsub, 1)
            ve.wait_ge(act_gexp, 1)
            ch.link(ve.tensor_reduce(out=bsum[:], in_=best[:], axis=AXX, op=ALU.add))
            ch.link(ve.reciprocal(bsum[:], bsum[:]))
            ve.tensor_tensor(pick[:, 2], best[:], bsum[:].unsqueeze(3).broadcast_to([P, NB, PH, TOPK]),
                             ALU.mult).then_inc(dve_pick, 1)
            select(PH - 1)

            ve.wait_ge(dve_pick, 1)
            ve.wait_ge(dve_sel, 2 * PH)
            number = best[:, GB].rearrange("p h k -> p (h k)")
            ch.mark(ve.tensor_copy(gate3[:], pick[:, 2, GB].rearrange("p h k -> p (h k)")))
            ch.link(ve.scalar_tensor_tensor(out=number, in0=pick[:, 0, GB].rearrange("p h k -> p (h k)"),
                                            scalar=float(KEYS), in1=pick[:, 1, GB].rearrange("p h k -> p (h k)"),
                                            op0=ALU.mult, op1=ALU.add))
            ve.tensor_copy(ids[:], number).then_inc(dve_ids, 1)
            ve.wait_ge(act_pick, 3)

            def hot_rows(m, u):
                some = TB - BY_ACT
                ve.tensor_tensor(onehot2[u][:, 0:some, :], iota[:].unsqueeze(1).broadcast_to([P, some, KEYS]),
                                 pickT[:, 1, bass.ds(m * TB, some)].unsqueeze(2).broadcast_to([P, some, KEYS]),
                                 ALU.is_equal).then_inc(dve_hot, 1)
                for k in range(TB - BY_POOL):
                    ve.tensor_scalar(gated1[u][:, k, :], iota[:], pickT[:, 0, bass.ds(m * TB + k, 1)],
                                     pickT[:, 2, bass.ds(m * TB + k, 1)], ALU.is_equal, ALU.mult).then_inc(dve_hot, 1)

            for u in range(2):
                hot_rows(u, u)
            with ve.Fori(1, TD // (2 * TB)) as i:
                for u in range(2):
                    ve.wait_ge(pe_g, 4 * i + 2 * u - 2)
                    hot_rows(2 * i + u, u)


            def down_lo(n, s, first=False):
                if n is not None and not first:
                    ve.wait_ge(pe_d, n - 1)
                for k in range(2):
                    ve.wait_ge(act_dhi, 2 * (0 if n is None else n) + k + 1)
                    part = slice(4 * k, 4 * k + 4)
                    ve.tensor_tensor(dlo[s][:, part, :].rearrange("p k e -> p (k e)"), bank[k][:],
                                     dhi[s][:, part, :].rearrange("p k e -> p (k e)").bitcast(F32),
                                     ALU.subtract).then_inc(dve_dlo, 1)

            def add_y(i, g, q):
                ve.wait_ge(pe_u, OUTS * i + q + 1)
                part = y[:, q // 2, (q % 2) * 512:(q % 2) * 512 + 512]
                ve.tensor_tensor(part, part, bank[4 + (OUTS * g + q) % 4][:], ALU.add).then_inc(dve_y, 1)

            def dot(n, k, turn):
                ve.wait_ge(rows_d_in[k], 4 * (n - k) + 16)
                if k or turn is not None:
                    ve.wait_ge(dve_dot, n)
                if turn is not None:
                    ve.wait_ge(act_g3, turn)
                ve.scalar_tensor_tensor(out=junk[:], in0=rows_d[k][:], scalar=1.0, in1=h2nat[:], op0=ALU.mult,
                                        op1=ALU.mult, accum_out=dots[:, k:k + 1]).then_inc(dve_dot, 1)

            def coefficients(i):
                ve.wait_ge(act_g3, i)
                ve.tensor_tensor(coef[:], gel3[:], gate3[:, bass.ds(4 * (i - 1), 4)], ALU.mult).then_inc(dve_coef, 1)
                ve.wait_ge(dve_coef, i)

            def add_up(n, k):
                ve.wait_ge(rows_u_in[k], 4 * (n - k) + 16)
                ve.scalar_tensor_tensor(out=y[:, GB, :], in0=rows_u[k][:], scalar=coef[:, k:k + 1], in1=y[:, GB, :],
                                        op0=ALU.mult, op1=ALU.add).then_inc(dve_add, 1)
                ve.wait_ge(dve_add, n + 1)

            def tile(i, g, s, turn, first=False, last=False):
                n, k = 2 * i + s, 2 * g + s
                if not last and not (first and s == 0):
                    down_lo(n + 1, 1 - s)
                if not first:
                    for q in range(3 * s, 3 * s + 3):
                        add_y(i - 1, 1 - g, q)
                ve.wait_ge(act_gelu, n + 1)
                ve.wait_ge(gate_in[s], 16 * i + 16)
                if not first:
                    ve.wait_ge(dve_alo, n - 1)
                ve.tensor_tensor(acts[s][:], gel[s][:], gate[s][:], ALU.mult).then_inc(dve_act, 1)
                ve.wait_ge(act_ahi, n + 1)
                ve.tensor_tensor(alo[g][s][:], acts[s][:], ahi[g][s][:].bitcast(F32), ALU.subtract).then_inc(dve_alo, 1)
                if turn is not None and k == 0:
                    coefficients(turn)
                if turn is not None:
                    add_up(n - 4, k)
                    dot(n, k, turn)

            down_lo(None, 0)
            down_lo(1, 1, first=True)
            ve.wait_ge(stored_part[0], 16)
            ch.mark(ve.memset(y[:, 0:GB, :], 0.0))
            for g in range(2):
                for s in range(2):
                    tile(g, g, s, None, first=g == 0)
            ve.wait_ge(stored_part[1], 16)
            ch.link(ve.memset(y[:, GB, :], 0.0))
            for k in range(4):
                dot(k, k, None)
            with ve.Fori(1, TILES // 4 - 1) as i:
                for g in range(2):
                    for s in range(2):
                        tile(2 * i + g, g, s, i)
            for g in range(2):
                for s in range(2):
                    tile(TILES // 2 - 2 + g, g, s, TILES // 4 - 1, last=g == 1 and s == 1)
            coefficients(TILES // 4)
            for q in range(OUTS):
                add_y(TILES // 2 - 1, 1, q)
                if q < 4:
                    add_up(PICKS - 4 + q, q)
                if q == 3:
                    ve.wait_ge(act_ss, NB + 3 * NB + 2)
                    mean_square(ssq[:, 24:26], ssq[:, 24:26], D).then_inc(dve_ms, 1)

            def normed(b):
                return ve.scalar_tensor_tensor(out=y[:, b, :], in0=y[:, b, :], scalar=root[:, 16 + b:17 + b], in1=gg2[:],
                                               op0=ALU.mult, op1=ALU.mult)

            ve.wait_ge(act_root, 2 + 2 * NB + 1)
            ch.link(ve.reciprocal(root[:, 16:18], root[:, 16:18]))
            normed(0).then_inc(dve_normed, 1)
            normed(1).then_inc(dve_normed, 1)
            ve.wait_ge(act_ss, NB + 3 * NB + NB)
            mean_square(ssq[:, 26:28], ssq[:, 26:28], D).then_inc(dve_ms, 1)
            ve.wait_ge(act_root, 2 + 2 * NB + 2)
            ch.link(ve.reciprocal(root[:, 18:20], root[:, 18:20]))
            for b in range(2, NB):
                ch.link(normed(b))
                ve.tensor_tensor(x1[:, b, :], x1[:, b, :], y[:, b, :], ALU.add).then_inc(dve_x1, 1)

        @block.tensor
        def _(pe):
            pe.wait_ge(act_silu, 1)
            pe.wait_ge(ident_ok, 3)
            pe.transpose(bank[7][:, 0:ROWS], rows[0:ROWS, :], ident[0:ROWS, 0:ROWS]).then_inc(pe_rows, 1)
            pe.wait_ge(sgw_in, 16)
            for g in range(GROUPS):
                last = pe.transpose(bank[6][:, g * P:(g + 1) * P], sgw[:, g, :], ident[:])
            last.then_inc(pe_wT, 1)

            def ada_chunk(n):
                pe.wait_ge(dve_ada, 2 * n + 2)
                if n in (4, 5, 10, 11):
                    if n != 4:
                        pe.wait_ge(dve_gg, {5: 1, 10: 2, 11: 3}[n])
                    for e in range(2):
                        last = pe.matmul(bank[7][:], ones[:], part[n % 2][:, e, :], start=e == 0, stop=e == 1)
                else:
                    for j in range(4):
                        col = 4 * ADA_ORDER[n] + j
                        for e in range(2):
                            last = pe.matmul(bank[0][:, col:col + 1], part[n % 2][:, e, j * P:(j + 1) * P],
                                             ones[:, 0:1], start=e == 0, stop=e == 1)
                last.then_inc(pe_ada, 1)

            for n in range(4):
                ada_chunk(n)
            for j in range(KT):
                if j == 0:
                    pe.wait_ge(dve_xn1, NB)
                if j >= 4:
                    pe.wait_ge(act_h1 if j % 2 else dve_h1, (j - 4) // 2 + 1)
                for b in range(NB):
                    last = pe.transpose(bank[1 + j % 4][:, b * P:(b + 1) * P], xn1[:, b, j * P:(j + 1) * P], ident[:])
                last.then_inc(pe_h1, 1)
            pe.wait_ge(act_h1, 4)
            pe.wait_ge(dve_h1, 4)
            pe.wait_ge(dve_wT, 1)
            def scores(b):
                if b >= 1:
                    pe.wait_ge(act_s, 2 * b)
                for s in range(2):
                    side = slice(s * HD, (s + 1) * HD)
                    for j in range(4):
                        for q in range(2):
                            at = b * P + q * CHUNK
                            last = pe.matmul(bank[1 + s][q * CHUNK:(q + 1) * CHUNK, j * P:(j + 1) * P],
                                             qT[side, j, at:at + CHUNK], kT[side, at:at + P], start=True, stop=True)
                    last.then_inc(pe_s, 1)

            def transpose_probs(b):
                pe.wait_ge(dve_p, b + 1)
                if b >= 1:
                    pe.wait_ge(act_o, b)
                for s in range(2):
                    for j in range(4):
                        last = pe.transpose(bank[3 + s][:, j * P:(j + 1) * P], s_sb[b % 2][:, 4 * s + j, :], ident[:])
                    last.then_inc(pe_pt, 1)

            def attend(b):
                pe.wait_ge(act_pt, 2 * b + 2)
                for h in range(HEADS):
                    for q in range(2):
                        last = pe.matmul(bank[3][(h % 2) * HD:(h % 2 + 1) * HD, (h // 2) * P + q * CHUNK:(h // 2) * P + (q + 1) * CHUNK],
                                         (v if q else vs)[:, b, (h // 4) * HD:(h // 4 + 1) * HD],
                                         pT[b % 2][:, h, q * CHUNK:(q + 1) * CHUNK], start=True, stop=True)
                last.then_inc(pe_o, 1)

            def mix_positions(g):
                pe.wait_ge(dve_vn, NB)
                if g >= 2:
                    pe.wait_ge(dve_sgu, g - 1)
                for b in range(NB):
                    last = pe.matmul(bank[5 + g % 2][:, b * P:(b + 1) * P], sv[:, b, g * P:(g + 1) * P], wT[:, g, :],
                                     start=True, stop=True)
                last.then_inc(pe_sgu, 1)

            pe.wait_ge(w_qkv_in, 16 * (1 + 2 * KT))
            for m in range(Z_JOBS):
                if m >= 5:
                    pe.wait_ge(act_z, m - 4 if m < Z_SV else m - 1)
                got = bank[Z_BANKS[m]]
                if m == Z_SV:
                    pe.wait_ge(w_sv_in, 16)
                elif m == Z_U:
                    pe.wait_ge(w_u_in, 16)
                if Z_SV <= m < Z_U:
                    at = CHUNK + (m - Z_SV) * P
                    for k in range(KT):
                        last = pe.matmul(got[:], hT[:, k, at:at + P], w_in_sb[:, k, SV_AT:SV_AT + SGU],
                                         start=k == 0, stop=k == KT - 1)
                elif m < Z_V or m >= Z_U:
                    for k in range(KT):
                        if m >= Z_U:
                            w = w_in_sb[:, k, U_AT + (m - Z_U) * P:U_AT + (m - Z_U + 1) * P]
                        elif m == Z_K:
                            w = w_in_sb[:, k, K_AT:K_AT + KVW]
                        else:
                            w = w_in_sb[:, k, (m - Z_Q) * P:(m - Z_Q + 1) * P]
                        last = pe.matmul(got[:], w, hT[:, k, CHUNK:], start=k == 0, stop=k == KT - 1)
                else:
                    at = CHUNK if m == Z_V else 0
                    for b in range(NB):
                        for k in range(KT):
                            last = pe.matmul(got[:, b * P:(b + 1) * P], hT[:, k, at + b * P:at + (b + 1) * P],
                                             w_in_sb[:, k, V_AT:V_AT + KVW], start=k == 0, stop=k == KT - 1)
                last.then_inc(pe_z, 1)
                if m in Z_ADA:
                    ada_chunk(Z_ADA[m])
                if m == Z_SV:
                    pe.wait_ge(act_z, Z_SV)
                    scores(0)
                elif m == Z_SV + 1:
                    scores(1)
                elif m == Z_SV + 2:
                    transpose_probs(0)
                elif m == Z_SV + 3:
                    attend(0)
                    scores(2)
                elif m == Z_U:
                    transpose_probs(1)
                elif m == Z_U + 1:
                    attend(1)
                    scores(3)
                elif m == Z_U + 2:
                    transpose_probs(2)
                elif m == Z_U + 3:
                    attend(2)
            pe.wait_ge(act_z, Z_JOBS)
            mix_positions(0)
            mix_positions(1)
            transpose_probs(3)
            for g in range(2, GROUPS):
                mix_positions(g)
            attend(3)

            def transpose_keys(m):
                pe.wait_ge(keys_in, 16)
                if m >= 2:
                    pe.wait_ge(act_keys, m - 1)
                for k in range(4):
                    last = pe.transpose(bank[5 + m % 2][:, k * P:(k + 1) * P], keys[:, 4 * m + k, :], ident[:])
                last.then_inc(pe_keys, 1)

            pe.wait_ge(w_out_in, 32)
            pe.wait_ge(act_o, NB)
            pe.wait_ge(dve_sgu, GROUPS)
            for b in range(NB):
                for s in range(2):
                    if b >= 2:
                        pe.wait_ge(dve_mix, 2 * (b - 2) + s + 1)
                    for k in range(KT):
                        last = pe.matmul(bank[1 + 2 * (b % 2) + s][:], catT[:, k, b * P:(b + 1) * P],
                                         w_out_sb[:, k, s * 512:s * 512 + 512], start=k == 0, stop=k == KT - 1)
                    last.then_inc(pe_mix, 1)
                if b in (1, 2):
                    transpose_keys(2 * b - 2)
                    transpose_keys(2 * b - 1)

            def query_part(s, k):
                pe.matmul(bank[1 + s][:], wqhi[s][:, k, :], h2hi[:, k, :], start=k == 0, stop=False)
                pe.matmul(bank[1 + s][:], wqhi[s][:, k, :], h2lo[:, k, :], start=False, stop=False)
                return pe.matmul(bank[1 + s][:], wqlo[s][:, k, :], h2hi[:, k, :], start=False, stop=k == KT - 1)

            pe.wait_ge(dve_xn2, NB)
            pe.wait_ge(act_keys, 4)
            for j in range(KT + 2):
                if j < KT:
                    if j >= 4:
                        pe.wait_ge(dve_htmp, j - 3)
                    for b in range(NB):
                        last = pe.transpose(bank[3 + j % 4][:, b * P:(b + 1) * P], xn2[:, b, j * P:(j + 1) * P], ident[:])
                    last.then_inc(pe_h2, 1)
                if 1 <= j <= KT:
                    k = j - 1
                    pe.wait_ge(dve_htmp, k + 1)
                    pe.transpose(bank[7 * (k // 4)][:, (k % 4) * P:(k % 4 + 1) * P], htmp[k % 2][:, GB * P:T],
                                 ident[:]).then_inc(pe_hn, 1)
                if j >= 2:
                    k = j - 2
                    pe.wait_ge(act_h2, k + 1)
                    pe.wait_ge(dve_h2, k + 1)
                    pe.wait_ge(act_wq, 1)
                    pe.wait_ge(pool_wq, 1)
                    last = query_part(0, k)
            last.then_inc(pe_q, 1)

            def queries(h, halves):
                for s in halves:
                    pe.wait_ge(act_wq, 2 * h + s + 1)
                    pe.wait_ge(pool_wq, 2 * h + s + 1)
                    for k in range(KT):
                        last = query_part(s, k)
                    last.then_inc(pe_q, 1)

            def scores_of(h, halves, first=False):
                for s in halves:
                    pe.wait_ge(act_q, 2 * h + s + 1)
                    if not first:
                        pe.wait_ge(act_sc, 2 * h)
                    for b in range(NB):
                        last = pe.matmul(bank[3 + s][:, b * P:(b + 1) * P], pqT[s][:, b * P:(b + 1) * P],
                                         keysT[:, bass.ds(2 * h + s, 1), :].rearrange("p o k -> p (o k)"),
                                         start=True, stop=True)
                    last.then_inc(pe_sc, 1)

            for s in range(2):
                if s == 1:
                    queries(0, (s,))
                scores_of(0, (s,), first=True)
            with pe.Fori(1, PH) as h:
                queries(h, (0, 1))
                scores_of(h, (0, 1))
            pe.wait_ge(dve_pick, 1)
            pe.wait_ge(dve_sel, 2 * PH)
            for k in range(3):
                for b in range(GB):
                    last = pe.transpose(bank[5 + k][:, b * P:(b + 1) * P], pick[:, k, b].rearrange("p h k -> p (h k)"), ident[:])
                last.then_inc(pe_pick, 1)

            def gate_products(m, u, first=False):
                pe.wait_ge(dve_hot, (1 + TB - BY_POOL) * (m + 1))
                for s in range(2):
                    if s:
                        pe.wait_ge(pool_hot, BY_POOL * (m + 1))
                        pe.wait_ge(act_hot, m + 1)
                    if not first:
                        pe.wait_ge(act_g, 2 * m + s - 3)
                    for k in range(4):
                        last = pe.matmul(bank[1 + 2 * u + s][:, k * P:(k + 1) * P], onehot2[u][:, 4 * s + k, :],
                                         gated1[u][:, 4 * s + k, :], start=True, stop=True)
                    last.then_inc(pe_g, 1)

            for u in range(2):
                gate_products(u, u, first=True)
            with pe.Fori(1, TD // (2 * TB)) as i:
                for u in range(2):
                    gate_products(2 * i + u, u)


            def transpose_down(n, s, first=False):
                pe.wait_ge(down_in[s], 8 * (n - s) + 16)
                for k in range(2):
                    if not first:
                        pe.wait_ge(dve_dlo, 2 * n + k - 1)
                    elif k:
                        pe.wait_ge(act_g, GB * (P // 4))
                    for q in range(4):
                        at = (4 * k + q) * P
                        last = pe.transpose(bank[k][:, q * P:(q + 1) * P], down[s][:, at:at + P], ident[:])
                    last.then_inc(pe_t, 1)

            def multiply_down(n, s, first=False):
                pe.wait_ge(dve_dlo, 2 * n + 2)
                if not first:
                    pe.wait_ge(act_gelu, n - 1)
                for k in range(KT):
                    pe.matmul(bank[2 + s][:, 0:TD], dhi[s][:, k, :], h2hi[:, k, 0:TD], start=k == 0, stop=False)
                    pe.matmul(bank[2 + s][:, 0:TD], dhi[s][:, k, :], h2lo[:, k, 0:TD], start=False, stop=False)
                    last = pe.matmul(bank[2 + s][:, 0:TD], dlo[s][:, k, :], h2hi[:, k, 0:TD], start=False, stop=k == KT - 1)
                last.then_inc(pe_d, 1)

            def multiply_up(i, g, q, first=False):
                if q >= 4 or not first:
                    pe.wait_ge(dve_y, OUTS * i + q - 3)
                got = bank[4 + (OUTS * g + q) % 4]
                tokens, half = slice((q // 2) * P, (q // 2 + 1) * P), slice((q % 2) * 512, (q % 2) * 512 + 512)
                for s in range(GROUP):
                    pe.matmul(got[:], ahi[g][s][:, tokens], uhi[g][s][:, half], start=s == 0, stop=False)
                    pe.matmul(got[:], ahi[g][s][:, tokens], ulo[g][s][:, half], start=False, stop=False)
                    last = pe.matmul(got[:], alo[g][s][:, tokens], uhi[g][s][:, half], start=False, stop=s == GROUP - 1)
                last.then_inc(pe_u, 1)

            def group_ready(i):
                pe.wait_ge(dve_alo, 2 * i + 2)
                pe.wait_ge(pool_ulo, 2 * i + 2)

            def tile(i, g, s, first=False, second=False, last=False):
                n = 2 * i + s
                if not last:
                    transpose_down(n + 1, 1 - s)
                multiply_down(n, s, first=first)
                if not first:
                    if s == 0:
                        group_ready(i - 1)
                    for q in range(3 * s, 3 * s + 3):
                        multiply_up(i - 1, 1 - g, q, first=second)

            transpose_down(0, 0, first=True)
            for g in range(2):
                for s in range(2):
                    tile(g, g, s, first=g == 0, second=g == 1)
            with pe.Fori(1, TILES // 4 - 1) as i:
                for g in range(2):
                    for s in range(2):
                        tile(2 * i + g, g, s)
            for g in range(2):
                for s in range(2):
                    tile(TILES // 2 - 2 + g, g, s, last=g == 1 and s == 1)
            group_ready(TILES // 2 - 1)
            for q in range(OUTS):
                multiply_up(TILES // 2 - 1, 1, q)


_INS = ["x", "c", "w_ada", "b_ada", "g_pre_mix", "g_post_mix", "g_pre_ffn", "g_post_ffn", "w_in", "attn_sinks",
        "sgu_norm", "sgu_w", "sgu_b", "w_out", "peer_query", "peer_keys", "peer_down", "peer_up"]


def kernel(**inputs):
    import numpy as np
    import concourse.bacc as bacc
    from concourse.bass_utils import run_bass_kernel_spmd

    nc = bacc.Bacc("TRN2", target_bir_lowering=False, num_devices=1)
    arrays = {f"in_{n}": np.ascontiguousarray(inputs[n]) for n in _INS}
    args = [nc.dram_tensor(n, a.shape, mybir.dt.from_np(a.dtype), kind="ExternalInput").ap() for n, a in arrays.items()]
    result = nc.dram_tensor("out_x", arrays["in_x"].shape, F32, kind="ExternalOutput").ap()
    build_block(nc, *args, result)
    ran = run_bass_kernel_spmd(nc, [arrays], core_ids=[0])
    return ran.results[0]["out_x"]
```
